# Optimizing a Trainium2 kernel written in Bass

```python
import math
import jax, jax.numpy as jnp
from jax import lax
import numpy as np

D_MODEL = 1024
BATCH = 1
SEQ = 2048
DEPTH = 1

CHUNK = 64
N_META = 16
Q_BLOCK = 128
MIX_WIDTH = D_MODEL
EPS = 1e-6
NEG = -1e30

DA_HEADS = 4
DA_WIDTH = MIX_WIDTH // 2
DA_V_DIM = DA_WIDTH // DA_HEADS
DA_HEAD_DIM = DA_V_DIM // 2
DA_QK = DA_HEADS * 2 * DA_HEAD_DIM

MLA_HEADS = 4
MLA_WIDTH = MIX_WIDTH - DA_WIDTH
MLA_V = MLA_WIDTH // MLA_HEADS
MLA_NOPE = 128
MLA_ROPE = 64
MLA_Q_RANK = D_MODEL // 4
MLA_KV_RANK = D_MODEL // 8
ROPE_THETA = 10000.0

IN_SIZES = (DA_QK, DA_QK, DA_WIDTH, MLA_Q_RANK, MLA_KV_RANK, MLA_ROPE)
IN_WIDTH = sum(IN_SIZES)
IN_SPLITS = tuple(int(s) for s in np.cumsum(IN_SIZES)[:-1])

D_FF = 4 * D_MODEL

kernel_name = "hymba_diffattn_mla_sandwich_block"

def _rms(x, g):
    xf = x.astype(jnp.float32)
    y = xf * lax.rsqrt(jnp.mean(xf * xf, axis=-1, keepdims=True) + EPS)
    return (y * g.astype(jnp.float32)).astype(x.dtype)

def _chunk_ids(pos):
    return jnp.where(pos < N_META, 0, (pos - N_META) // CHUNK + 1)

def _chunk_mask(qpos, kpos):
    return _chunk_ids(kpos)[None, :] <= _chunk_ids(qpos)[:, None]

def _sweep_query_blocks(fn, qs, L):
    n_blk = -(-L // Q_BLOCK)
    Lp = n_blk * Q_BLOCK

    def prep(q):
        b, h, _, d = q.shape
        q = jnp.pad(q, ((0, 0), (0, 0), (0, Lp - L), (0, 0)))
        return jnp.moveaxis(q.reshape(b, h, n_blk, Q_BLOCK, d), 2, 0)

    qpos = jnp.arange(Lp, dtype=jnp.int32).reshape(n_blk, Q_BLOCK)
    out = lax.map(lambda a: fn(a[0], *a[1]), (qpos, tuple(prep(q) for q in qs)))
    nb, b, h, qb, dv = out.shape
    out = jnp.moveaxis(out, 0, 2).reshape(b, h, Lp, dv)
    return out[:, :, :L]

def _rope_tables(L):
    inv_freq = 1.0 / (ROPE_THETA ** (jnp.arange(0, MLA_ROPE, 2, dtype=jnp.float32) / MLA_ROPE))
    ang = jnp.arange(L, dtype=jnp.float32)[:, None] * inv_freq[None, :]
    return jnp.cos(ang), jnp.sin(ang)

def _rope(x, cos, sin):
    half = x.shape[-1] // 2
    x1, x2 = x[..., :half], x[..., half:]
    c = cos.astype(x.dtype)
    s = sin.astype(x.dtype)
    return jnp.concatenate([x1 * c - x2 * s, x2 * c + x1 * s], axis=-1)

def _diff_attention(q, k, v, lq1, lk1, lq2, lk2, g_sub, lambda_init):
    B, L, _ = q.shape
    q = q.reshape(B, L, DA_HEADS, 2, DA_HEAD_DIM).transpose(0, 2, 1, 3, 4)
    k = k.reshape(B, L, DA_HEADS, 2, DA_HEAD_DIM).transpose(0, 2, 1, 3, 4)
    q1, q2 = q[..., 0, :], q[..., 1, :]
    k1, k2 = k[..., 0, :], k[..., 1, :]
    v = v.reshape(B, L, DA_HEADS, DA_V_DIM).transpose(0, 2, 1, 3)

    f32 = jnp.float32
    lam = (jnp.exp(jnp.sum(lq1.astype(f32) * lk1.astype(f32)))
           - jnp.exp(jnp.sum(lq2.astype(f32) * lk2.astype(f32))) + lambda_init)
    slopes = 2.0 ** (-8.0 * jnp.arange(1, DA_HEADS + 1, dtype=f32) / DA_HEADS)
    scale = DA_HEAD_DIM ** -0.5
    kpos = jnp.arange(L, dtype=jnp.int32)

    def blk(qp, q1b, q2b):
        mask = _chunk_mask(qp, kpos)
        dist = jnp.abs(qp[:, None] - kpos[None, :]).astype(f32)
        bias = jnp.where(mask[None], -slopes[:, None, None] * dist[None], NEG)
        s1 = jnp.einsum('bhqd,bhkd->bhqk', q1b, k1).astype(f32) * scale + bias
        s2 = jnp.einsum('bhqd,bhkd->bhqk', q2b, k2).astype(f32) * scale + bias
        a = jax.nn.softmax(s1, axis=-1) - lam * jax.nn.softmax(s2, axis=-1)
        return jnp.einsum('bhqk,bhkv->bhqv', a.astype(v.dtype), v)

    o = _sweep_query_blocks(blk, (q1, q2), L)
    o = _rms(o, g_sub) * (1.0 - lambda_init)
    return o.transpose(0, 2, 1, 3).reshape(B, L, DA_WIDTH)

def _mla(cq, ckv, kr, g_q, w_q_up, g_kv, w_kv_up, cos, sin):
    B, L, _ = cq.shape
    q = (_rms(cq, g_q) @ w_q_up).reshape(B, L, MLA_HEADS, MLA_NOPE + MLA_ROPE)
    q_nope = q[..., :MLA_NOPE]
    q_rope = _rope(q[..., MLA_NOPE:], cos[:, None, :], sin[:, None, :])
    kv = (_rms(ckv, g_kv) @ w_kv_up).reshape(B, L, MLA_HEADS, MLA_NOPE + MLA_V)
    k_nope, v = kv[..., :MLA_NOPE], kv[..., MLA_NOPE:]
    k_rope = _rope(kr, cos, sin)

    q = jnp.concatenate([q_nope, q_rope], axis=-1).transpose(0, 2, 1, 3)
    k = jnp.concatenate(
        [k_nope, jnp.broadcast_to(k_rope[:, :, None, :], (B, L, MLA_HEADS, MLA_ROPE))],
        axis=-1).transpose(0, 2, 1, 3)
    v = v.transpose(0, 2, 1, 3)
    scale = (MLA_NOPE + MLA_ROPE) ** -0.5
    kpos = jnp.arange(L, dtype=jnp.int32)

    def blk(qp, qb):
        bias = jnp.where(_chunk_mask(qp, kpos), 0.0, NEG).astype(jnp.float32)
        s = jnp.einsum('bhqd,bhkd->bhqk', qb, k).astype(jnp.float32) * scale + bias
        p = jax.nn.softmax(s, axis=-1)
        return jnp.einsum('bhqk,bhkv->bhqv', p.astype(v.dtype), v)

    o = _sweep_query_blocks(blk, (q,), L)
    return o.transpose(0, 2, 1, 3).reshape(B, L, MLA_WIDTH)

def setup_inputs(seed: int = 0) -> dict:
    key = jax.random.key(seed)
    ks = jax.random.split(key, 24)
    f32 = jnp.float32

    def nrm(k, shape, scale):
        return jax.random.normal(k, shape, f32) * scale

    def gain(k, shape):
        return 1.0 + 0.02 * jax.random.normal(k, shape, f32)

    return {
        "x": nrm(ks[0], (BATCH, SEQ, D_MODEL), 1.0),
        "meta_tokens": nrm(ks[1], (N_META, D_MODEL), 1.0),
        "g_attn_pre": gain(ks[2], (DEPTH, D_MODEL)),
        "w_in": nrm(ks[3], (DEPTH, D_MODEL, IN_WIDTH), D_MODEL ** -0.5),
        "da_lambda_q1": nrm(ks[4], (DEPTH, DA_HEAD_DIM), 0.1),
        "da_lambda_k1": nrm(ks[5], (DEPTH, DA_HEAD_DIM), 0.1),
        "da_lambda_q2": nrm(ks[6], (DEPTH, DA_HEAD_DIM), 0.1),
        "da_lambda_k2": nrm(ks[7], (DEPTH, DA_HEAD_DIM), 0.1),
        "g_da_sub": gain(ks[8], (DEPTH, DA_V_DIM)),
        "g_mla_q": gain(ks[9], (DEPTH, MLA_Q_RANK)),
        "w_mla_q_up": nrm(ks[10], (DEPTH, MLA_Q_RANK, MLA_HEADS * (MLA_NOPE + MLA_ROPE)), MLA_Q_RANK ** -0.5),
        "g_mla_kv": gain(ks[11], (DEPTH, MLA_KV_RANK)),
        "w_mla_kv_up": nrm(ks[12], (DEPTH, MLA_KV_RANK, MLA_HEADS * (MLA_NOPE + MLA_V)), MLA_KV_RANK ** -0.5),
        "w_o": nrm(ks[13], (DEPTH, MIX_WIDTH, D_MODEL), MIX_WIDTH ** -0.5),
        "g_attn_post": gain(ks[14], (DEPTH, D_MODEL)),
        "g_mlp_pre": gain(ks[15], (DEPTH, D_MODEL)),
        "w_ff1": nrm(ks[16], (DEPTH, D_MODEL, D_FF), D_MODEL ** -0.5),
        "w_ff2": nrm(ks[17], (DEPTH, D_FF, D_MODEL), D_FF ** -0.5),
        "g_mlp_post": gain(ks[18], (DEPTH, D_MODEL)),
    }

def reference(x, meta_tokens, g_attn_pre, w_in, da_lambda_q1, da_lambda_k1, da_lambda_q2,
              da_lambda_k2, g_da_sub, g_mla_q, w_mla_q_up, g_mla_kv, w_mla_kv_up, w_o,
              g_attn_post, g_mlp_pre, w_ff1, w_ff2, g_mlp_post):
    B = x.shape[0]
    meta = jnp.broadcast_to(meta_tokens.astype(x.dtype)[None], (B, N_META, D_MODEL))
    h = jnp.concatenate([meta, x], axis=1)
    L = h.shape[1]
    cos, sin = _rope_tables(L)

    for l in range(DEPTH):
        lambda_init = 0.8 - 0.6 * math.exp(-0.3 * l)
        u = _rms(h, g_attn_pre[l])
        proj = u @ w_in[l]
        q_da, k_da, v_da, cq, ckv, kr = jnp.split(proj, IN_SPLITS, axis=-1)
        y_da = _diff_attention(q_da, k_da, v_da, da_lambda_q1[l], da_lambda_k1[l],
                               da_lambda_q2[l], da_lambda_k2[l], g_da_sub[l], lambda_init)
        y_mla = _mla(cq, ckv, kr, g_mla_q[l], w_mla_q_up[l], g_mla_kv[l], w_mla_kv_up[l], cos, sin)
        mix = jnp.concatenate([y_da, y_mla], axis=-1) @ w_o[l]
        h = h + _rms(mix, g_attn_post[l])
        u = _rms(h, g_mlp_pre[l])
        f = jnp.square(jax.nn.relu(u @ w_ff1[l])) @ w_ff2[l]
        h = h + _rms(f, g_mlp_post[l])

    return h[:, N_META:]


_drawn_inputs = setup_inputs


def setup_inputs(seed=0):
    import zlib

    import numpy as np

    out = dict(_drawn_inputs(seed))
    spreads = {}
    factors = {'g_da_sub': 26.389,
     'g_mla_q': 8.0,
     'g_mla_kv': 8.0,
     'g_attn_post': 10.396,
     'g_mlp_pre': 38.593,
     'g_mlp_post': 62.882,
     'da_lambda_k1': 4.626,
     'da_lambda_q2': 4.882}
    for name, (base, spread) in spreads.items():
        noise = np.random.default_rng([zlib.crc32(name.encode()), seed]).standard_normal(out[name].shape)
        drawn = base * np.exp(spread * noise) if base else spread * noise
        out[name] = __import__('jax').numpy.asarray(drawn.astype(out[name].dtype))
    for name, factor in factors.items():
        out[name] = (out[name] * factor).astype(out[name].dtype)
    return out
```

```python
import math
from contextlib import ExitStack

import numpy as np
import concourse.bass as bass
from concourse import mybir

F32 = mybir.dt.float32
F32R = mybir.dt.float32r
ALU = mybir.AluOpType
ACT = mybir.ActivationFunctionType
AX = mybir.AxisListType

P = 128
D = 1024
SEQ = 2048
META = 16
L = SEQ + META
CHUNK = 64
NT = SEQ // P
KD = D // P
EPS = 1e-6
NEG = -1e30
LOWEST = -3.0e38
DA_H, DA_HD, DA_V = 4, 64, 128
MLA_H, NOPE, ROPE, MLA_V = 4, 128, 64, 128
QR, KVR = 256, 128
DFF = 4096
DA_W = DA_H * DA_V
C_Q, C_KV, C_R = 3 * DA_W, 3 * DA_W + QR, 3 * DA_W + QR + KVR
IN_W = C_R + ROPE
LAMBDA_INIT = 0.8 - 0.6 * math.exp(-0.0)
DA_SCALE = DA_HD ** -0.5
MLA_SCALE = (NOPE + ROPE) ** -0.5
TOK_CHUNKS = [(0, META)] + [(META + 512 * i, 512) for i in range(SEQ // 512)]
TILES = [(0, META)] + [(META + P * i, P) for i in range(NT)]
ds = bass.ds


def f32(ap):
    return ap.bitcast(F32)


def hold(engine, sem, value):
    engine.wait_ge(sem, value)
    engine.nop(nofuse=True)


def flat(ap):
    return ap.rearrange("a p n -> p (a n)")


class Memory:

    def __init__(self, nc, ctx):
        self.nc, self.ctx, self.sems = nc, ctx, []
        ctx.callback(self.clear)

    def clear(self):
        if self.sems:
            self.nc.clear_and_free_semaphores(self.sems)
            self.nc.all_engine_barrier()

    def sb(self, name, shape, dt=F32):
        return self.ctx.enter_context(self.nc.sbuf_tensor(name, shape, dt))

    def ps(self, name, cols=512):
        return self.ctx.enter_context(self.nc.psum_tensor(name, [P, cols], F32))

    def sem(self, name):
        self.sems.append(self.nc.alloc_semaphore(name))
        return self.sems[-1]


def norm_in(nc, io, u_hi, u_lo, ident, g_col, eps):
    with ExitStack() as ctx:
        mem = Memory(nc, ctx)
        xt = mem.sb("ni_xt", [P, 2, D])
        xn = mem.sb("ni_xn", [P, 2, D])
        junk = mem.sb("ni_junk", [P, D])
        ssq = mem.sb("ni_ssq", [P, 2])
        std = mem.sb("ni_std", [P, 2])
        rstd = mem.sb("ni_rstd", [P, 2])
        pt = [mem.ps(f"ni_pt{i}", D) for i in range(2)]
        const_loaded, eps_ready = mem.sem("ni_const_loaded"), mem.sem("ni_eps_ready")
        x_loaded = [mem.sem(f"ni_x_loaded{u}") for u in range(2)]
        ssq_ready, std_ready, rstd_ready = (mem.sem(f"ni_{s}_ready") for s in ("ssq", "std", "rstd"))
        xn_ready, xT_ready = mem.sem("ni_xn_ready"), mem.sem("ni_xT_ready")
        hi_ready, lo_ready = mem.sem("ni_hi_ready"), mem.sem("ni_lo_ready")

        def turned(u, rows):
            return pt[u][:, :].rearrange("p (k t) -> p k t", k=KD)[:, :, 0:rows]

        with nc.Block() as block:
            @block.sync
            def _(sp):
                sp.dma_start(xt[0:META, 0, :], io.meta).then_inc(x_loaded[0], 16)
                sp.dma_start(xt[:, 1, :], io.x[0, 0:P, :]).then_inc(x_loaded[1], 16)
                sp.dma_start(ident[:, :], io.ident).then_inc(const_loaded, 16)
                sp.dma_start(g_col[:, :], io.g_attn_pre).then_inc(const_loaded, 16)

                def load(n, u):
                    sp.wait_ge(xn_ready, n - 1)
                    sp.dma_start(xt[:, u, :], flat(io.x[:, ds((n - 1) * P, P), :])).then_inc(x_loaded[u], 16)

                with sp.Fori(0, NT // 2 - 1) as j:
                    load(2 * j + 2, 0)
                    load(2 * j + 3, 1)
                load(NT, 0)
                sp.wait_ge(const_loaded, 32)

            @block.gpsimd
            def _(pool):
                pool.memset(eps[:, :], EPS).then_inc(eps_ready, 1)

            @block.scalar
            def _(act):
                def stats(n, u, nth, rows):
                    act.wait_ge(x_loaded[u], 16 * nth + 16)
                    act.activation(junk[0:rows, :], xt[0:rows, u, :], ACT.Square,
                                   accum_out=ssq[0:rows, u:u + 1]).then_inc(ssq_ready, 1)

                def root(n, u, rows):
                    act.wait_ge(ssq_ready, n + 1)
                    act.activation(std[0:rows, u:u + 1], ssq[0:rows, u:u + 1], ACT.Sqrt,
                                   bias=eps[0:rows, :], scale=1.0 / D).then_inc(std_ready, 1)

                def high(n, u, rows, col):
                    act.wait_ge(xT_ready, n + 1)
                    act.activation(u_hi[:, :, ds(col, rows)], turned(u, rows), ACT.Copy).then_inc(hi_ready, 1)

                act.wait_ge(eps_ready, 1)
                stats(0, 0, 0, META)
                root(0, 0, META)
                stats(1, 1, 0, P)
                high(0, 0, META, 0)
                root(1, 1, P)
                with act.Fori(0, NT // 2 - 1) as j:
                    for v in range(2):
                        n = 2 * j + 2 + v
                        stats(n, v, j + 1, P)
                        high(n - 1, 1 - v, P, META + (2 * j + v) * P)
                        root(n, v, P)
                stats(NT, 0, NT // 2, P)
                high(NT - 1, 1, P, META + (NT - 2) * P)
                root(NT, 0, P)
                high(NT, 0, P, META + (NT - 1) * P)

            @block.vector
            def _(dve):
                def scale(n, u, rows, first):
                    dve.wait_ge(std_ready, n + 1)
                    dve.reciprocal(rstd[0:rows, u:u + 1], std[0:rows, u:u + 1]).then_inc(rstd_ready, 1)
                    if not first:
                        dve.wait_ge(xT_ready, n - 1)
                    dve.wait_ge(rstd_ready, n + 1)
                    dve.tensor_scalar(xn[0:rows, u, :], xt[0:rows, u, :], rstd[0:rows, u:u + 1], None,
                                      ALU.mult).then_inc(xn_ready, 1)

                def low(n, u, rows, col):
                    dve.wait_ge(hi_ready, n + 1)
                    dve.tensor_tensor(u_lo[:, :, ds(col, rows)], turned(u, rows), f32(u_hi[:, :, ds(col, rows)]),
                                      ALU.subtract).then_inc(lo_ready, 1)

                scale(0, 0, META, True)
                scale(1, 1, P, True)
                low(0, 0, META, 0)
                with dve.Fori(0, NT // 2 - 1) as j:
                    for v in range(2):
                        n = 2 * j + 2 + v
                        scale(n, v, P, False)
                        low(n - 1, 1 - v, P, META + (2 * j + v) * P)
                scale(NT, 0, P, False)
                low(NT - 1, 1, P, META + (NT - 2) * P)
                low(NT, 0, P, META + (NT - 1) * P)

            @block.tensor
            def _(pe):
                def turn(n, u, rows, first):
                    pe.wait_ge(xn_ready, n + 1)
                    if not first:
                        pe.wait_ge(lo_ready, n - 1)
                    for k in range(KD):
                        t = pe.transpose(pt[u][:, k * P:k * P + rows], xn[0:rows, u, k * P:(k + 1) * P],
                                         ident[0:rows, 0:rows])
                    t.then_inc(xT_ready, 1)

                pe.wait_ge(const_loaded, 32)
                turn(0, 0, META, True)
                turn(1, 1, P, True)
                with pe.Fori(0, NT // 2 - 1) as j:
                    turn(2 * j + 2, 0, P, False)
                    turn(2 * j + 3, 1, P, False)
                turn(NT, 0, P, False)


def qk_proj(nc, io, scr, u_hi, u_lo, g_col):
    NM, NQ = 2 * DA_W // P, len(TOK_CHUNKS)
    with ExitStack() as ctx:
        mem = Memory(nc, ctx)
        w_raw = mem.sb("qk_w_raw", [P, 2, KD, P])
        w_hi = mem.sb("qk_w_hi", [P, 2, KD, P], F32R)
        w_lo = mem.sb("qk_w_lo", [P, 2, KD, P], F32R)
        o_hi = mem.sb("qk_o_hi", [P, L], F32R)
        o_lo = mem.sb("qk_o_lo", [P, L], F32R)
        ps = [mem.ps(f"qk_ps{q}") for q in range(NQ)]
        w_loaded = [mem.sem(f"qk_w_loaded{u}") for u in range(2)]
        w_gained, w_hi_ready, w_lo_ready = (mem.sem(f"qk_w_{s}") for s in ("gained", "hi_ready", "lo_ready"))
        sums_ready, hi_ready, lo_ready = (mem.sem(f"qk_{s}_ready") for s in ("sums", "hi", "lo"))
        stored = [mem.sem(f"qk_stored{q}") for q in range(NQ)]
        w_v = io.w_in.rearrange("a (k p) n -> p (a k) n", p=P)

        with nc.Block() as block:
            @block.sync
            def _(sp):
                def store(m):
                    for q, (c0, n) in enumerate(TOK_CHUNKS):
                        sp.wait_ge(lo_ready, NQ * m + q + 1)
                        for src, dst in ((o_hi, scr.qk_hi), (o_lo, scr.qk_lo)):
                            sp.dma_start(flat(dst[ds(m, 1), :, c0:c0 + n]), f32(src[:, c0:c0 + n])).then_inc(stored[q], 16)

                for u in range(2):
                    sp.dma_start(w_raw[:, u], w_v[:, :, u * P:(u + 1) * P]).then_inc(w_loaded[u], 16)
                with sp.Fori(0, NM // 2 - 1) as j:
                    for u in range(2):
                        sp.wait_ge(w_lo_ready, 2 * j + u + 1)
                        sp.dma_start(w_raw[:, u], w_v[:, :, ds((2 * j + u + 2) * P, P)]).then_inc(w_loaded[u], 16)
                        store(2 * j + u)
                store(NM - 2)
                store(NM - 1)
                for q in range(NQ):
                    sp.wait_ge(stored[q], 32 * NM)

            @block.gpsimd
            def _(pool):
                with pool.Fori(0, NM // 2) as j:
                    for u in range(2):
                        pool.wait_ge(w_loaded[u], 16 * j + 16)
                        pool.tensor_tensor(w_raw[:, u], w_raw[:, u], g_col[:, :].unsqueeze(2).broadcast_to([P, KD, P]),
                                           ALU.mult).then_inc(w_gained, 1)

            @block.scalar
            def _(act):
                def split(m, u, first):
                    act.wait_ge(w_gained, m + 1)
                    if not first:
                        act.wait_ge(sums_ready, NQ * (m - 1))
                    act.activation(w_hi[:, u], w_raw[:, u], ACT.Copy).then_inc(w_hi_ready, 1)

                def high(m, first):
                    for q, (c0, n) in enumerate(TOK_CHUNKS):
                        act.wait_ge(sums_ready, NQ * m + q + 1)
                        if not first:
                            act.wait_ge(stored[q], 32 * m)
                        act.activation(o_hi[:, c0:c0 + n], ps[q][:, 0:n], ACT.Copy).then_inc(hi_ready, 1)

                split(0, 0, True)
                split(1, 1, True)
                high(0, True)
                split(2, 0, False)
                high(1, False)
                with act.Fori(0, NM // 2 - 2) as j:
                    split(2 * j + 3, 1, False)
                    high(2 * j + 2, False)
                    split(2 * j + 4, 0, False)
                    high(2 * j + 3, False)
                split(NM - 1, 1, False)
                high(NM - 2, False)
                high(NM - 1, False)

            @block.vector
            def _(dve):
                def split(m, u):
                    dve.wait_ge(w_hi_ready, m + 1)
                    dve.tensor_tensor(w_lo[:, u], w_raw[:, u], f32(w_hi[:, u]), ALU.subtract).then_inc(w_lo_ready, 1)

                def low(m):
                    for q, (c0, n) in enumerate(TOK_CHUNKS):
                        dve.wait_ge(hi_ready, NQ * m + q + 1)
                        dve.tensor_tensor(o_lo[:, c0:c0 + n], ps[q][:, 0:n], f32(o_hi[:, c0:c0 + n]),
                                          ALU.subtract).then_inc(lo_ready, 1)

                split(0, 0)
                split(1, 1)
                low(0)
                split(2, 0)
                low(1)
                with dve.Fori(0, NM // 2 - 2) as j:
                    split(2 * j + 3, 1)
                    low(2 * j + 2)
                    split(2 * j + 4, 0)
                    low(2 * j + 3)
                split(NM - 1, 1)
                low(NM - 2)
                low(NM - 1)

            @block.tensor
            def _(pe):
                def product(m, u, first):
                    pe.wait_ge(w_lo_ready, m + 1)
                    for q, (c0, n) in enumerate(TOK_CHUNKS):
                        if not first:
                            pe.wait_ge(lo_ready, NQ * (m - 1) + q + 1)
                        for k in range(KD):
                            for i, (w, a) in enumerate(((w_hi, u_hi), (w_hi, u_lo), (w_lo, u_hi))):
                                t = pe.matmul(ps[q][:, 0:n], w[:, u, k], a[:, k, c0:c0 + n],
                                              start=(k == 0 and i == 0), stop=(k == KD - 1 and i == 2))
                        t.then_inc(sums_ready, 1)

                product(0, 0, True)
                product(1, 1, False)
                with pe.Fori(0, NM // 2 - 1) as j:
                    product(2 * j + 2, 0, False)
                    product(2 * j + 3, 1, False)


def cv_proj(nc, io, scr, u_hi, u_lo, g_col, ident, eps):
    W = 512
    NP = 4
    with ExitStack() as ctx:
        mem = Memory(nc, ctx)
        w_raw = mem.sb("cv_w_raw", [P, 2, KD // NP, W])
        w_hi = mem.sb("cv_w_hi", [P, KD, W], F32R)
        w_lo = mem.sb("cv_w_lo", [P, KD, W], F32R)
        trig = mem.sb("cv_trig", [P, 2, 2, ROPE])
        cn = mem.sb("cv_cn", [P, 2, W])
        tmp = mem.sb("cv_tmp", [P, 2, 2, ROPE])
        junk = mem.sb("cv_junk", [P, QR])
        ssq = mem.sb("cv_ssq", [P, 2, 2])
        std = mem.sb("cv_std", [P, 2, 2])
        rstd = mem.sb("cv_rstd", [P, 2, 2])
        o_hi = mem.sb("cv_o_hi", [P, 2, W], F32R)
        o_lo = mem.sb("cv_o_lo", [P, 2, W], F32R)
        v_out = mem.sb("cv_v_out", [P, 2, W])
        v_copied = mem.sem("cv_v_copied")
        v_stored = [mem.sem(f"cv_v_stored{u}") for u in range(2)]
        ps = [mem.ps(f"cv_ps{i}") for i in range(2)]
        pt = [mem.ps(f"cv_pt{i}") for i in range(2)]
        w_loaded = [mem.sem(f"cv_w_loaded{u}") for u in range(2)]
        w_gained, w_hi_ready, w_lo_ready = (mem.sem(f"cv_w_{s}") for s in ("gained", "hi_ready", "lo_ready"))
        trig_loaded = [mem.sem(f"cv_trig_loaded{u}") for u in range(2)]
        sums_ready, ssq_ready, root_ready, rstd_ready = (mem.sem(f"cv_{s}_ready") for s in ("sums", "ssq", "root", "rstd"))
        rot_ready, cn_ready, cT_ready = (mem.sem(f"cv_{s}_ready") for s in ("rot", "cn", "cT"))
        hi_ready, lo_ready = mem.sem("cv_hi_ready"), mem.sem("cv_lo_ready")
        stored = [mem.sem(f"cv_stored{u}") for u in range(2)]
        w_v = io.w_in.rearrange("a (k p) n -> p (a k) n", p=P)
        N = len(TILES)
        HALF = ROPE // 2
        COLS = [[(0, C_Q, QR + KVR + ROPE), (QR + KVR + ROPE, C_R + HALF, HALF), (QR + KVR + ROPE + HALF, C_R, HALF)],
                [(0, 2 * DA_W, DA_W)]]
        piece_loads = [0, 0]
        load_count = []
        for b in range(2):
            for q in range(NP):
                piece_loads[q % 2] += 16 * len(COLS[b])
                load_count.append(piece_loads[q % 2])
        KP = KD // NP

        with nc.Block() as block:
            @block.sync
            def _(sp):
                def load(b, q):
                    g = NP * b + q
                    if g >= 2:
                        sp.wait_ge(w_lo_ready, g - 1)
                    for at, c0, n in COLS[b]:
                        sp.dma_start(w_raw[:, q % 2, :, at:at + n], w_v[:, q * KP:(q + 1) * KP, c0:c0 + n]).then_inc(w_loaded[q % 2], 16)

                def load_trig(n):
                    r0, rows = TILES[n]
                    if n >= 2:
                        sp.wait_ge(rot_ready, 2 * (n - 1))
                    sp.dma_start(trig[0:rows, n % 2], io.trig_tm[r0:r0 + rows]).then_inc(trig_loaded[n % 2], 16)

                for q in range(NP):
                    load(0, q)
                load_trig(0)
                load_trig(1)
                for q in range(2):
                    load(1, q)
                for n, (r0, rows) in enumerate(TILES):
                    sp.wait_ge(lo_ready, n + 1)
                    for src, dst in ((o_hi, scr.c_hi), (o_lo, scr.c_lo)):
                        sp.dma_start(dst[:, :, r0:r0 + rows], f32(src[:, n % 2]).rearrange("p (f t) -> p f t", f=4)[:, :, 0:rows]).then_inc(stored[n % 2], 16)
                    if n + 2 < N:
                        load_trig(n + 2)
                for q in range(2, NP):
                    load(1, q)
                for n, (r0, rows) in enumerate(TILES):
                    sp.wait_ge(v_copied, n + 1)
                    sp.dma_start(scr.v[r0:r0 + rows, :], v_out[0:rows, n % 2]).then_inc(v_stored[n % 2], 16)
                for u in range(2):
                    sp.wait_ge(stored[u], 32 * len(range(u, N, 2)))
                    sp.wait_ge(v_stored[u], 16 * len(range(u, N, 2)))

            @block.gpsimd
            def _(pool):
                for g in range(2 * NP):
                    pool.wait_ge(w_loaded[g % 2], load_count[g])
                    q = g % NP
                    pool.tensor_tensor(w_raw[:, g % 2], w_raw[:, g % 2],
                                       g_col[:, q * KP:(q + 1) * KP].unsqueeze(2).broadcast_to([P, KP, W]),
                                       ALU.mult).then_inc(w_gained, 1)

            @block.scalar
            def _(act):
                def split(g):
                    act.wait_ge(w_gained, g + 1)
                    if g >= NP:
                        act.wait_ge(sums_ready, N)
                    q = g % NP
                    act.activation(w_hi[:, q * KP:(q + 1) * KP], w_raw[:, g % 2], ACT.Copy).then_inc(w_hi_ready, 1)

                def stats(n):
                    rows = TILES[n][1]
                    act.wait_ge(sums_ready, n + 1)
                    act.activation(junk[0:rows, 0:QR], ps[n % 2][0:rows, 0:QR], ACT.Square,
                                   accum_out=ssq[0:rows, n % 2, 0:1]).then_inc(ssq_ready, 1)
                    act.wait_ge(ssq_ready, 2 * n + 1)
                    act.activation(junk[0:rows, 0:KVR], ps[n % 2][0:rows, QR:QR + KVR], ACT.Square,
                                   accum_out=ssq[0:rows, n % 2, 1:2]).then_inc(ssq_ready, 1)
                    act.wait_ge(ssq_ready, 2 * n + 2)
                    act.activation(std[0:rows, n % 2, 0:1], ssq[0:rows, n % 2, 0:1], ACT.Sqrt,
                                   bias=eps[0:rows, :], scale=1.0 / QR)
                    act.activation(std[0:rows, n % 2, 1:2], ssq[0:rows, n % 2, 1:2], ACT.Sqrt,
                                   bias=eps[0:rows, :], scale=1.0 / KVR).then_inc(root_ready, 1)

                def high(n):
                    rows = TILES[n][1]
                    act.wait_ge(cT_ready, n + 1)
                    if n >= 2:
                        act.wait_ge(stored[n % 2], 32 * (n // 2))
                    act.activation(o_hi[:, n % 2].rearrange("p (f t) -> p f t", f=4)[:, :, 0:rows],
                                   pt[n % 2][:, :].rearrange("p (f t) -> p f t", f=4)[:, :, 0:rows],
                                   ACT.Copy).then_inc(hi_ready, 1)

                for g in range(NP):
                    split(g)
                for n in range(N):
                    stats(n)
                    if n:
                        high(n - 1)
                high(N - 1)
                for g in range(NP, 2 * NP):
                    split(g)
                for n in range(N):
                    m, rows = N + n, TILES[n][1]
                    act.wait_ge(sums_ready, m + 1)
                    if n >= 2:
                        act.wait_ge(v_stored[n % 2], 16 * (n // 2))
                    act.activation(v_out[0:rows, n % 2], ps[m % 2][0:rows, :], ACT.Copy).then_inc(v_copied, 1)

            @block.vector
            def _(dve):
                def split(g):
                    q = g % NP
                    dve.wait_ge(w_hi_ready, g + 1)
                    dve.tensor_tensor(w_lo[:, q * KP:(q + 1) * KP], w_raw[:, g % 2], f32(w_hi[:, q * KP:(q + 1) * KP]),
                                      ALU.subtract).then_inc(w_lo_ready, 1)

                def normalise(n):
                    u, rows = n % 2, TILES[n][1]
                    kr, swapped = QR + KVR, QR + KVR + ROPE
                    dve.wait_ge(trig_loaded[u], 16 * (n // 2) + 16)
                    dve.wait_ge(ssq_ready, 2 * n + 2)
                    dve.tensor_tensor(tmp[0:rows, u, 0], ps[u][0:rows, kr:kr + ROPE], trig[0:rows, u, 0], ALU.mult).then_inc(rot_ready, 1)
                    dve.tensor_tensor(tmp[0:rows, u, 1], ps[u][0:rows, swapped:swapped + ROPE], trig[0:rows, u, 1],
                                      ALU.mult).then_inc(rot_ready, 1)
                    dve.wait_ge(root_ready, n + 1)
                    dve.reciprocal(rstd[0:rows, u], std[0:rows, u]).then_inc(rstd_ready, 1)
                    dve.wait_ge(rot_ready, 2 * n + 2)
                    if n >= 2:
                        dve.wait_ge(cT_ready, n - 1)
                    dve.tensor_tensor(cn[0:rows, u, kr:kr + ROPE], tmp[0:rows, u, 0], tmp[0:rows, u, 1], ALU.add)
                    dve.tensor_tensor(cn[0:rows, u, swapped:swapped + ROPE], tmp[0:rows, u, 0], tmp[0:rows, u, 1], ALU.add)
                    dve.wait_ge(rstd_ready, n + 1)
                    dve.tensor_scalar(cn[0:rows, u, 0:QR], ps[u][0:rows, 0:QR], rstd[0:rows, u, 0:1], None, ALU.mult)
                    dve.tensor_scalar(cn[0:rows, u, QR:kr], ps[u][0:rows, QR:kr], rstd[0:rows, u, 1:2], None,
                                      ALU.mult).then_inc(cn_ready, 1)

                def low(m, bank):
                    rows = TILES[m][1]
                    o, h, s = (a.rearrange("p (f t) -> p f t", f=4)[:, :, 0:rows]
                               for a in (o_lo[:, m % 2], f32(o_hi[:, m % 2]), bank[:, :]))
                    dve.wait_ge(hi_ready, m + 1)
                    dve.tensor_tensor(o, s, h, ALU.subtract).then_inc(lo_ready, 1)

                for g in range(NP):
                    split(g)
                for n in range(N):
                    normalise(n)
                    if n:
                        low(n - 1, pt[(n - 1) % 2])
                low(N - 1, pt[(N - 1) % 2])
                for g in range(NP, 2 * NP):
                    split(g)

            @block.tensor
            def _(pe):
                def product(m):
                    c0, rows = TILES[m % N]
                    if m >= N + 2:
                        pe.wait_ge(v_copied, m - 1 - N)
                    elif m >= 2:
                        pe.wait_ge(cn_ready, m - 1)
                    for k in range(KD):
                        if m % N == 0 and k % KP == 0:
                            pe.wait_ge(w_lo_ready, NP * (m // N) + k // KP + 1)
                        for i, (a, w) in enumerate(((u_hi, w_hi), (u_hi, w_lo), (u_lo, w_hi))):
                            t = pe.matmul(ps[m % 2][0:rows, :], a[:, k, c0:c0 + rows], w[:, k],
                                          start=(k == 0 and i == 0), stop=(k == KD - 1 and i == 2))
                    t.then_inc(sums_ready, 1)

                def turn(n):
                    rows = TILES[n][1]
                    pe.wait_ge(cn_ready, n + 1)
                    if n >= 2:
                        pe.wait_ge(lo_ready, n - 1)
                    for f in range(4):
                        t = pe.transpose(pt[n % 2][:, f * P:f * P + rows], cn[0:rows, n % 2, f * P:(f + 1) * P],
                                         ident[0:rows, 0:rows])
                    t.then_inc(cT_ready, 1)

                for n in range(N):
                    product(n)
                    if n:
                        turn(n - 1)
                turn(N - 1)
                for n in range(N):
                    product(N + n)


def mla_up(nc, io, scr):
    NQF, NR = MLA_H * NOPE, MLA_H * ROPE
    WQ = NQF + 2 * NR
    WKV = MLA_H * (NOPE + MLA_V)
    KQ = QR // P
    HALF = ROPE // 2
    with ExitStack() as ctx:
        mem = Memory(nc, ctx)
        c_hi = mem.sb("mu_c_hi", [P, KQ + 1, L], F32R)
        c_lo = mem.sb("mu_c_lo", [P, KQ + 1, L], F32R)
        w_raw = mem.sb("mu_w_raw", [P, KQ * WQ + WKV])
        w_hi = mem.sb("mu_w_hi", [P, KQ * WQ + WKV], F32R)
        w_lo = mem.sb("mu_w_lo", [P, KQ * WQ + WKV], F32R)
        g_q = mem.sb("mu_g_q", [P, KQ])
        g_kv = mem.sb("mu_g_kv", [P, 1])
        trig = mem.sb("mu_trig", [P, 2, SEQ])
        rot = mem.sb("mu_rot", [P, 2, 2, 512])
        NS = 4
        o_hi = mem.sb("mu_o_hi", [P, NS, 512], F32R)
        o_lo = mem.sb("mu_o_lo", [P, NS, 512], F32R)
        NB = 6
        ps = [mem.ps(f"mu_ps{i}") for i in range(NB)]
        c_loaded, w_loaded, trig_loaded = mem.sem("mu_c_loaded"), mem.sem("mu_w_loaded"), mem.sem("mu_trig_loaded")
        w_gained, w_hi_ready, w_lo_ready = (mem.sem(f"mu_w_{s}") for s in ("gained", "hi_ready", "lo_ready"))
        sums_ready, rot_ready, hi_ready, lo_ready = (mem.sem(f"mu_{s}_ready") for s in ("sums", "rot", "hi", "lo"))
        rotated = mem.sem("mu_rotated")
        stored = [mem.sem(f"mu_stored{u}") for u in range(NS)]
        q_w = [w[:, 0:KQ * WQ].rearrange("p (k n) -> p k n", k=KQ) for w in (w_raw, w_hi, w_lo)]
        kv_w = [w[:, KQ * WQ:KQ * WQ + WKV] for w in (w_raw, w_hi, w_lo)]

        jobs = []
        for p in range(NR // P):
            for c0, n in TOK_CHUNKS[1:]:
                jobs.append(("rope", NQF + p * P, (c0, n), (scr.mqr_hi[p], scr.mqr_lo[p])))
        for h in range(MLA_H):
            jobs += [("q", h * NOPE, t, (scr.mq_hi[h], scr.mq_lo[h])) for t in TOK_CHUNKS[1:]]
            jobs += [("k", h * NOPE, t, (scr.mk_hi[h], scr.mk_lo[h])) for t in TOK_CHUNKS]
        jobs += [("v", MLA_H * NOPE, t, (scr.mv,)) for t in TILES]
        stores = [sum(16 * len(b[3]) for b in jobs[i % NS:i:NS]) for i in range(len(jobs))]
        bank, first_banks, ropes = 0, [], []
        for kind, *_ in jobs:
            first_banks.append(bank)
            ropes.append(sum(b == "rope" for b, *_ in jobs[:len(ropes)]))
            bank += 2 if kind == "rope" else 1

        def size(job):
            kind, _, (c0, n), _ = job
            return (n, 512) if kind == "v" else (P, n)

        def before(first, last):
            return max((i for i, b in enumerate(first_banks) for w in range(2 if jobs[i][0] == "rope" else 1)
                        if b + w <= last - NB), default=None)

        with nc.Block() as block:
            @block.sync
            def _(sp):
                for k in range(KQ):
                    for src, dst in ((scr.c_hi, c_hi), (scr.c_lo, c_lo)):
                        sp.dma_start(f32(dst[:, k]), src[:, k]).then_inc(c_loaded, 16)
                    src = io.w_q_up[0, k * P:(k + 1) * P, :].rearrange("p (h n) -> p h n", h=MLA_H)
                    to = q_w[0][:, k]
                    swapped = to[:, NQF + NR:WQ].rearrange("p (h n) -> p h n", h=MLA_H)
                    for dst, part in ((to[:, 0:NQF].rearrange("p (h n) -> p h n", h=MLA_H), src[:, :, 0:NOPE]),
                                      (to[:, NQF:NQF + NR].rearrange("p (h n) -> p h n", h=MLA_H), src[:, :, NOPE:NOPE + ROPE]),
                                      (swapped[:, :, 0:HALF], src[:, :, NOPE + HALF:NOPE + ROPE]),
                                      (swapped[:, :, HALF:ROPE], src[:, :, NOPE:NOPE + HALF])):
                        sp.dma_start(dst, part).then_inc(w_loaded, 16)
                for src, dst in ((scr.c_hi, c_hi), (scr.c_lo, c_lo)):
                    sp.dma_start(f32(dst[:, KQ]), src[:, KQ]).then_inc(c_loaded, 16)
                src = io.w_kv_up[0].rearrange("p (h n) -> p h n", h=MLA_H)
                for part in range(2):
                    sp.dma_start(kv_w[0][:, part * 512:(part + 1) * 512].rearrange("p (h n) -> p h n", h=MLA_H),
                                 src[:, :, part * NOPE:part * NOPE + 128]).then_inc(w_loaded, 16)
                sp.dma_start(g_q[:, :], io.g_mla_q).then_inc(w_loaded, 16)
                sp.dma_start(g_kv[:, :], io.g_mla_kv).then_inc(w_loaded, 16)
                sp.dma_start(trig[:, :, :], io.trig_fm).then_inc(trig_loaded, 16)
                for i, job in enumerate(jobs):
                    kind, _, (c0, n), dsts = job
                    rows, cols = size(job)
                    sp.wait_ge(hi_ready if kind == "v" else lo_ready, i + 1)
                    for src, dst in zip((o_hi, o_lo), dsts):
                        if kind == "v":
                            dst = dst[c0:c0 + n, :]
                        elif kind == "k":
                            dst = dst[:, c0:c0 + n]
                        else:
                            dst = dst[:, c0 - META:c0 - META + n]
                        sp.dma_start(dst, f32(src[0:rows, i % NS, 0:cols])).then_inc(stored[i % NS], 16)
                for u in range(NS):
                    sp.wait_ge(stored[u], sum(16 * len(b[3]) for b in jobs[u::NS]))

            @block.gpsimd
            def _(pool):
                pool.wait_ge(w_loaded, 16 * (4 * KQ + 4))
                for k in range(KQ):
                    pool.tensor_scalar(q_w[0][:, k], q_w[0][:, k], g_q[:, k:k + 1], 1.0, ALU.mult, ALU.mult).then_inc(w_gained, 1)
                pool.tensor_scalar(kv_w[0], kv_w[0], g_kv[:, :], 1.0, ALU.mult, ALU.mult).then_inc(w_gained, 1)
                r = 0
                for i, job in enumerate(jobs):
                    if job[0] == "rope":
                        pool.wait_ge(rot_ready, 2 * r + 2)
                        pool.tensor_tensor(rot[:, r % 2, 0], rot[:, r % 2, 0], rot[:, r % 2, 1], ALU.add).then_inc(rotated, 1)
                        r += 1

            @block.scalar
            def _(act):
                for g in range(KQ + 1):
                    act.wait_ge(w_gained, g + 1)
                    dst, src = (q_w[1][:, g], q_w[0][:, g]) if g < KQ else (kv_w[1], kv_w[0])
                    act.activation(dst, src, ACT.Copy).then_inc(w_hi_ready, 1)
                for i, job in enumerate(jobs):
                    rows, cols = size(job)
                    if i >= NS:
                        act.wait_ge(stored[i % NS], stores[i])
                    if job[0] == "rope":
                        act.wait_ge(rotated, ropes[i] + 1)
                        src = rot[:, ropes[i] % 2, 0]
                    else:
                        act.wait_ge(sums_ready, i + 1)
                        src = ps[first_banks[i] % NB][0:rows, 0:cols]
                    dst = o_hi[0:rows, i % NS, 0:cols]
                    act.activation(f32(dst) if job[0] == "v" else dst, src, ACT.Copy).then_inc(hi_ready, 1)

            @block.vector
            def _(dve):
                for g in range(KQ + 1):
                    dve.wait_ge(w_hi_ready, g + 1)
                    dst, hi, src = (q_w[2][:, g], q_w[1][:, g], q_w[0][:, g]) if g < KQ else (kv_w[2], kv_w[1], kv_w[0])
                    dve.tensor_tensor(dst, src, f32(hi), ALU.subtract).then_inc(w_lo_ready, 1)
                dve.wait_ge(trig_loaded, 16)
                for i, job in enumerate(jobs):
                    kind, _, (c0, n), _ = job
                    rows, cols = size(job)
                    if kind == "v":
                        break
                    if kind == "rope":
                        dve.wait_ge(sums_ready, i + 1)
                        if ropes[i] >= 2:
                            dve.wait_ge(lo_ready, ropes[i] - 1)
                        for part in range(2):
                            dve.tensor_tensor(rot[:, ropes[i] % 2, part], ps[(first_banks[i] + part) % NB][:, :],
                                              trig[:, part, c0 - META:c0 - META + n], ALU.mult).then_inc(rot_ready, 1)
                        src = rot[:, ropes[i] % 2, 0]
                    else:
                        src = ps[first_banks[i] % NB][0:rows, 0:cols]
                    dve.wait_ge(hi_ready, i + 1)
                    dve.tensor_tensor(o_lo[0:rows, i % NS, 0:cols], src, f32(o_hi[0:rows, i % NS, 0:cols]),
                                      ALU.subtract).then_inc(lo_ready, 1)

            @block.tensor
            def _(pe):
                pe.wait_ge(w_lo_ready, KQ + 1)
                pe.wait_ge(c_loaded, 16 * 2 * (KQ + 1))
                for i, job in enumerate(jobs):
                    kind, w0, (c0, n), _ = job
                    banks = [first_banks[i], first_banks[i] + 1] if kind == "rope" else [first_banks[i]]
                    last = before(banks[0], banks[-1])
                    if last is not None:
                        pe.wait_ge(hi_ready if jobs[last][0] == "v" else lo_ready, last + 1)
                    for part, bank in enumerate(banks):
                        steps = [(k, i3) for k in (range(KQ) if kind in ("q", "rope") else range(1)) for i3 in range(3)]
                        for k, i3 in steps:
                            wi, ci = ((1, c_hi), (1, c_lo), (2, c_hi))[i3]
                            if kind in ("q", "rope"):
                                w = q_w[wi][:, k, w0 + part * NR:w0 + part * NR + P]
                                c = ci[:, k, c0:c0 + n]
                            else:
                                w = kv_w[wi][:, w0:w0 + (512 if kind == "v" else P)]
                                c = ci[:, KQ, c0:c0 + n]
                            first, stop = (k, i3) == steps[0], (k, i3) == steps[-1]
                            if kind == "v":
                                t = pe.matmul(ps[bank % NB][0:n, :], c, w, start=first, stop=stop)
                            else:
                                t = pe.matmul(ps[bank % NB][:, 0:n], w, c, start=first, stop=stop)
                    t.then_inc(sums_ready, 1)


def row_chunks(i):
    width = META + P * (i + 1)
    n = -(-width // 512)
    step = -(-width // n // 4) * 4
    return [(c, min(step, width - c)) for c in range(0, width, step)]


def attention(nc, io, scr, ident_d, da):
    name = "da" if da else "ml"
    H = DA_H if da else MLA_H
    COMPS = 2 if da else 1
    NG = NT // 4
    scale = DA_SCALE if da else MLA_SCALE
    NKB = 4 if da else 2
    with ExitStack() as ctx:
        mem = Memory(nc, ctx)
        keys = mem.sb(f"{name}_keys", [P, 2, NKB, L], F32R)
        rope_keys = None if da else mem.sb("ml_rope_keys", [P, 2, L], F32R)
        NQB = 2 if da else 3
        qs = mem.sb(f"{name}_qs", [P, 2, NQB, 512], F32R)
        v = mem.sb(f"{name}_v", [P, NT, P])
        v_meta = mem.sb(f"{name}_v_meta", [META, P])
        bias = mem.sb(f"{name}_bias", [P, 2 if da else 1, L])
        rows_even = mem.sb(f"{name}_rows_even", [P, 4, META + 1536])
        rows_odd = mem.sb(f"{name}_rows_odd", [P, 4, L])
        second = mem.sb(f"{name}_second", [P, 2, L]) if da else None
        NPT = 4
        DVE_EVERY = 6 if da else 2
        pT = mem.sb(f"{name}_pT", [P, NPT, 512])
        o_out = mem.sb(f"{name}_o_out", [P, 2, 512])
        ident = mem.sb(f"{name}_ident", [P, P])
        mx = mem.sb(f"{name}_mx", [P, 2, COMPS, 5])
        nmax = mem.sb(f"{name}_nmax", [P, 2, COMPS])
        nmax_all = mem.sb(f"{name}_nmax_all", [P, 5])
        total = mem.sb(f"{name}_total", [P, 2, COMPS])
        inv = mem.sb(f"{name}_inv", [P, 2, COMPS])
        inv2 = mem.sb(f"{name}_inv2", [P, 2])
        lam_in = mem.sb(f"{name}_lam_in", [P, 4, DA_HD])
        lam = mem.sb(f"{name}_lam", [P, 4])
        NSB = 4
        ps_s = [mem.ps(f"{name}_ps_s{i}") for i in range(NSB)]
        NTB = 3
        ps_t = [mem.ps(f"{name}_ps_t{i}") for i in range(NTB)]
        ps_o = mem.ps(f"{name}_ps_o")
        const_loaded = mem.sem(f"{name}_const_loaded")
        lam_step = mem.sem(f"{name}_lam_step")
        lam_exp = mem.sem(f"{name}_lam_exp")
        keys_loaded = [mem.sem(f"{name}_keys_loaded{u}") for u in range(2)]
        bias_loaded = [mem.sem(f"{name}_bias_loaded{u}") for u in range(2)]
        q_loaded = [mem.sem(f"{name}_q_loaded{u}") for u in range(2)]
        v_loaded = [mem.sem(f"{name}_v_loaded{g}") for g in range(NG)]
        scores_ready, scores_read = mem.sem(f"{name}_scores_ready"), mem.sem(f"{name}_scores_read")
        max_ready, exp_ready = mem.sem(f"{name}_max_ready"), mem.sem(f"{name}_exp_ready")
        inv_ready, first_scaled, probs_ready = (mem.sem(f"{name}_{s}") for s in ("inv_ready", "first_scaled", "probs_ready"))
        inv2_step = mem.sem(f"{name}_inv2_step")
        pT_ready, pv_done = mem.sem(f"{name}_pT_ready"), mem.sem(f"{name}_pv_done")
        act_copied, dve_copied = mem.sem(f"{name}_act_copied"), mem.sem(f"{name}_dve_copied")
        o_copied = mem.sem(f"{name}_o_copied")
        o_stored = [mem.sem(f"{name}_o_stored{u}") for u in range(2)]

        chunks = [(i, c, k0, n) for i in range(NT) for c in range(COMPS) for k0, n in row_chunks(i)]
        NCH = len(chunks)
        tiles_of = lambda g: 1 + 4 * (g + 1)
        NKT = sum(tiles_of(g) for g in range(NG))
        kt_base = [sum(tiles_of(a) for a in range(g)) for g in range(NG)]
        KEY_LOADS = {True: 8, False: 2}[da]
        Q_LOADS = {True: 4, False: 4}[da]

        def row(i):
            buf = rows_odd if (i // 4) % 2 else rows_even
            return buf[:, i % 4, 0:META + P * (i + 1)]

        def comp_row(i, c):
            return row(i) if c == 0 else second[:, i % 2, 0:META + P * (i + 1)]

        def head_steps(carried):
            steps, later = [], list(carried)

            def pass_by(chunk_count=1):
                nonlocal later
                later = [(left - chunk_count, step) for left, step in later]
                steps.extend(step for left, step in later if left <= 0)
                later = [(left, step) for left, step in later if left > 0]

            def end(i):
                while any(step[0] == "end" and step[2] - NT * step[1] == i for _, step in later):
                    pass_by()

            for g in range(NG):
                back, vg = (0, g - 1) if g else (1, NG - 1)
                mine = [n for n, ch in enumerate(chunks) if ch[0] // 4 == g]
                lead = sum(1 for n in mine if chunks[n][0] < 4 * g + LEAD_TILES[g])
                places, done = tiles_of(vg) + 2, 0
                for at, n in enumerate(mine):
                    i, c, k0, w = chunks[n]
                    if c == 0 and k0 == 0:
                        end(i - 2)
                    steps.append(("chunk", 0, n))
                    pass_by()
                    if k0 + w == META + P * (i + 1):
                        later.append((1, ("exp", 0, i, c)))
                        if c == 0:
                            later.append((SCALE_AFTER, ("scale", 0, i)))
                        if c == COMPS - 1:
                            later.append((END_AFTER, ("end", 0, i)))
                    while at >= lead and done < -(-places * (at + 1 - lead) // (len(mine) - lead)):
                        if done == 0:
                            end(4 * vg + 3 - NT * back)
                        if done < places - 2:
                            steps.append(("turn", back, vg, done))
                        if done >= 2:
                            steps.append(("product", back, vg, done - 2))
                        done += 1
                steps.append(("out", back, vg))
            return steps, [(left, (step[0], 1) + step[2:]) for left, step in later]

        LEAD_TILES = (2, 1, 1, 1)
        SCALE_AFTER, END_AFTER = (2, 4) if da else (2, 2)
        STEPS = head_steps(head_steps([])[1])[0]

        def walk(h, handlers, back=(0, 1)):
            for kind, b, *args in STEPS:
                if b in back and kind in handlers:
                    handlers[kind](h - b if b else h, *args)

        def heads(engine, handlers):
            def head(h, pair, u, back=(0, 1)):
                walk(h, {kind: (lambda hh, *args, f=f: f(hh, *args, pair=pair, u=u)) for kind, f in handlers.items()}, back)

            head(0, 0, 0, (0,))
            with engine.Fori(0, H // 2 - 1) as j:
                head(2 * j + 1, j, 1)
                head(2 * j + 2, j + 1, 0)
            head(H - 1, H // 2 - 1, 1)
            head(H, H // 2, 0, (1,))

        def key_cols(t):
            return (0, META) if t == 0 else (META + P * (t - 1), P)

        def first_tile(g, t):
            return max(0, t - 1 - 4 * g)

        BY_DVE = [at % DVE_EVERY == 1 for at in range(NKT)]

        def slot_free(engine, h, n):
            if not (isinstance(h, int) and h == 0 and n < NPT):
                engine.wait_ge(pv_done, NKT * h + n - NPT + 1)

        with nc.Block() as block:
            @block.sync
            def _(sp):
                def load_keys(h, u):
                    if da:
                        for c in range(2):
                            rows = slice(c * DA_HD, (c + 1) * DA_HD)
                            for j, src in enumerate((scr.qk_hi, scr.qk_lo)):
                                for half in range(2):
                                    sp.dma_start(f32(keys[half * 64:half * 64 + 64, u, 2 * c + j]),
                                                 flat(src[ds(h + DA_H, 1), rows, :])).then_inc(keys_loaded[u], 16)
                    else:
                        for j, src in enumerate((scr.mk_hi, scr.mk_lo)):
                            sp.dma_start(f32(keys[:, u, j]), flat(src[ds(h, 1), :, :])).then_inc(keys_loaded[u], 16)
                    if da:
                        sp.dma_start(bias[:, u], flat(io.bias[ds(h, 1), :, :])).then_inc(bias_loaded[u], 16)

                def load_q(h, pair, u, g):
                    cols = slice(512 * g, 512 * g + 512)
                    if da:
                        for c in range(2):
                            for j, src in enumerate((scr.qk_hi, scr.qk_lo)):
                                sp.dma_start(f32(qs[64 * j:64 * j + 64, g % 2, c]),
                                             flat(src[ds(h, 1), c * 64:c * 64 + 64, META + 512 * g:META + 512 * g + 512])).then_inc(q_loaded[g % 2], 16)
                    else:
                        for j, src in enumerate((scr.mq_hi, scr.mq_lo)):
                            sp.dma_start(f32(qs[:, g % 2, j]), flat(src[ds(h, 1), :, cols])).then_inc(q_loaded[g % 2], 16)
                        for j, src in enumerate((scr.mqr_hi, scr.mqr_lo)):
                            sp.dma_start(f32(qs[64 * j:64 * j + 64, g % 2, 2]),
                                         flat(src[ds(pair, 1), u * 64:u * 64 + 64, cols])).then_inc(q_loaded[g % 2], 16)

                def load_v(h, g):
                    src = scr.v if da else scr.mv
                    cols = ds(h * P, P)
                    sp.dma_start(v[:, 4 * g:4 * g + 4, :],
                                 src[META + 512 * g:META + 512 * g + 512, cols].rearrange("(t p) n -> p t n", p=P)).then_inc(v_loaded[g], 16)
                    if g == 0:
                        sp.dma_start(v_meta[:, :], src[0:META, cols]).then_inc(v_loaded[g], 16)

                def store(h, g):
                    sp.wait_ge(o_copied, NG * h + g + 1)
                    sp.dma_start(flat(scr.yT[ds(h + (0 if da else DA_H), 1), :, 512 * g:512 * g + 512]), o_out[:, g % 2]).then_inc(o_stored[g % 2], 16)

                def scores_done(h, g):
                    sp.wait_ge(scores_ready, NCH * h + sum(1 for i, *_ in chunks if i < 4 * (g + 1)))

                def head(h, pair, u):
                    first, last = isinstance(h, int) and h == 0, isinstance(h, int) and h == H - 1
                    scores_done(h, 0)
                    load_q(h, pair, u, 2)
                    if not first:
                        for g in range(NG):
                            sp.wait_ge(pv_done, NKT * (h - 1) + kt_base[NG - 1] + 5 + 4 * g)
                            load_v(h, g)
                        store(h - 1, NG - 1)
                    if not last:
                        if not first:
                            sp.wait_ge(scores_read, NCH * h)
                        load_keys(h + 1, 1 - u)
                    scores_done(h, 1)
                    load_q(h, pair, u, 3)
                    store(h, 0)
                    if not last:
                        scores_done(h, 2)
                        load_q(h + 1, pair + u, 1 - u, 0)
                    store(h, 1)
                    if not last:
                        scores_done(h, 3)
                        load_q(h + 1, pair + u, 1 - u, 1)
                    store(h, 2)

                load_keys(0, 0)
                load_q(0, 0, 0, 0)
                load_q(0, 0, 0, 1)
                sp.dma_start(ident[:, :], ident_d).then_inc(const_loaded, 16)
                if da:
                    for j, src in enumerate((io.lam_q1, io.lam_k1, io.lam_q2, io.lam_k2)):
                        sp.dma_start(lam_in[:, j], src.broadcast_to([P, DA_HD])).then_inc(const_loaded, 16)
                else:
                    sp.dma_start(bias[:, 0], io.bias[DA_H]).then_inc(const_loaded, 16)
                    for j, src in enumerate((scr.c_hi, scr.c_lo)):
                        sp.dma_start(f32(rope_keys[:, j]), src[:, 3]).then_inc(const_loaded, 16)
                for g in range(NG):
                    load_v(0, g)
                head(0, 0, 0)
                with sp.Fori(0, H // 2 - 1) as j:
                    head(2 * j + 1, j, 1)
                    head(2 * j + 2, j + 1, 0)
                head(H - 1, H // 2 - 1, 1)
                store(H - 1, NG - 1)
                for u in range(2):
                    sp.wait_ge(o_stored[u], 16 * 2 * H)

            @block.gpsimd
            def _(pool):
                def scaled(h, i, **at):
                    hold(pool, inv_ready, NT * h + i + 1)
                    pool.tensor_scalar(row(i), row(i), inv[:, i % 2, 0:1], 1.0, ALU.mult,
                                       ALU.mult).then_inc(first_scaled if da else probs_ready, 1)

                heads(pool, {"scale": scaled})

            @block.scalar
            def _(act):
                def exp(h, i, c, **at):
                    act.wait_ge(max_ready, NT * COMPS * h + COMPS * i + c + 1)
                    act.activation(comp_row(i, c), comp_row(i, c), ACT.Exp, bias=nmax[:, i % 2, c:c + 1], scale=scale,
                                   accum_out=total[:, i % 2, c:c + 1]).then_inc(exp_ready, 1)

                def copy(h, g, t, **at):
                    n = kt_base[g] + t
                    if not BY_DVE[n]:
                        c0 = P * first_tile(g, t)
                        rows = key_cols(t)[1]
                        slot_free(act, h, n)
                        act.wait_ge(pT_ready, NKT * h + n + 1)
                        act.activation(pT[0:rows, n % NPT, c0:512], ps_t[n % NTB][0:rows, c0:512], ACT.Copy).then_inc(act_copied, 1)

                def out(h, g, **at):
                    act.wait_ge(pv_done, NKT * h + kt_base[g] + tiles_of(g))
                    if not (isinstance(h, int) and h == 0 and g < 2):
                        act.wait_ge(o_stored[g % 2], 16 * (2 * h + g // 2))
                    act.activation(o_out[:, g % 2], ps_o[:, :], ACT.Copy).then_inc(o_copied, 1)

                if da:
                    for j in range(2):
                        act.wait_ge(lam_step, j + 1)
                        act.activation(lam[:, j:j + 1], lam[:, j:j + 1], ACT.Exp).then_inc(lam_exp, 1)
                heads(act, {"exp": exp, "turn": copy, "out": out})

            @block.vector
            def _(dve):
                def chunk(h, n, pair, u):
                    i, c, k0, w = chunks[n]
                    g = i // 4
                    if n == 0 and da:
                        dve.wait_ge(bias_loaded[u], 16 * (pair + 1))
                    if i % 4 == 0 and c == 0 and k0 == 0 and not (isinstance(h, int) and h == 0 and g < 2):
                        if g >= 2:
                            dve.wait_ge(pT_ready, NKT * h + kt_base[g - 2] + tiles_of(g - 2))
                        else:
                            dve.wait_ge(pT_ready, NKT * (h - 1) + kt_base[g + 2] + tiles_of(g + 2))
                    nth = sum(1 for m in range(n) if chunks[m][:2] == (i, c))
                    b0 = (NT - 1 - i) * P + k0
                    hold(dve, scores_ready, NCH * h + n + 1)
                    dve.tensor_tensor_reduce(out=comp_row(i, c)[:, k0:k0 + w], in0=ps_s[n % NSB][:, 0:w],
                                             in1=bias[:, u if da else 0, b0:b0 + w], scale=1.0, scalar=LOWEST,
                                             op0=ALU.add, op1=ALU.max,
                                             accum_out=mx[:, i % 2, c, nth:nth + 1]).then_inc(scores_read, 1)
                    if k0 + w == META + P * (i + 1):
                        dve.wait_ge(scores_read, NCH * h + n + 1)
                        dve.tensor_scalar(nmax_all[:, 0:nth + 1], mx[:, i % 2, c, 0:nth + 1], -scale, None, ALU.mult, ALU.min,
                                          accum_out=nmax[:, i % 2, c:c + 1]).then_inc(max_ready, 1)

                def invert(h, i, **at):
                    dve.wait_ge(exp_ready, NT * COMPS * h + COMPS * i + 1)
                    if not (isinstance(h, int) and h == 0 and i < 2):
                        dve.wait_ge(first_scaled if da else probs_ready, NT * h + i - 1)
                    dve.reciprocal(inv[:, i % 2, 0:1], total[:, i % 2, 0:1]).then_inc(inv_ready, 1)

                def end(h, i, **at):
                    if not da:
                        return
                    n = 2 * (NT * h + i)
                    dve.wait_ge(exp_ready, NT * COMPS * h + COMPS * (i + 1))
                    dve.reciprocal(inv[:, i % 2, 1:2], total[:, i % 2, 1:2]).then_inc(inv2_step, 1)
                    dve.wait_ge(inv2_step, n + 1)
                    dve.tensor_scalar(inv2[:, i % 2:i % 2 + 1], inv[:, i % 2, 1:2], lam[:, 3:4], None, ALU.mult).then_inc(inv2_step, 1)
                    dve.wait_ge(inv2_step, n + 2)
                    dve.wait_ge(first_scaled, NT * h + i + 1)
                    dve.scalar_tensor_tensor(out=row(i), in0=comp_row(i, 1), scalar=inv2[:, i % 2:i % 2 + 1], in1=row(i),
                                             op0=ALU.mult, op1=ALU.add).then_inc(probs_ready, 1)

                def copy(h, g, t, **at):
                    n = kt_base[g] + t
                    if BY_DVE[n]:
                        c0 = P * first_tile(g, t)
                        rows = key_cols(t)[1]
                        slot_free(dve, h, n)
                        dve.wait_ge(pT_ready, NKT * h + n + 1)
                        dve.tensor_copy(pT[0:rows, n % NPT, c0:512], ps_t[n % NTB][0:rows, c0:512]).then_inc(dve_copied, 1)

                dve.wait_ge(const_loaded, 16 * (5 if da else 4))
                if da:
                    for j in range(2):
                        dve.tensor_tensor_reduce(out=lam_in[:, 2 * j], in0=lam_in[:, 2 * j], in1=lam_in[:, 2 * j + 1], scale=1.0,
                                                 scalar=0.0, op0=ALU.mult, op1=ALU.add, accum_out=lam[:, j:j + 1]).then_inc(lam_step, 1)
                    dve.wait_ge(lam_exp, 2)
                    dve.tensor_tensor(lam[:, 2:3], lam[:, 1:2], lam[:, 0:1], ALU.subtract).then_inc(lam_step, 1)
                    dve.wait_ge(lam_step, 3)
                    dve.tensor_scalar(lam[:, 3:4], lam[:, 2:3], -LAMBDA_INIT, None, ALU.add).then_inc(lam_step, 1)
                    dve.wait_ge(lam_step, 4)
                heads(dve, {"chunk": chunk, "scale": invert, "end": end, "turn": copy})

            @block.tensor
            def _(pe):
                def chunk(h, n, pair, u):
                    i, c, k0, w = chunks[n]
                    g, b = i // 4, i % 4
                    if n == 0:
                        pe.wait_ge(keys_loaded[u], 16 * KEY_LOADS * (pair + 1))
                    if b == 0 and c == 0 and k0 == 0:
                        pe.wait_ge(q_loaded[g % 2], 16 * Q_LOADS * (2 * h + g // 2 + 1))
                    if not (isinstance(h, int) and h == 0 and n < NSB):
                        pe.wait_ge(scores_read, NCH * h + n - NSB + 1)
                    cols = slice(P * b, P * b + P)
                    if da:
                        pairs = [(qs[:, g % 2, c, cols], keys[:, u, 2 * c + j, k0:k0 + w]) for j in range(2)]
                    else:
                        q_hi, q_lo, q_rope = (qs[:, g % 2, j, cols] for j in range(3))
                        k_hi, k_lo = (keys[:, u, j, k0:k0 + w] for j in range(2))
                        pairs = [(q_hi, k_hi), (q_hi, k_lo), (q_lo, k_hi)]
                        pairs += [(q_rope, rope_keys[:, j, k0:k0 + w]) for j in range(2)]
                    for j, (q, k) in enumerate(pairs):
                        m = pe.matmul(ps_s[n % NSB][:, 0:w], q, k, start=j == 0, stop=j == len(pairs) - 1)
                    m.then_inc(scores_ready, 1)

                def turn(h, g, t, **at):
                    if t == 0:
                        pe.wait_ge(probs_ready, NT * h + 4 * g + 4)
                    n, (k0, rows) = kt_base[g] + t, key_cols(t)
                    for b in range(first_tile(g, t), 4):
                        m = pe.transpose(ps_t[n % NTB][0:rows, P * b:P * b + P], row(4 * g + b)[:, k0:k0 + rows], ident[:, :])
                    m.then_inc(pT_ready, 1)

                def product(h, g, t, **at):
                    n, rows = kt_base[g] + t, key_cols(t)[1]
                    by_dve = sum(BY_DVE[:n + 1])
                    if BY_DVE[n]:
                        pe.wait_ge(dve_copied, sum(BY_DVE) * h + by_dve)
                    else:
                        pe.wait_ge(act_copied, (NKT - sum(BY_DVE)) * h + n + 1 - by_dve)
                    if t == 0:
                        pe.wait_ge(v_loaded[0], 32 * (h + 1))
                        if not (isinstance(h, int) and h == 0 and g == 0):
                            pe.wait_ge(o_copied, NG * h + g)
                    elif t % 4 == 1 and t > 1:
                        pe.wait_ge(v_loaded[t // 4], 16 * (h + 1))
                    c0 = P * first_tile(g, t)
                    pe.matmul(ps_o[:, c0:512], v_meta[:, :] if t == 0 else v[:, t - 1], pT[0:rows, n % NPT, c0:512],
                              start=t == 0, stop=t == tiles_of(g) - 1).then_inc(pv_done, 1)

                pe.wait_ge(const_loaded, 16 * (5 if da else 4))
                heads(pe, {"chunk": chunk, "turn": turn, "product": product})


def mix_out(nc, io, scr):
    with ExitStack() as ctx:
        mem = Memory(nc, ctx)
        w_raw = mem.sb("mo_w_raw", [P, 2, D])
        w_hi = mem.sb("mo_w_hi", [P, KD, D], F32R)
        w_lo = mem.sb("mo_w_lo", [P, KD, D], F32R)
        g_sub = mem.sb("mo_g_sub", [P, 2])
        ones = mem.sb("mo_ones", [P, P])
        eps = mem.sb("mo_eps", [P, 1])
        ident = mem.sb("mo_ident", [P, P])
        g_post = mem.sb("mo_g_post", [P, D])
        y = mem.sb("mo_y", [P, 2, KD, P])
        y_hi = mem.sb("mo_y_hi", [P, 2, KD, P], F32R)
        y_lo = mem.sb("mo_y_lo", [P, 2, KD, P], F32R)
        sq = mem.sb("mo_sq", [P, DA_H * P])
        y_rstd = mem.sb("mo_y_rstd", [P, DA_H * P])
        xres = mem.sb("mo_xres", [P, 2, D])
        h = mem.sb("mo_h", [P, 2, D])
        hn = mem.sb("mo_hn", [P, 2, D])
        junk = mem.sb("mo_junk", [P, D])
        u_hi = mem.sb("mo_u_hi", [P, 2, KD, P], F32R)
        u_lo = mem.sb("mo_u_lo", [P, 2, KD, P], F32R)
        stat = mem.sb("mo_stat", [P, 2, 6])
        ps_r = mem.ps("mo_ps_r")
        ps_m = [mem.ps(f"mo_ps_m{i}", D) for i in range(2)]
        ps_t = mem.ps("mo_ps_t", D)
        const_loaded, const_set = mem.sem("mo_const_loaded"), mem.sem("mo_const_set")
        w_loaded = [mem.sem(f"mo_w_loaded{u}") for u in range(2)]
        w_gained, w_hi_ready, w_lo_ready = (mem.sem(f"mo_w_{s}") for s in ("gained", "hi_ready", "lo_ready"))
        y_loaded = [mem.sem(f"mo_y_loaded{u}") for u in range(2)]
        x_loaded = [mem.sem(f"mo_x_loaded{u}") for u in range(2)]
        sq_ready, mean_ready, y_log_ready, y_rstd_ready, y_normed = (mem.sem(f"mo_y_{s}") for s in ("sq", "mean", "log", "rstd", "normed"))
        y_hi_ready, y_lo_ready, mix_ready = (mem.sem(f"mo_{s}") for s in ("y_hi_ready", "y_lo_ready", "mix_ready"))
        stat_step = mem.sem("mo_stat_step")
        post_ready, h_ready, hn_ready, hT_ready = (mem.sem(f"mo_{s}_ready") for s in ("post", "h", "hn", "hT"))
        u_hi_ready, u_lo_ready = mem.sem("mo_u_hi_ready"), mem.sem("mo_u_lo_ready")
        h_stored = [mem.sem(f"mo_h_stored{u}") for u in range(2)]
        u_stored = [mem.sem(f"mo_u_stored{u}") for u in range(2)]

        def steps(engine, body):
            for s in range(4):
                body(s, s % 2, s // 2, True, s >= 2, True)
            with engine.Fori(0, NT // 2 - 2) as j:
                for u in range(2):
                    body(2 * j + 4 + u, u, j + 2, True, True, False)
            for s in range(NT, NT + 2):
                body(s, s % 2, s // 2, False, True, False)

        with nc.Block() as block:
            @block.sync
            def _(sp):
                def load_w(k):
                    if k >= 2:
                        sp.wait_ge(w_lo_ready, k - 1)
                    sp.dma_start(w_raw[:, k % 2], io.w_o[0, k * P:(k + 1) * P, :]).then_inc(w_loaded[k % 2], 16)

                def load_y(t, u):
                    sp.dma_start(y[:, u], scr.yT[:, :, ds(t * P, P)].rearrange("f p t -> p f t")).then_inc(y_loaded[u], 16)

                def load_x(t, u):
                    sp.dma_start(xres[:, u], flat(io.x[:, ds(t * P, P), :])).then_inc(x_loaded[u], 16)

                load_w(0)
                load_w(1)
                sp.dma_start(g_sub[:, 0:1], io.g_da_sub).then_inc(const_loaded, 16)
                sp.dma_start(ident[:, :], io.ident).then_inc(const_loaded, 16)
                sp.dma_start(g_post[:, :], io.g_attn_post.broadcast_to([P, D])).then_inc(const_loaded, 16)
                for t in range(2):
                    load_y(t, t)
                for k in range(2, KD):
                    load_w(k)
                for t in range(2):
                    load_x(t, t)

                def body(s, u, nth, prep, post, first):
                    if not post:
                        return
                    if prep:
                        hold(sp, y_lo_ready, s - 1)
                        load_y(s, u)
                    cols = ds((s - 2) * P, P)
                    hold(sp, h_ready, s - 1)
                    sp.dma_start(scr.h[cols, :], h[:, u]).then_inc(h_stored[u], 16)
                    if prep:
                        load_x(s, u)
                    hold(sp, u_lo_ready, s - 1)
                    for src, dst in ((u_hi, scr.u_hi), (u_lo, scr.u_lo)):
                        sp.dma_start(dst[:, :, cols], f32(src[:, u])).then_inc(u_stored[u], 16)

                steps(sp, body)
                for u in range(2):
                    sp.wait_ge(h_stored[u], 16 * NT // 2)
                    sp.wait_ge(u_stored[u], 32 * NT // 2)

            @block.gpsimd
            def _(pool):
                pool.memset(ones[:, :], 1.0 / DA_V).then_inc(const_set, 1)
                pool.memset(eps[:, :], EPS).then_inc(const_set, 1)
                pool.wait_ge(const_loaded, 48)
                pool.tensor_scalar(g_sub[:, 1:2], g_sub[:, 0:1], 1.0 - LAMBDA_INIT, 1.0, ALU.mult, ALU.mult).then_inc(const_set, 1)
                pool.wait_ge(const_set, 3)
                for k in range(DA_H):
                    pool.wait_ge(w_loaded[k % 2], 16 * (k // 2) + 16)
                    pool.tensor_scalar(w_raw[:, k % 2], w_raw[:, k % 2], g_sub[:, 1:2], 1.0, ALU.mult, ALU.mult).then_inc(w_gained, 1)

                def body(s, u, nth, prep, post, first):
                    if not post:
                        return
                    if not first:
                        pool.wait_ge(hT_ready, s - 3)
                    pool.wait_ge(stat_step, 6 * (s - 1))
                    pool.nop(nofuse=True)
                    pool.tensor_scalar(hn[:, u], h[:, u], stat[:, u, 5:6], 1.0, ALU.mult, ALU.mult).then_inc(hn_ready, 1)

                steps(pool, body)

            @block.scalar
            def _(act):
                act.preload_act_table_set("natural_log_exp_and_others")
                act.wait_ge(const_set, 3)
                for k in range(KD):
                    if k < DA_H:
                        act.wait_ge(w_gained, k + 1)
                    else:
                        act.wait_ge(w_loaded[k % 2], 16 * (k // 2) + 16)
                    act.activation(w_hi[:, k], w_raw[:, k % 2], ACT.Copy).then_inc(w_hi_ready, 1)

                def rstd(src, s, u, at):
                    n = 6 * (s - 2) + at
                    act.activation(junk[:, :], src, ACT.Square, accum_out=stat[:, u, at:at + 1]).then_inc(stat_step, 1)
                    act.wait_ge(stat_step, n + 1)
                    act.activation(stat[:, u, at + 1:at + 2], stat[:, u, at:at + 1], ACT.Ln, bias=eps[:, :], scale=1.0 / D).then_inc(stat_step, 1)
                    act.wait_ge(stat_step, n + 2)
                    act.activation(stat[:, u, at + 2:at + 3], stat[:, u, at + 1:at + 2], ACT.Exp, scale=-0.5).then_inc(stat_step, 1)

                def body(s, u, nth, prep, post, first):
                    if post:
                        act.wait_ge(mix_ready, s - 1)
                        rstd(ps_m[u][:, :], s, u, 0)
                    if prep:
                        act.wait_ge(y_loaded[u], 16 * nth + 16)
                        act.activation(sq[:, :].rearrange("p (f t) -> p f t", f=DA_H), y[:, u, 0:DA_H], ACT.Square).then_inc(sq_ready, 1)
                    if post:
                        act.wait_ge(h_ready, s - 1)
                        rstd(h[:, u], s, u, 3)
                    if prep:
                        act.wait_ge(mean_ready, s + 1)
                        act.activation(y_rstd[:, :], ps_r[:, :], ACT.Ln, bias=eps[:, :]).then_inc(y_log_ready, 1)
                        act.wait_ge(y_log_ready, s + 1)
                        act.activation(y_rstd[:, :], y_rstd[:, :], ACT.Exp, scale=-0.5).then_inc(y_rstd_ready, 1)
                        act.wait_ge(y_normed, s + 1)
                        act.activation(y_hi[:, u], y[:, u], ACT.Copy).then_inc(y_hi_ready, 1)
                    if post:
                        act.wait_ge(hT_ready, s - 1)
                        if not first:
                            act.wait_ge(u_stored[u], 32 * (nth - 1))
                        act.activation(u_hi[:, u], ps_t[:, :].rearrange("p (k t) -> p k t", k=KD), ACT.Copy).then_inc(u_hi_ready, 1)

                steps(act, body)

            @block.vector
            def _(dve):
                for k in range(KD):
                    dve.wait_ge(w_hi_ready, k + 1)
                    dve.tensor_tensor(w_lo[:, k], w_raw[:, k % 2], f32(w_hi[:, k]), ALU.subtract).then_inc(w_lo_ready, 1)

                def body(s, u, nth, prep, post, first):
                    if post:
                        if not first:
                            dve.wait_ge(h_stored[u], 16 * (nth - 1))
                            dve.wait_ge(hn_ready, s - 3)
                        dve.wait_ge(stat_step, 6 * (s - 2) + 3)
                        dve.scalar_tensor_tensor(out=h[:, u], in0=ps_m[u][:, :], scalar=stat[:, u, 2:3], in1=g_post[:, :],
                                                 op0=ALU.mult, op1=ALU.mult).then_inc(post_ready, 1)
                        dve.wait_ge(x_loaded[u], 16 * nth)
                        dve.wait_ge(post_ready, s - 1)
                        dve.tensor_tensor(h[:, u], h[:, u], xres[:, u], ALU.add).then_inc(h_ready, 1)
                    if prep:
                        dve.wait_ge(y_rstd_ready, s + 1)
                        dve.tensor_tensor(y[:, u, 0:DA_H], y[:, u, 0:DA_H], y_rstd[:, :].rearrange("p (f t) -> p f t", f=DA_H),
                                          ALU.mult).then_inc(y_normed, 1)
                        dve.wait_ge(y_hi_ready, s + 1)
                        dve.tensor_tensor(y_lo[:, u], y[:, u], f32(y_hi[:, u]), ALU.subtract).then_inc(y_lo_ready, 1)
                    if post:
                        dve.wait_ge(u_hi_ready, s - 1)
                        dve.tensor_tensor(u_lo[:, u], ps_t[:, :].rearrange("p (k t) -> p k t", k=KD), f32(u_hi[:, u]),
                                          ALU.subtract).then_inc(u_lo_ready, 1)

                dve.wait_ge(const_loaded, 48)
                steps(dve, body)

            @block.tensor
            def _(pe):
                pe.wait_ge(const_set, 3)
                pe.wait_ge(const_loaded, 48)

                def product(s, u, half):
                    cols = slice(512 * half, 512 * half + 512)
                    for k in range(KD):
                        for i, (a, w) in enumerate(((y_hi, w_hi), (y_hi, w_lo), (y_lo, w_hi))):
                            m = pe.matmul(ps_m[1 - u][:, cols], a[:, 1 - u, k], w[:, k, cols],
                                          start=k == 0 and i == 0, stop=k == KD - 1 and i == 2)
                    return m

                def body(s, u, nth, prep, post, first):
                    has_product = not isinstance(s, int) or 1 <= s <= NT
                    if has_product:
                        if isinstance(s, int) and s == 1:
                            pe.wait_ge(w_lo_ready, KD)
                        pe.wait_ge(y_lo_ready, s)
                        if not isinstance(s, int) or s >= 3:
                            pe.wait_ge(post_ready, s - 2)
                        product(s, u, 0)
                    if prep:
                        pe.wait_ge(sq_ready, s + 1)
                        pe.matmul(ps_r[:, :], ones[:, :], sq[:, :], start=True, stop=True).then_inc(mean_ready, 1)
                    if has_product:
                        product(s, u, 1).then_inc(mix_ready, 1)
                    if post:
                        pe.wait_ge(hn_ready, s - 1)
                        if not (isinstance(s, int) and s == 2):
                            pe.wait_ge(u_lo_ready, s - 2)
                        for k in range(KD):
                            m = pe.transpose(ps_t[:, k * P:(k + 1) * P], hn[:, u, k * P:(k + 1) * P], ident[:, :])
                        m.then_inc(hT_ready, 1)

                steps(pe, body)


def mlp(nc, io, scr):
    GT = 1024
    NGR = SEQ // GT
    TG = GT // P
    NM = DFF // P
    NC = NM // 2
    with ExitStack() as ctx:
        mem = Memory(nc, ctx)
        u_hi = mem.sb("ff_u_hi", [P, KD, GT], F32R)
        u_lo = mem.sb("ff_u_lo", [P, KD, GT], F32R)
        hid_hi = mem.sb("ff_hid_hi", [P, 4, GT], F32R)
        hid_lo = mem.sb("ff_hid_lo", [P, 4, GT], F32R)
        acc = mem.sb("ff_acc", [P, TG, D])
        w1_raw = mem.sb("ff_w1_raw", [P, KD, P])
        w1_hi = mem.sb("ff_w1_hi", [P, 2, KD, P], F32R)
        w1_lo = mem.sb("ff_w1_lo", [P, 2, KD, P], F32R)
        w2_raw = mem.sb("ff_w2_raw", [P, D])
        w2_hi = mem.sb("ff_w2_hi", [P, 4, D], F32R)
        w2_lo = mem.sb("ff_w2_lo", [P, 4, D], F32R)
        relu = mem.sb("ff_relu", [P, GT])
        square = mem.sb("ff_square", [P, GT])
        g_post = mem.sb("ff_g_post", [P, D])
        h_in = mem.sb("ff_h_in", [P, 2, D])
        g_pre = mem.sb("ff_g_pre", [P, KD])
        eps = mem.sb("ff_eps", [P, 1])
        stat = mem.sb("ff_stat", [P, 3])
        ps1 = [mem.ps(f"ff_ps1_{i}", GT) for i in range(2)]
        ps2 = [mem.ps(f"ff_ps2_{i}", D) for i in range(2)]
        const_loaded, eps_set = mem.sem("ff_const_loaded"), mem.sem("ff_eps_set")
        u_loaded = [mem.sem(f"ff_u_loaded{k}") for k in range(KD)]
        w1_loaded, w1_gained, w1_hi_ready, w1_lo_ready = (mem.sem(f"ff_w1_{s}") for s in ("loaded", "gained", "hi_ready", "lo_ready"))
        w2_loaded, w2_hi_ready, w2_lo_ready = (mem.sem(f"ff_w2_{s}") for s in ("loaded", "hi_ready", "lo_ready"))
        pre_ready, relu_ready, square_ready = (mem.sem(f"ff_{s}_ready") for s in ("pre", "relu", "square"))
        hid_hi_ready, hid_lo_ready = mem.sem("ff_hid_hi_ready"), mem.sem("ff_hid_lo_ready")
        part_ready, part_added = mem.sem("ff_part_ready"), mem.sem("ff_part_added")
        stat_step = mem.sem("ff_stat_step")
        post_ready, out_ready = mem.sem("ff_post_ready"), mem.sem("ff_out_ready")
        h_loaded = [mem.sem(f"ff_h_loaded{u}") for u in range(2)]
        out_stored = [mem.sem(f"ff_out_stored{t}") for t in range(TG)]
        w1_v = io.w_ff1.rearrange("a (k p) n -> p (a k) n", p=P)

        def chunk_steps(engine, body, peeled=2):
            body(0, 0)
            body(1, 1)
            end = NC if peeled == 2 else NC - 2
            with engine.Fori(0, (end - 2) // 2) as j:
                body(2 * j + 2, 0)
                body(2 * j + 3, 1)
            for c in range(end, NC):
                body(c, c % 2)

        with nc.Block() as block:
            @block.sync
            def _(sp):
                def load_w1(G, m):
                    static = isinstance(m, int)
                    if not (static and NM * G + m == 0):
                        hold(sp, w1_lo_ready, NM * G + m)
                    col = (m % NM) * P if static else m * P
                    sp.dma_start(w1_raw[:, :, :], w1_v[:, :, ds(col, P)]).then_inc(w1_loaded, 16)

                def load_w2(G, m):
                    if not (isinstance(m, int) and NM * G + m == 0):
                        hold(sp, w2_lo_ready, NM * G + m)
                    sp.dma_start(w2_raw[:, :], flat(io.w_ff2[:, ds(m * P, P), :])).then_inc(w2_loaded, 16)

                def load_u(G):
                    for k in range(KD):
                        for src, dst in ((scr.u_hi, u_hi), (scr.u_lo, u_lo)):
                            sp.dma_start(f32(dst[:, k]), src[:, k, G * GT:(G + 1) * GT]).then_inc(u_loaded[k], 16)

                def load_h(n):
                    sp.dma_start(h_in[:, n % 2], scr.h[n * P:(n + 1) * P, :]).then_inc(h_loaded[n % 2], 16)

                sp.dma_start(g_pre[:, :], io.g_mlp_pre).then_inc(const_loaded, 16)
                load_w1(0, 0)
                load_u(0)
                sp.dma_start(g_post[:, :], io.g_mlp_post.broadcast_to([P, D])).then_inc(const_loaded, 16)
                load_w1(0, 1)
                load_h(0)
                for G in range(NGR):
                    load_w2(G, 0)
                    load_w1(G, 2)
                    with sp.Fori(1, NM - 2) as m:
                        load_w2(G, m)
                        load_w1(G, m + 2)
                    for m in range(NM - 2, NM):
                        load_w2(G, m)
                        if G < NGR - 1:
                            load_w1(G, m + 2)
                    if G < NGR - 1:
                        sp.wait_ge(pre_ready, NM * (G + 1))
                        load_u(G + 1)
                    for t in range(TG):
                        n = TG * G + t
                        if n + 1 < TG * NGR:
                            if n:
                                sp.wait_ge(out_ready, n)
                            load_h(n + 1)
                        sp.wait_ge(out_ready, n + 1)
                        sp.dma_start(io.out[0, n * P:(n + 1) * P, :], acc[:, t]).then_inc(out_stored[t], 16)
                for t in range(TG):
                    sp.wait_ge(out_stored[t], 16 * NGR)

            @block.gpsimd
            def _(pool):
                def gain(n):
                    pool.wait_ge(w1_loaded, 16 * n + 16)
                    pool.tensor_tensor(w1_raw[:, :, :], w1_raw[:, :, :], g_pre[:, :].unsqueeze(2).broadcast_to([P, KD, P]),
                                       ALU.mult).then_inc(w1_gained, 1)

                pool.memset(eps[:, :], EPS).then_inc(eps_set, 1)
                pool.wait_ge(const_loaded, 32)
                gain(0)
                gain(1)
                for G in range(NGR):
                    def body(c, u):
                        for e in range(2):
                            n = NM * G + 2 * c + e
                            if not (isinstance(n, int) and n == 0):
                                pool.wait_ge(hid_lo_ready, n)
                            pool.wait_ge(relu_ready, n + 1)
                            pool.tensor_tensor(square[:, :], relu[:, :], relu[:, :], ALU.mult).then_inc(square_ready, 1)
                            if not (isinstance(n, int) and n + 2 >= NM * NGR):
                                gain(n + 2)

                    chunk_steps(pool, body, 4)

            @block.scalar
            def _(act):
                def split_w1(n, slot):
                    act.wait_ge(w1_gained, n + 1)
                    if not (isinstance(n, int) and n < 2):
                        act.wait_ge(pre_ready, n - 1)
                    act.activation(w1_hi[:, slot], w1_raw[:, :, :], ACT.Copy).then_inc(w1_hi_ready, 1)

                act.preload_act_table_set("natural_log_exp_and_others")
                split_w1(0, 0)
                split_w1(1, 1)
                act.wait_ge(eps_set, 1)
                for G in range(NGR):
                    def body(c, u):
                        for e in range(2):
                            n = NM * G + 2 * c + e
                            act.wait_ge(w2_loaded, 16 * n + 16)
                            if not (isinstance(n, int) and n < 4):
                                act.wait_ge(part_ready, TG * (NC * G + c - 1))
                            act.activation(w2_hi[:, 2 * u + e], w2_raw[:, :], ACT.Copy).then_inc(w2_hi_ready, 1)
                            act.wait_ge(pre_ready, n + 1)
                            if not (isinstance(n, int) and n == 0):
                                act.wait_ge(square_ready, n)
                                act.wait_ge(hid_hi_ready, n)
                            act.activation(relu[:, :], ps1[e][:, :], ACT.Relu).then_inc(relu_ready, 1)
                            act.wait_ge(relu_ready, n + 1)
                            act.activation(hid_hi[:, 2 * u + e], relu[:, :], ACT.Square).then_inc(hid_hi_ready, 1)
                            if not (isinstance(n, int) and n + 2 >= NM * NGR):
                                split_w1(n + 2, e)

                    chunk_steps(act, body, 4)
                    for t in range(TG):
                        n = TG * G + t
                        act.wait_ge(part_added, TG * NC * (G + 1) - TG + t + 1)
                        if n:
                            act.wait_ge(post_ready, n)
                        act.activation(relu[:, :], acc[:, t], ACT.Square, accum_out=stat[:, 0:1]).then_inc(stat_step, 1)
                        act.wait_ge(stat_step, 3 * n + 1)
                        act.activation(stat[:, 1:2], stat[:, 0:1], ACT.Ln, bias=eps[:, :], scale=1.0 / D).then_inc(stat_step, 1)
                        act.wait_ge(stat_step, 3 * n + 2)
                        act.activation(stat[:, 2:3], stat[:, 1:2], ACT.Exp, scale=-0.5).then_inc(stat_step, 1)

            @block.vector
            def _(dve):
                def split_w1(n, slot):
                    dve.wait_ge(w1_hi_ready, n + 1)
                    dve.tensor_tensor(w1_lo[:, slot], w1_raw[:, :, :], f32(w1_hi[:, slot]), ALU.subtract).then_inc(w1_lo_ready, 1)

                def add(G, c, t):
                    dve.wait_ge(part_ready, TG * (NC * G + c) + t + 1)
                    if isinstance(c, int) and c == 0:
                        if G:
                            dve.wait_ge(out_stored[t], 16 * G)
                        dve.tensor_copy(acc[:, t], ps2[t % 2][:, :]).then_inc(part_added, 1)
                    else:
                        dve.wait_ge(part_added, TG * (NC * G + c - 1) + t + 1)
                        dve.tensor_tensor(acc[:, t], acc[:, t], ps2[t % 2][:, :], ALU.add).then_inc(part_added, 1)

                split_w1(0, 0)
                split_w1(1, 1)
                dve.wait_ge(const_loaded, 32)
                for G in range(NGR):
                    def body(c, u):
                        for e in range(2):
                            n = NM * G + 2 * c + e
                            dve.wait_ge(w2_hi_ready, n + 1)
                            dve.tensor_tensor(w2_lo[:, 2 * u + e], w2_raw[:, :], f32(w2_hi[:, 2 * u + e]), ALU.subtract).then_inc(w2_lo_ready, 1)
                            adds = [] if isinstance(c, int) and c == 0 else list(range(TG // 2 * e, TG // 2 * (e + 1)))
                            for t in adds[:1]:
                                add(G, c - 1, t)
                            dve.wait_ge(hid_hi_ready, n + 1)
                            dve.wait_ge(square_ready, n + 1)
                            dve.tensor_tensor(hid_lo[:, 2 * u + e], square[:, :], f32(hid_hi[:, 2 * u + e]),
                                              ALU.subtract).then_inc(hid_lo_ready, 1)
                            for t in adds[1:3]:
                                add(G, c - 1, t)
                            if not (isinstance(n, int) and n + 2 >= NM * NGR):
                                split_w1(n + 2, e)
                            for t in adds[3:]:
                                add(G, c - 1, t)

                    chunk_steps(dve, body, 4)
                    add(G, NC - 1, 0)
                    for t in range(TG):
                        if t + 1 < TG:
                            add(G, NC - 1, t + 1)
                        n = TG * G + t
                        dve.wait_ge(stat_step, 3 * n + 3)
                        dve.scalar_tensor_tensor(out=acc[:, t], in0=acc[:, t], scalar=stat[:, 2:3], in1=g_post[:, :],
                                                 op0=ALU.mult, op1=ALU.mult).then_inc(post_ready, 1)
                        dve.wait_ge(h_loaded[n % 2], 16 * (n // 2) + 16)
                        dve.wait_ge(post_ready, n + 1)
                        dve.tensor_tensor(acc[:, t], acc[:, t], h_in[:, n % 2], ALU.add).then_inc(out_ready, 1)

            @block.tensor
            def _(pe):
                def hidden(G, c, e):
                    n = NM * G + 2 * c + e
                    pe.wait_ge(w1_lo_ready, n + 1)
                    if not (isinstance(n, int) and n < 2):
                        pe.wait_ge(relu_ready, n - 1)
                    for half in range(2):
                        cols = slice(512 * half, 512 * half + 512)
                        for k in range(KD):
                            if isinstance(c, int) and c == e == half == 0:
                                pe.wait_ge(u_loaded[k], 32 * (G + 1))
                            for i, (w, a) in enumerate(((w1_hi, u_hi), (w1_hi, u_lo), (w1_lo, u_hi))):
                                m = pe.matmul(ps1[e][:, cols], w[:, e, k], a[:, k, cols],
                                              start=k == 0 and i == 0, stop=k == KD - 1 and i == 2)
                    m.then_inc(pre_ready, 1)

                def part(G, c, u, t):
                    n = TG * (NC * G + c) + t
                    if not (isinstance(n, int) and n < 2):
                        pe.wait_ge(part_added, n - 1)
                    if t == 0:
                        pe.wait_ge(w2_lo_ready, NM * G + 2 * c + 2)
                        pe.wait_ge(hid_lo_ready, NM * G + 2 * c + 2)
                    for half in range(2):
                        cols = slice(512 * half, 512 * half + 512)
                        for e in range(2):
                            for i, (a, w) in enumerate(((hid_hi, w2_hi), (hid_hi, w2_lo), (hid_lo, w2_hi))):
                                m = pe.matmul(ps2[t % 2][:, cols], a[:, 2 * u + e, t * P:(t + 1) * P], w[:, 2 * u + e, cols],
                                              start=e == 0 and i == 0, stop=e == 1 and i == 2)
                    m.then_inc(part_ready, 1)

                for G in range(NGR):
                    def body(c, u):
                        last = isinstance(c, int) and c == NC - 1
                        for e in range(2):
                            hidden(G, c, e)
                            if last and e == 0:
                                continue
                            if not (isinstance(c, int) and c == 0):
                                for t in range(0 if last else TG // 2 * e, TG // 2 * (e + 1)):
                                    part(G, c - 1, 1 - u, t)

                    chunk_steps(pe, body, 4)
                    for t in range(TG):
                        part(G, NC - 1, 1, t)


class Arrays:
    pass


SCRATCH = {
    "qk_hi": (8, P, L), "qk_lo": (8, P, L),
    "c_hi": (P, 4, L), "c_lo": (P, 4, L),
    "v": (L, DA_W), "mv": (L, MLA_H * MLA_V),
    "mq_hi": (MLA_H, P, SEQ), "mq_lo": (MLA_H, P, SEQ),
    "mqr_hi": (2, P, SEQ), "mqr_lo": (2, P, SEQ),
    "mk_hi": (MLA_H, P, L), "mk_lo": (MLA_H, P, L),
    "yT": (8, P, SEQ),
    "u_hi": (P, KD, SEQ), "u_lo": (P, KD, SEQ),
    "h": (SEQ, D),
}


def build(nc, ins, out, stages=7, scratch_aps=None):
    io, scr = Arrays(), Arrays()
    (io.x, io.meta, io.g_attn_pre, io.w_in, io.lam_q1, io.lam_k1, io.lam_q2, io.lam_k2, io.g_da_sub, io.g_mla_q,
     io.w_q_up, io.g_mla_kv, io.w_kv_up, io.w_o, io.g_attn_post, io.g_mlp_pre, io.w_ff1, io.w_ff2, io.g_mlp_post,
     io.ident, io.trig_tm, io.trig_fm, io.bias) = ins
    io.out = out
    a = scratch_aps or {n: nc.dram_tensor(f"scr_{n}", s, F32).ap() for n, s in SCRATCH.items()}
    (scr.qk_hi, scr.qk_lo, scr.c_hi, scr.c_lo, scr.v, scr.mv, scr.mq_hi, scr.mq_lo, scr.mqr_hi, scr.mqr_lo, scr.mk_hi, scr.mk_lo,
     scr.yT, scr.u_hi, scr.u_lo, scr.h) = (a[n] for n in SCRATCH)
    if stages & 1:
        with ExitStack() as ctx:
            mem = Memory(nc, ctx)
            u_hi = mem.sb("u_hi", [P, KD, L], F32R)
            u_lo = mem.sb("u_lo", [P, KD, L], F32R)
            ident = mem.sb("ident", [P, P])
            g_col = mem.sb("g_col", [P, KD])
            eps = mem.sb("eps", [P, 1])
            norm_in(nc, io, u_hi, u_lo, ident, g_col, eps)
            qk_proj(nc, io, scr, u_hi, u_lo, g_col)
            cv_proj(nc, io, scr, u_hi, u_lo, g_col, ident, eps)
    if stages & 2:
        mla_up(nc, io, scr)
    if stages & 4:
        attention(nc, io, scr, io.ident, True)
    if stages & 8:
        attention(nc, io, scr, io.ident, False)
    if stages & 16:
        mix_out(nc, io, scr)
    if stages & 32:
        mlp(nc, io, scr)


def constants():
    inv_freq = (1.0 / (np.float32(10000.0) ** (np.arange(0, ROPE, 2, dtype=np.float32) / np.float32(ROPE)))).astype(np.float32)
    ang = np.arange(L, dtype=np.float32)[:, None] * inv_freq[None, :]
    cos, sin = np.cos(ang).astype(np.float32), np.sin(ang).astype(np.float32)
    trig_tm = np.stack([np.concatenate([cos, cos], 1), np.concatenate([-sin, sin], 1)], 1)
    trig_fm = np.ascontiguousarray(np.tile(trig_tm[META:].transpose(2, 1, 0), (2, 1, 1)))
    p, c = np.arange(P)[:, None], np.arange(L)[None, :]
    dist = np.abs(META + p + (NT - 1) * P - c).astype(np.float32)
    seen = (p >= CHUNK) | (c < (NT - 1) * P + META + CHUNK)
    bias = np.zeros((DA_H + 1, P, L), np.float32)
    for h in range(DA_H):
        slope = np.float32(2.0 ** (-8.0 * (h + 1) / DA_H))
        bias[h] = np.where(seen, -slope * dist / np.float32(DA_SCALE), np.float32(NEG))
    bias[DA_H] = np.where(seen, 0.0, NEG)
    return {"ident": np.eye(P, dtype=np.float32), "trig_tm": np.ascontiguousarray(trig_tm), "trig_fm": trig_fm, "bias": bias}


INPUTS = ["x", "meta_tokens", "g_attn_pre", "w_in", "da_lambda_q1", "da_lambda_k1", "da_lambda_q2", "da_lambda_k2", "g_da_sub",
          "g_mla_q", "w_mla_q_up", "g_mla_kv", "w_mla_kv_up", "w_o", "g_attn_post", "g_mlp_pre", "w_ff1", "w_ff2", "g_mlp_post"]


COLUMNS = ("g_attn_pre", "g_da_sub", "g_mla_q", "g_mla_kv", "g_mlp_pre")


def laid_out(inputs):
    arrays = {n: np.ascontiguousarray(inputs[n]) for n in INPUTS}
    for n in COLUMNS:
        arrays[n] = np.ascontiguousarray(arrays[n].reshape(-1, P).T)
    arrays.update(constants())
    return arrays


def kernel(**inputs):
    import concourse.bacc as bacc
    from concourse.bass_utils import run_bass_kernel_spmd

    nc = bacc.Bacc("TRN2", target_bir_lowering=False, num_devices=1)
    arrays = laid_out(inputs)
    ins = [nc.dram_tensor(f"in_{n}", a.shape, mybir.dt.from_np(a.dtype), kind="ExternalInput").ap() for n, a in arrays.items()]
    out = nc.dram_tensor("out", (1, SEQ, D), F32, kind="ExternalOutput").ap()
    build(nc, ins, out, 63)
    r = run_bass_kernel_spmd(nc, [{f"in_{n}": a for n, a in arrays.items()}], core_ids=[0])
    return r.results[0]["out"]
```

```python
import math
from contextlib import ExitStack

import numpy as np
import concourse.bass as bass
from concourse import mybir

F32 = mybir.dt.float32
F32R = mybir.dt.float32r
ALU = mybir.AluOpType
ACT = mybir.ActivationFunctionType
AX = mybir.AxisListType

P = 128
D = 1024
SEQ = 2048
META = 16
L = SEQ + META
CHUNK = 64
NT = SEQ // P
KD = D // P
EPS = 1e-6
NEG = -1e30
LOWEST = -3.0e38
DA_H, DA_HD, DA_V = 4, 64, 128
MLA_H, NOPE, ROPE, MLA_V = 4, 128, 64, 128
QR, KVR = 256, 128
DFF = 4096
DA_W = DA_H * DA_V
C_Q, C_KV, C_R = 3 * DA_W, 3 * DA_W + QR, 3 * DA_W + QR + KVR
IN_W = C_R + ROPE
LAMBDA_INIT = 0.8 - 0.6 * math.exp(-0.0)
DA_SCALE = DA_HD ** -0.5
MLA_SCALE = (NOPE + ROPE) ** -0.5
TOK_CHUNKS = [(0, META)] + [(META + 512 * i, 512) for i in range(SEQ // 512)]
EVEN_CHUNKS = [(c, min(416, L - c)) for c in range(0, L, 416)]
TILES = [(0, META)] + [(META + P * i, P) for i in range(NT)]
ds = bass.ds


def f32(ap):
    return ap.bitcast(F32)


def hold(engine, sem, value):
    engine.wait_ge(sem, value)
    engine.nop(nofuse=True)


def flat(ap):
    return ap.rearrange("a p n -> p (a n)")


class Memory:

    def __init__(self, nc, ctx):
        self.nc, self.ctx, self.sems = nc, ctx, []
        ctx.callback(self.clear)

    def clear(self):
        if self.sems:
            self.nc.clear_and_free_semaphores(self.sems)
            self.nc.all_engine_barrier()

    def sb(self, name, shape, dt=F32):
        return self.ctx.enter_context(self.nc.sbuf_tensor(name, shape, dt))

    def ps(self, name, cols=512):
        return self.ctx.enter_context(self.nc.psum_tensor(name, [P, cols], F32))

    def sem(self, name):
        self.sems.append(self.nc.alloc_semaphore(name))
        return self.sems[-1]


def w_in_rows(io):
    return io.w_in.rearrange("a (k p) n -> p (a k) n", p=P)


def norm_in(nc, io, u_hi, u_lo, ident, g_col, eps, w_first):
    with ExitStack() as ctx:
        mem = Memory(nc, ctx)
        NX = 4
        xt = mem.sb("ni_xt", [P, NX, D])
        xn = mem.sb("ni_xn", [P, 2, D])
        junk = mem.sb("ni_junk", [P, D])
        ssq = mem.sb("ni_ssq", [P, NX])
        std = mem.sb("ni_std", [P, NX])
        rstd = mem.sb("ni_rstd", [P, NX])
        pt = [mem.ps(f"ni_pt{i}", D) for i in range(2)]
        const_loaded, eps_ready, w_loaded = (mem.sem(f"ni_{s}") for s in ("const_loaded", "eps_ready", "w_loaded"))
        x_loaded = [mem.sem(f"ni_x_loaded{v}") for v in range(NX)]
        ssq_ready, std_ready, rstd_ready = (mem.sem(f"ni_{s}_ready") for s in ("ssq", "std", "rstd"))
        xn_ready, xT_ready = mem.sem("ni_xn_ready"), mem.sem("ni_xT_ready")
        hi_ready, lo_ready = mem.sem("ni_hi_ready"), mem.sem("ni_lo_ready")

        def turned(u, rows):
            return pt[u][:, :].rearrange("p (k t) -> p k t", k=KD)[:, :, 0:rows]

        with nc.Block() as block:
            @block.sync
            def _(sp):
                sp.dma_start(xt[0:META, 0, :], io.meta).then_inc(x_loaded[0], 16)
                sp.dma_start(xt[:, 1, :], io.x[0, 0:P, :]).then_inc(x_loaded[1], 16)
                sp.dma_start(ident[:, :], io.ident).then_inc(const_loaded, 16)
                sp.dma_start(g_col[:, :], io.g_attn_pre).then_inc(const_loaded, 16)

                def load(n, v):
                    sp.wait_ge(xn_ready, n - NX + 1)
                    sp.dma_start(xt[:, v, :], flat(io.x[:, ds((n - 1) * P, P), :])).then_inc(x_loaded[v], 16)

                for v in range(2, NX):
                    sp.dma_start(xt[:, v, :], io.x[0, (v - 1) * P:v * P, :]).then_inc(x_loaded[v], 16)
                for u in range(2):
                    sp.dma_start(w_first[:, u], w_in_rows(io)[:, :, u * P:(u + 1) * P]).then_inc(w_loaded, 16)
                with sp.Fori(0, NT // NX - 1) as j:
                    for v in range(NX):
                        load(NX * j + NX + v, v)
                load(NT, 0)
                sp.wait_ge(const_loaded, 32)

            @block.gpsimd
            def _(pool):
                pool.memset(eps[:, :], EPS).then_inc(eps_ready, 1)
                pool.wait_ge(const_loaded, 32)
                pool.wait_ge(w_loaded, 32)
                for u in range(2):
                    pool.tensor_tensor(w_first[:, u], w_first[:, u], g_col[:, :].unsqueeze(2).broadcast_to([P, KD, P]), ALU.mult)

            @block.scalar
            def _(act):
                def stats(n, v, nth, rows):
                    act.wait_ge(x_loaded[v], 16 * nth + 16)
                    act.activation(junk[0:rows, :], xt[0:rows, v, :], ACT.Square,
                                   accum_out=ssq[0:rows, v:v + 1]).then_inc(ssq_ready, 1)

                def root(n, v, rows):
                    act.wait_ge(ssq_ready, n + 1)
                    act.activation(std[0:rows, v:v + 1], ssq[0:rows, v:v + 1], ACT.Sqrt,
                                   bias=eps[0:rows, :], scale=1.0 / D).then_inc(std_ready, 1)

                def high(n, u, rows, col):
                    act.wait_ge(xT_ready, n + 1)
                    act.activation(u_hi[:, :, ds(col, rows)], turned(u, rows), ACT.Copy).then_inc(hi_ready, 1)

                act.wait_ge(eps_ready, 1)
                def high_of(n):
                    high(n, n % 2, TILES[n][1], TILES[n][0])

                for n in range(NX):
                    stats(n, n, 0, TILES[n][1])
                    root(n, n, TILES[n][1])
                    if n >= 2:
                        high_of(n - 2)
                with act.Fori(0, NT // NX - 1) as j:
                    for v in range(NX):
                        n = NX * j + NX + v
                        stats(n, v, j + 1, P)
                        root(n, v, P)
                        high(n - 2, v % 2, P, META + (n - 3) * P)
                stats(NT, 0, NT // NX, P)
                root(NT, 0, P)
                for n in range(NT - 2, NT + 1):
                    high_of(n)

            @block.vector
            def _(dve):
                def scale(n, v, rows, first):
                    u = v % 2
                    dve.wait_ge(std_ready, n + 1)
                    dve.reciprocal(rstd[0:rows, v:v + 1], std[0:rows, v:v + 1]).then_inc(rstd_ready, 1)
                    if not first:
                        dve.wait_ge(xT_ready, n - 1)
                    dve.wait_ge(rstd_ready, n + 1)
                    dve.tensor_scalar(xn[0:rows, u, :], xt[0:rows, v, :], rstd[0:rows, v:v + 1], None,
                                      ALU.mult).then_inc(xn_ready, 1)

                def low(n, u, rows, col):
                    dve.wait_ge(hi_ready, n + 1)
                    dve.tensor_tensor(u_lo[:, :, ds(col, rows)], turned(u, rows), f32(u_hi[:, :, ds(col, rows)]),
                                      ALU.subtract).then_inc(lo_ready, 1)

                def low_of(n):
                    low(n, n % 2, TILES[n][1], TILES[n][0])

                for n in range(NX):
                    scale(n, n, TILES[n][1], n < 2)
                    if n >= 2:
                        low_of(n - 2)
                with dve.Fori(0, NT // NX - 1) as j:
                    for v in range(NX):
                        n = NX * j + NX + v
                        scale(n, v, P, False)
                        low(n - 2, v % 2, P, META + (n - 3) * P)
                scale(NT, 0, P, False)
                for n in range(NT - 2, NT + 1):
                    low_of(n)

            @block.tensor
            def _(pe):
                def turn(n, u, rows, first):
                    pe.wait_ge(xn_ready, n + 1)
                    if not first:
                        pe.wait_ge(lo_ready, n - 1)
                    for k in range(KD):
                        t = pe.transpose(pt[u][:, k * P:k * P + rows], xn[0:rows, u, k * P:(k + 1) * P],
                                         ident[0:rows, 0:rows])
                    t.then_inc(xT_ready, 1)

                pe.wait_ge(const_loaded, 32)
                turn(0, 0, META, True)
                turn(1, 1, P, True)
                with pe.Fori(0, NT // 2 - 1) as j:
                    turn(2 * j + 2, 0, P, False)
                    turn(2 * j + 3, 1, P, False)
                turn(NT, 0, P, False)


def qk_proj(nc, io, scr, u_hi, u_lo, g_col, w_raw, cv_w):
    NM, NQ = 2 * DA_W // P, len(EVEN_CHUNKS)
    with ExitStack() as ctx:
        mem = Memory(nc, ctx)
        w_hi = mem.sb("qk_w_hi", [P, 2, KD, P], F32R)
        w_lo = mem.sb("qk_w_lo", [P, 2, KD, P], F32R)
        o_hi = mem.sb("qk_o_hi", [P, L], F32R)
        o_lo = mem.sb("qk_o_lo", [P, L], F32R)
        ps = [mem.ps(f"qk_ps{q}") for q in range(NQ)]
        w_loaded = [mem.sem(f"qk_w_loaded{u}") for u in range(2)]
        w_gained, w_hi_ready, w_lo_ready = (mem.sem(f"qk_w_{s}") for s in ("gained", "hi_ready", "lo_ready"))
        sums_ready, hi_ready, lo_ready = (mem.sem(f"qk_{s}_ready") for s in ("sums", "hi", "lo"))
        stored = [mem.sem(f"qk_stored{q}") for q in range(NQ)]
        cv_loaded = mem.sem("qk_cv_loaded")
        w_v = w_in_rows(io)

        with nc.Block() as block:
            @block.sync
            def _(sp):
                def store(m):
                    for q, (c0, n) in enumerate(EVEN_CHUNKS):
                        sp.wait_ge(lo_ready, NQ * m + q + 1)
                        for src, dst in ((o_hi, scr.qk_hi), (o_lo, scr.qk_lo)):
                            sp.dma_start(flat(dst[ds(m, 1), :, c0:c0 + n]), f32(src[:, c0:c0 + n])).then_inc(stored[q], 16)

                for at, c0, n in CV_COLS[0]:
                    sp.dma_start(cv_w[:, :, at:at + n], w_v[:, :, c0:c0 + n]).then_inc(cv_loaded, 16)
                with sp.Fori(0, NM // 2 - 1) as j:
                    for u in range(2):
                        sp.wait_ge(w_lo_ready, 2 * j + u + 1)
                        sp.dma_start(w_raw[:, u], w_v[:, :, ds((2 * j + u + 2) * P, P)]).then_inc(w_loaded[u], 16)
                        store(2 * j + u)
                store(NM - 2)
                store(NM - 1)
                for q in range(NQ):
                    sp.wait_ge(stored[q], 32 * NM)

            @block.gpsimd
            def _(pool):
                with pool.Fori(0, NM // 2 - 1) as j:
                    for u in range(2):
                        pool.wait_ge(w_loaded[u], 16 * j + 16)
                        pool.tensor_tensor(w_raw[:, u], w_raw[:, u], g_col[:, :].unsqueeze(2).broadcast_to([P, KD, P]),
                                           ALU.mult).then_inc(w_gained, 1)
                pool.wait_ge(cv_loaded, 16 * len(CV_COLS[0]))
                pool.tensor_tensor(cv_w[:, :, :], cv_w[:, :, :], g_col[:, :].unsqueeze(2).broadcast_to([P, KD, CV_W]), ALU.mult)

            @block.scalar
            def _(act):
                def split(m, u, first):
                    if not first:
                        act.wait_ge(w_gained, m - 1)
                        act.wait_ge(sums_ready, NQ * (m - 1))
                    act.activation(w_hi[:, u], w_raw[:, u], ACT.Copy).then_inc(w_hi_ready, 1)

                def high(m, first):
                    for q, (c0, n) in enumerate(EVEN_CHUNKS):
                        act.wait_ge(sums_ready, NQ * m + q + 1)
                        if not first:
                            act.wait_ge(stored[q], 32 * m)
                        act.activation(o_hi[:, c0:c0 + n], ps[q][:, 0:n], ACT.Copy).then_inc(hi_ready, 1)

                split(0, 0, True)
                split(1, 1, True)
                high(0, True)
                split(2, 0, False)
                high(1, False)
                with act.Fori(0, NM // 2 - 2) as j:
                    split(2 * j + 3, 1, False)
                    high(2 * j + 2, False)
                    split(2 * j + 4, 0, False)
                    high(2 * j + 3, False)
                split(NM - 1, 1, False)
                high(NM - 2, False)
                high(NM - 1, False)

            @block.vector
            def _(dve):
                def split(m, u):
                    dve.wait_ge(w_hi_ready, m + 1)
                    dve.tensor_tensor(w_lo[:, u], w_raw[:, u], f32(w_hi[:, u]), ALU.subtract).then_inc(w_lo_ready, 1)

                def low(m):
                    for q, (c0, n) in enumerate(EVEN_CHUNKS):
                        dve.wait_ge(hi_ready, NQ * m + q + 1)
                        dve.tensor_tensor(o_lo[:, c0:c0 + n], ps[q][:, 0:n], f32(o_hi[:, c0:c0 + n]),
                                          ALU.subtract).then_inc(lo_ready, 1)

                split(0, 0)
                split(1, 1)
                low(0)
                split(2, 0)
                low(1)
                with dve.Fori(0, NM // 2 - 2) as j:
                    split(2 * j + 3, 1)
                    low(2 * j + 2)
                    split(2 * j + 4, 0)
                    low(2 * j + 3)
                split(NM - 1, 1)
                low(NM - 2)
                low(NM - 1)

            @block.tensor
            def _(pe):
                def product(m, u, first):
                    pe.wait_ge(w_lo_ready, m + 1)
                    for q, (c0, n) in enumerate(EVEN_CHUNKS):
                        if not first:
                            pe.wait_ge(lo_ready, NQ * (m - 1) + q + 1)
                        for k in range(KD):
                            for i, (w, a) in enumerate(((w_hi, u_hi), (w_hi, u_lo), (w_lo, u_hi))):
                                t = pe.matmul(ps[q][:, 0:n], w[:, u, k], a[:, k, c0:c0 + n],
                                              start=(k == 0 and i == 0), stop=(k == KD - 1 and i == 2))
                        t.then_inc(sums_ready, 1)

                product(0, 0, True)
                product(1, 1, False)
                with pe.Fori(0, NM // 2 - 1) as j:
                    product(2 * j + 2, 0, False)
                    product(2 * j + 3, 1, False)


CV_W = 512
CV_COLS = [[(0, C_Q, QR + KVR + ROPE), (QR + KVR + ROPE, C_R + ROPE // 2, ROPE // 2), (QR + KVR + ROPE + ROPE // 2, C_R, ROPE // 2)],
           [(0, 2 * DA_W, DA_W)]]


def cv_proj(nc, io, scr, u_hi, u_lo, ident, g_col, eps, cv_w):
    W = CV_W
    NP = 4
    with ExitStack() as ctx:
        mem = Memory(nc, ctx)
        w_hi = mem.sb("cv_w_hi", [P, KD, W], F32R)
        w_lo = mem.sb("cv_w_lo", [P, KD, W], F32R)
        trig = mem.sb("cv_trig", [P, 2, 2, ROPE])
        cn = mem.sb("cv_cn", [P, 2, W])
        tmp = mem.sb("cv_tmp", [P, 2, 2, ROPE])
        junk = mem.sb("cv_junk", [P, QR])
        ssq = mem.sb("cv_ssq", [P, 2, 2])
        std = mem.sb("cv_std", [P, 2, 2])
        rstd = mem.sb("cv_rstd", [P, 2, 2])
        o_hi = mem.sb("cv_o_hi", [P, 2, W], F32R)
        o_lo = mem.sb("cv_o_lo", [P, 2, W], F32R)
        v_out = mem.sb("cv_v_out", [P, 2, W])
        v_copied = mem.sem("cv_v_copied")
        v_stored = [mem.sem(f"cv_v_stored{u}") for u in range(2)]
        ps = [mem.ps(f"cv_ps{i}") for i in range(2)]
        pt = [mem.ps(f"cv_pt{i}") for i in range(2)]
        w_loaded, w_gained, w_hi_ready, w_lo_ready = (mem.sem(f"cv_w_{s}") for s in ("loaded", "gained", "hi_ready", "lo_ready"))
        trig_loaded = [mem.sem(f"cv_trig_loaded{u}") for u in range(2)]
        sums_ready, ssq_ready, root_ready, rstd_ready = (mem.sem(f"cv_{s}_ready") for s in ("sums", "ssq", "root", "rstd"))
        rot_ready, cn_ready, cT_ready = (mem.sem(f"cv_{s}_ready") for s in ("rot", "cn", "cT"))
        hi_ready, lo_ready = mem.sem("cv_hi_ready"), mem.sem("cv_lo_ready")
        stored = [mem.sem(f"cv_stored{u}") for u in range(2)]
        N = len(TILES)
        KP = KD // NP

        with nc.Block() as block:
            @block.sync
            def _(sp):
                def load_trig(n):
                    r0, rows = TILES[n]
                    if n >= 2:
                        sp.wait_ge(rot_ready, 2 * (n - 1))
                    sp.dma_start(trig[0:rows, n % 2], io.trig_tm[r0:r0 + rows]).then_inc(trig_loaded[n % 2], 16)

                load_trig(0)
                load_trig(1)
                sp.wait_ge(w_lo_ready, NP)
                for at, c0, n in CV_COLS[1]:
                    sp.dma_start(cv_w[:, :, at:at + n], w_in_rows(io)[:, :, c0:c0 + n]).then_inc(w_loaded, 16)
                for n, (r0, rows) in enumerate(TILES):
                    sp.wait_ge(lo_ready, n + 1)
                    for src, dst in ((o_hi, scr.c_hi), (o_lo, scr.c_lo)):
                        sp.dma_start(dst[:, :, r0:r0 + rows], f32(src[:, n % 2]).rearrange("p (f t) -> p f t", f=4)[:, :, 0:rows]).then_inc(stored[n % 2], 16)
                    if n + 2 < N:
                        load_trig(n + 2)
                for n, (r0, rows) in enumerate(TILES):
                    sp.wait_ge(v_copied, n + 1)
                    sp.dma_start(scr.v[r0:r0 + rows, :], v_out[0:rows, n % 2]).then_inc(v_stored[n % 2], 16)
                for u in range(2):
                    sp.wait_ge(stored[u], 32 * len(range(u, N, 2)))
                    sp.wait_ge(v_stored[u], 16 * len(range(u, N, 2)))

            @block.gpsimd
            def _(pool):
                pool.wait_ge(w_loaded, 16 * len(CV_COLS[1]))
                pool.tensor_tensor(cv_w[:, :, :], cv_w[:, :, :], g_col[:, :].unsqueeze(2).broadcast_to([P, KD, W]), ALU.mult).then_inc(w_gained, 1)

            @block.scalar
            def _(act):
                def split(g):
                    if g >= NP:
                        act.wait_ge(w_gained, 1)
                        act.wait_ge(sums_ready, N)
                    q = g % NP
                    act.activation(w_hi[:, q * KP:(q + 1) * KP], cv_w[:, q * KP:(q + 1) * KP], ACT.Copy).then_inc(w_hi_ready, 1)

                def stats(n):
                    rows = TILES[n][1]
                    act.wait_ge(sums_ready, n + 1)
                    act.activation(junk[0:rows, 0:QR], ps[n % 2][0:rows, 0:QR], ACT.Square,
                                   accum_out=ssq[0:rows, n % 2, 0:1]).then_inc(ssq_ready, 1)
                    act.wait_ge(ssq_ready, 2 * n + 1)
                    act.activation(junk[0:rows, 0:KVR], ps[n % 2][0:rows, QR:QR + KVR], ACT.Square,
                                   accum_out=ssq[0:rows, n % 2, 1:2]).then_inc(ssq_ready, 1)
                    act.wait_ge(ssq_ready, 2 * n + 2)
                    act.activation(std[0:rows, n % 2, 0:1], ssq[0:rows, n % 2, 0:1], ACT.Sqrt,
                                   bias=eps[0:rows, :], scale=1.0 / QR)
                    act.activation(std[0:rows, n % 2, 1:2], ssq[0:rows, n % 2, 1:2], ACT.Sqrt,
                                   bias=eps[0:rows, :], scale=1.0 / KVR).then_inc(root_ready, 1)

                def high(n):
                    rows = TILES[n][1]
                    act.wait_ge(cT_ready, n + 1)
                    if n >= 2:
                        act.wait_ge(stored[n % 2], 32 * (n // 2))
                    act.activation(o_hi[:, n % 2].rearrange("p (f t) -> p f t", f=4)[:, :, 0:rows],
                                   pt[n % 2][:, :].rearrange("p (f t) -> p f t", f=4)[:, :, 0:rows],
                                   ACT.Copy).then_inc(hi_ready, 1)

                for g in range(NP):
                    split(g)
                for n in range(N):
                    stats(n)
                    if n:
                        high(n - 1)
                high(N - 1)
                for g in range(NP, 2 * NP):
                    split(g)
                for n in range(N):
                    m, rows = N + n, TILES[n][1]
                    act.wait_ge(sums_ready, m + 1)
                    if n >= 2:
                        act.wait_ge(v_stored[n % 2], 16 * (n // 2))
                    act.activation(v_out[0:rows, n % 2], ps[m % 2][0:rows, :], ACT.Copy).then_inc(v_copied, 1)

            @block.vector
            def _(dve):
                def split(g):
                    q = g % NP
                    dve.wait_ge(w_hi_ready, g + 1)
                    dve.tensor_tensor(w_lo[:, q * KP:(q + 1) * KP], cv_w[:, q * KP:(q + 1) * KP], f32(w_hi[:, q * KP:(q + 1) * KP]),
                                      ALU.subtract).then_inc(w_lo_ready, 1)

                def normalise(n):
                    u, rows = n % 2, TILES[n][1]
                    kr, swapped = QR + KVR, QR + KVR + ROPE
                    dve.wait_ge(trig_loaded[u], 16 * (n // 2) + 16)
                    dve.wait_ge(ssq_ready, 2 * n + 2)
                    dve.tensor_tensor(tmp[0:rows, u, 0], ps[u][0:rows, kr:kr + ROPE], trig[0:rows, u, 0], ALU.mult).then_inc(rot_ready, 1)
                    dve.tensor_tensor(tmp[0:rows, u, 1], ps[u][0:rows, swapped:swapped + ROPE], trig[0:rows, u, 1],
                                      ALU.mult).then_inc(rot_ready, 1)
                    dve.wait_ge(root_ready, n + 1)
                    dve.reciprocal(rstd[0:rows, u], std[0:rows, u]).then_inc(rstd_ready, 1)
                    dve.wait_ge(rot_ready, 2 * n + 2)
                    if n >= 2:
                        dve.wait_ge(cT_ready, n - 1)
                    dve.tensor_tensor(cn[0:rows, u, kr:kr + ROPE], tmp[0:rows, u, 0], tmp[0:rows, u, 1], ALU.add)
                    dve.tensor_tensor(cn[0:rows, u, swapped:swapped + ROPE], tmp[0:rows, u, 0], tmp[0:rows, u, 1], ALU.add)
                    dve.wait_ge(rstd_ready, n + 1)
                    dve.tensor_scalar(cn[0:rows, u, 0:QR], ps[u][0:rows, 0:QR], rstd[0:rows, u, 0:1], None, ALU.mult)
                    dve.tensor_scalar(cn[0:rows, u, QR:kr], ps[u][0:rows, QR:kr], rstd[0:rows, u, 1:2], None,
                                      ALU.mult).then_inc(cn_ready, 1)

                def low(m, bank):
                    rows = TILES[m][1]
                    o, h, s = (a.rearrange("p (f t) -> p f t", f=4)[:, :, 0:rows]
                               for a in (o_lo[:, m % 2], f32(o_hi[:, m % 2]), bank[:, :]))
                    dve.wait_ge(hi_ready, m + 1)
                    dve.tensor_tensor(o, s, h, ALU.subtract).then_inc(lo_ready, 1)

                for g in range(NP):
                    split(g)
                for n in range(N):
                    normalise(n)
                    if n:
                        low(n - 1, pt[(n - 1) % 2])
                low(N - 1, pt[(N - 1) % 2])
                for g in range(NP, 2 * NP):
                    split(g)

            @block.tensor
            def _(pe):
                def product(m):
                    c0, rows = TILES[m % N]
                    if m >= N + 2:
                        pe.wait_ge(v_copied, m - 1 - N)
                    elif m >= 2:
                        pe.wait_ge(cn_ready, m - 1)
                    for k in range(KD):
                        if m % N == 0 and k % KP == 0:
                            pe.wait_ge(w_lo_ready, NP * (m // N) + k // KP + 1)
                        for i, (a, w) in enumerate(((u_hi, w_hi), (u_hi, w_lo), (u_lo, w_hi))):
                            t = pe.matmul(ps[m % 2][0:rows, :], a[:, k, c0:c0 + rows], w[:, k],
                                          start=(k == 0 and i == 0), stop=(k == KD - 1 and i == 2))
                    t.then_inc(sums_ready, 1)

                def turn(n):
                    rows = TILES[n][1]
                    pe.wait_ge(cn_ready, n + 1)
                    if n >= 2:
                        pe.wait_ge(lo_ready, n - 1)
                    for f in range(4):
                        t = pe.transpose(pt[n % 2][:, f * P:f * P + rows], cn[0:rows, n % 2, f * P:(f + 1) * P],
                                         ident[0:rows, 0:rows])
                    t.then_inc(cT_ready, 1)

                for n in range(N):
                    product(n)
                    if n:
                        turn(n - 1)
                turn(N - 1)
                for n in range(N):
                    product(N + n)


def mla_up(nc, io, scr):
    NQF, NR = MLA_H * NOPE, MLA_H * ROPE
    WQ = NQF + 2 * NR
    WKV = MLA_H * (NOPE + MLA_V)
    KQ = QR // P
    HALF = ROPE // 2
    with ExitStack() as ctx:
        mem = Memory(nc, ctx)
        c_hi = mem.sb("mu_c_hi", [P, KQ + 1, L], F32R)
        c_lo = mem.sb("mu_c_lo", [P, KQ + 1, L], F32R)
        w_raw = mem.sb("mu_w_raw", [P, KQ * WQ + WKV])
        w_hi = mem.sb("mu_w_hi", [P, KQ * WQ + WKV], F32R)
        w_lo = mem.sb("mu_w_lo", [P, KQ * WQ + WKV], F32R)
        g_q = mem.sb("mu_g_q", [P, KQ])
        g_kv = mem.sb("mu_g_kv", [P, 1])
        trig = mem.sb("mu_trig", [P, 2, SEQ])
        rot = mem.sb("mu_rot", [P, 2, 2, 512])
        NS = 4
        o_hi = mem.sb("mu_o_hi", [P, NS, 512], F32R)
        o_lo = mem.sb("mu_o_lo", [P, NS, 512], F32R)
        NB = 6
        ps = [mem.ps(f"mu_ps{i}") for i in range(NB)]
        c_loaded, w_loaded, trig_loaded = mem.sem("mu_c_loaded"), mem.sem("mu_w_loaded"), mem.sem("mu_trig_loaded")
        w_gained, w_hi_ready, w_lo_ready = (mem.sem(f"mu_w_{s}") for s in ("gained", "hi_ready", "lo_ready"))
        sums_ready, rot_ready, hi_ready, lo_ready = (mem.sem(f"mu_{s}_ready") for s in ("sums", "rot", "hi", "lo"))
        rotated = mem.sem("mu_rotated")
        stored = [mem.sem(f"mu_stored{u}") for u in range(NS)]
        q_w = [w[:, 0:KQ * WQ].rearrange("p (k n) -> p k n", k=KQ) for w in (w_raw, w_hi, w_lo)]
        kv_w = [w[:, KQ * WQ:KQ * WQ + WKV] for w in (w_raw, w_hi, w_lo)]

        jobs = []
        for p in range(NR // P):
            for c0, n in TOK_CHUNKS[1:]:
                jobs.append(("rope", NQF + p * P, (c0, n), (scr.mqr_hi[p], scr.mqr_lo[p])))
        for h in range(MLA_H):
            jobs += [("q", h * NOPE, t, (scr.mq_hi[h], scr.mq_lo[h])) for t in TOK_CHUNKS[1:]]
            jobs += [("k", h * NOPE, t, (scr.mk_hi[h], scr.mk_lo[h])) for t in TOK_CHUNKS]
        jobs += [("v", MLA_H * NOPE, t, (scr.mv,)) for t in TILES]
        stores = [sum(16 * len(b[3]) for b in jobs[i % NS:i:NS]) for i in range(len(jobs))]
        bank, first_banks, ropes = 0, [], []
        for kind, *_ in jobs:
            first_banks.append(bank)
            ropes.append(sum(b == "rope" for b, *_ in jobs[:len(ropes)]))
            bank += 2 if kind == "rope" else 1

        def size(job):
            kind, _, (c0, n), _ = job
            return (n, 512) if kind == "v" else (P, n)

        def before(first, last):
            return max((i for i, b in enumerate(first_banks) for w in range(2 if jobs[i][0] == "rope" else 1)
                        if b + w <= last - NB), default=None)

        with nc.Block() as block:
            @block.sync
            def _(sp):
                for k in range(KQ):
                    for src, dst in ((scr.c_hi, c_hi), (scr.c_lo, c_lo)):
                        sp.dma_start(f32(dst[:, k]), src[:, k]).then_inc(c_loaded, 16)
                    src = io.w_q_up[0, k * P:(k + 1) * P, :].rearrange("p (h n) -> p h n", h=MLA_H)
                    to = q_w[0][:, k]
                    swapped = to[:, NQF + NR:WQ].rearrange("p (h n) -> p h n", h=MLA_H)
                    for dst, part in ((to[:, 0:NQF].rearrange("p (h n) -> p h n", h=MLA_H), src[:, :, 0:NOPE]),
                                      (to[:, NQF:NQF + NR].rearrange("p (h n) -> p h n", h=MLA_H), src[:, :, NOPE:NOPE + ROPE]),
                                      (swapped[:, :, 0:HALF], src[:, :, NOPE + HALF:NOPE + ROPE]),
                                      (swapped[:, :, HALF:ROPE], src[:, :, NOPE:NOPE + HALF])):
                        sp.dma_start(dst, part).then_inc(w_loaded, 16)
                for src, dst in ((scr.c_hi, c_hi), (scr.c_lo, c_lo)):
                    sp.dma_start(f32(dst[:, KQ]), src[:, KQ]).then_inc(c_loaded, 16)
                src = io.w_kv_up[0].rearrange("p (h n) -> p h n", h=MLA_H)
                for part in range(2):
                    sp.dma_start(kv_w[0][:, part * 512:(part + 1) * 512].rearrange("p (h n) -> p h n", h=MLA_H),
                                 src[:, :, part * NOPE:part * NOPE + 128]).then_inc(w_loaded, 16)
                sp.dma_start(g_q[:, :], io.g_mla_q).then_inc(w_loaded, 16)
                sp.dma_start(g_kv[:, :], io.g_mla_kv).then_inc(w_loaded, 16)
                sp.dma_start(trig[:, :, :], io.trig_fm).then_inc(trig_loaded, 16)
                for i, job in enumerate(jobs):
                    kind, _, (c0, n), dsts = job
                    rows, cols = size(job)
                    sp.wait_ge(hi_ready if kind == "v" else lo_ready, i + 1)
                    for src, dst in zip((o_hi, o_lo), dsts):
                        if kind == "v":
                            dst = dst[c0:c0 + n, :]
                        elif kind == "k":
                            dst = dst[:, c0:c0 + n]
                        else:
                            dst = dst[:, c0 - META:c0 - META + n]
                        sp.dma_start(dst, f32(src[0:rows, i % NS, 0:cols])).then_inc(stored[i % NS], 16)
                for u in range(NS):
                    sp.wait_ge(stored[u], sum(16 * len(b[3]) for b in jobs[u::NS]))

            @block.gpsimd
            def _(pool):
                pool.wait_ge(w_loaded, 16 * (4 * KQ + 4))
                for k in range(KQ):
                    pool.tensor_scalar(q_w[0][:, k], q_w[0][:, k], g_q[:, k:k + 1], 1.0, ALU.mult, ALU.mult).then_inc(w_gained, 1)
                pool.tensor_scalar(kv_w[0], kv_w[0], g_kv[:, :], 1.0, ALU.mult, ALU.mult).then_inc(w_gained, 1)
                r = 0
                for i, job in enumerate(jobs):
                    if job[0] == "rope":
                        pool.wait_ge(rot_ready, 2 * r + 2)
                        pool.tensor_tensor(rot[:, r % 2, 0], rot[:, r % 2, 0], rot[:, r % 2, 1], ALU.add).then_inc(rotated, 1)
                        r += 1

            @block.scalar
            def _(act):
                for g in range(KQ + 1):
                    act.wait_ge(w_gained, g + 1)
                    dst, src = (q_w[1][:, g], q_w[0][:, g]) if g < KQ else (kv_w[1], kv_w[0])
                    act.activation(dst, src, ACT.Copy).then_inc(w_hi_ready, 1)
                for i, job in enumerate(jobs):
                    rows, cols = size(job)
                    if i >= NS:
                        act.wait_ge(stored[i % NS], stores[i])
                    if job[0] == "rope":
                        act.wait_ge(rotated, ropes[i] + 1)
                        src = rot[:, ropes[i] % 2, 0]
                    else:
                        act.wait_ge(sums_ready, i + 1)
                        src = ps[first_banks[i] % NB][0:rows, 0:cols]
                    dst = o_hi[0:rows, i % NS, 0:cols]
                    act.activation(f32(dst) if job[0] == "v" else dst, src, ACT.Copy).then_inc(hi_ready, 1)

            @block.vector
            def _(dve):
                for g in range(KQ + 1):
                    dve.wait_ge(w_hi_ready, g + 1)
                    dst, hi, src = (q_w[2][:, g], q_w[1][:, g], q_w[0][:, g]) if g < KQ else (kv_w[2], kv_w[1], kv_w[0])
                    dve.tensor_tensor(dst, src, f32(hi), ALU.subtract).then_inc(w_lo_ready, 1)
                dve.wait_ge(trig_loaded, 16)
                for i, job in enumerate(jobs):
                    kind, _, (c0, n), _ = job
                    rows, cols = size(job)
                    if kind == "v":
                        break
                    if kind == "rope":
                        dve.wait_ge(sums_ready, i + 1)
                        if ropes[i] >= 2:
                            dve.wait_ge(lo_ready, ropes[i] - 1)
                        for part in range(2):
                            dve.tensor_tensor(rot[:, ropes[i] % 2, part], ps[(first_banks[i] + part) % NB][:, :],
                                              trig[:, part, c0 - META:c0 - META + n], ALU.mult).then_inc(rot_ready, 1)
                        src = rot[:, ropes[i] % 2, 0]
                    else:
                        src = ps[first_banks[i] % NB][0:rows, 0:cols]
                    dve.wait_ge(hi_ready, i + 1)
                    dve.tensor_tensor(o_lo[0:rows, i % NS, 0:cols], src, f32(o_hi[0:rows, i % NS, 0:cols]),
                                      ALU.subtract).then_inc(lo_ready, 1)

            @block.tensor
            def _(pe):
                pe.wait_ge(w_lo_ready, KQ + 1)
                pe.wait_ge(c_loaded, 16 * 2 * (KQ + 1))
                for i, job in enumerate(jobs):
                    kind, w0, (c0, n), _ = job
                    banks = [first_banks[i], first_banks[i] + 1] if kind == "rope" else [first_banks[i]]
                    last = before(banks[0], banks[-1])
                    if last is not None:
                        pe.wait_ge(hi_ready if jobs[last][0] == "v" else lo_ready, last + 1)
                    for part, bank in enumerate(banks):
                        steps = [(k, i3) for k in (range(KQ) if kind in ("q", "rope") else range(1)) for i3 in range(3)]
                        for k, i3 in steps:
                            wi, ci = ((1, c_hi), (1, c_lo), (2, c_hi))[i3]
                            if kind in ("q", "rope"):
                                w = q_w[wi][:, k, w0 + part * NR:w0 + part * NR + P]
                                c = ci[:, k, c0:c0 + n]
                            else:
                                w = kv_w[wi][:, w0:w0 + (512 if kind == "v" else P)]
                                c = ci[:, KQ, c0:c0 + n]
                            first, stop = (k, i3) == steps[0], (k, i3) == steps[-1]
                            if kind == "v":
                                t = pe.matmul(ps[bank % NB][0:n, :], c, w, start=first, stop=stop)
                            else:
                                t = pe.matmul(ps[bank % NB][:, 0:n], w, c, start=first, stop=stop)
                    t.then_inc(sums_ready, 1)


def row_chunks(i):
    width = META + P * (i + 1)
    n = -(-width // 512)
    step = -(-width // n // 4) * 4
    return [(c, min(step, width - c)) for c in range(0, width, step)]


def attention(nc, io, scr, ident_d, da):
    name = "da" if da else "ml"
    H = DA_H if da else MLA_H
    COMPS = 2 if da else 1
    NG = NT // 4
    scale = DA_SCALE if da else MLA_SCALE
    NKB = 4 if da else 2
    with ExitStack() as ctx:
        mem = Memory(nc, ctx)
        keys = mem.sb(f"{name}_keys", [P, 2, NKB, L], F32R)
        rope_keys = None if da else mem.sb("ml_rope_keys", [P, 2, L], F32R)
        NQB = 2 if da else 3
        qs = mem.sb(f"{name}_qs", [P, 2, NQB, 512], F32R)
        v = mem.sb(f"{name}_v", [P, NT, P])
        v_meta = mem.sb(f"{name}_v_meta", [META, P])
        bias = mem.sb(f"{name}_bias", [P, 2 if da else 1, L])
        GROUP0_W = META + 512
        rows = [mem.sb(f"{name}_rows{u}", [P, 4, L]) for u in range(2)]
        second = mem.sb(f"{name}_second", [P, 2, L]) if da else None
        NPT = 8
        NTB = 3
        pT = mem.sb(f"{name}_pT", [P, NPT, 512])
        o_out = mem.sb(f"{name}_o_out", [P, 2, 512])
        ident = mem.sb(f"{name}_ident", [P, P])
        mx = mem.sb(f"{name}_mx", [P, 2, COMPS, 5])
        nmax = mem.sb(f"{name}_nmax", [P, 2, COMPS])
        nmax_all = mem.sb(f"{name}_nmax_all", [P, 5])
        total = mem.sb(f"{name}_total", [P, 2, COMPS])
        inv = mem.sb(f"{name}_inv", [P, 2, COMPS])
        inv2 = mem.sb(f"{name}_inv2", [P, 2])
        lam_in = mem.sb(f"{name}_lam_in", [P, 4, DA_HD])
        lam = mem.sb(f"{name}_lam", [P, 4])
        NSB = 4
        ps_s = [mem.ps(f"{name}_ps_s{i}") for i in range(NSB)]
        ps_t = [mem.ps(f"{name}_ps_t{i}") for i in range(NTB)]
        ps_o = mem.ps(f"{name}_ps_o")
        start_loaded = mem.sem(f"{name}_start_loaded")
        const_loaded = mem.sem(f"{name}_const_loaded")
        lam_step = mem.sem(f"{name}_lam_step")
        lam_exp = mem.sem(f"{name}_lam_exp")
        keys_loaded = [mem.sem(f"{name}_keys_loaded{u}") for u in range(2)]
        bias_loaded = [mem.sem(f"{name}_bias_loaded{u}") for u in range(2)]
        q_loaded = [mem.sem(f"{name}_q_loaded{u}") for u in range(2)]
        v_loaded = [mem.sem(f"{name}_v_loaded{g}") for g in range(NG)]
        scores_ready, scores_read = mem.sem(f"{name}_scores_ready"), mem.sem(f"{name}_scores_read")
        max_ready, exp_ready = mem.sem(f"{name}_max_ready"), mem.sem(f"{name}_exp_ready")
        inv_ready, first_scaled, probs_ready = (mem.sem(f"{name}_{s}") for s in ("inv_ready", "first_scaled", "probs_ready"))
        inv2_step = mem.sem(f"{name}_inv2_step")
        pT_ready, pv_done = mem.sem(f"{name}_pT_ready"), mem.sem(f"{name}_pv_done")
        act_copied, dve_copied = mem.sem(f"{name}_act_copied"), mem.sem(f"{name}_dve_copied")
        o_copied = mem.sem(f"{name}_o_copied")
        o_stored = [mem.sem(f"{name}_o_stored{u}") for u in range(2)]

        chunks = [(i, c, k0, n) for i in range(NT) for c in range(COMPS) for k0, n in row_chunks(i)]
        NCH = len(chunks)
        tiles_of = lambda g: 1 + 4 * (g + 1)
        NKT = sum(tiles_of(g) for g in range(NG))
        kt_base = [sum(tiles_of(a) for a in range(g)) for g in range(NG)]
        KEY_LOADS = {True: 8, False: 2}[da]
        START_LOADS = KEY_LOADS + 1 + (4 if da else 2)
        Q_LOADS = {True: 4, False: 4}[da]

        def row(i, u):
            g = i // 4
            start = GROUP0_W if g == 1 else 0
            return rows[u ^ (g == 2)][:, i % 4, start:start + META + P * (i + 1)]

        def comp_row(i, c, u):
            return row(i, u) if c == 0 else second[:, i % 2, 0:META + P * (i + 1)]

        def row_steps(carried):
            phases, later = [], list(carried)
            for groups, *_ in PHASES:
                steps = []
                for n, (i, c, k0, w) in enumerate(chunks):
                    if i // 4 not in groups:
                        continue
                    steps.append(("chunk", 0, n))
                    later = [(left - 1, step) for left, step in later]
                    steps += [step for left, step in later if left <= 0]
                    later = [(left, step) for left, step in later if left > 0]
                    if k0 + w == META + P * (i + 1):
                        steps += [step for _, step in later if step[2] - NT * step[1] < i]
                        later = [(left, step) for left, step in later if step[2] - NT * step[1] >= i]
                        later.append((1, ("exp", 0, i, c)))
                        if c == 0:
                            later.append((SCALE_AFTER, ("scale", 0, i)))
                        if c == COMPS - 1:
                            later.append((END_AFTER, ("end", 0, i)))
                phases.append(steps)
            return phases, [(left, (step[0], 1) + step[2:]) for left, step in later]

        def cost(step):
            if step[0] == "chunk":
                return chunks[step[2]][3] + 60
            return META + P * (step[2] + 1) + 250 if step[0] == "end" and da else 0

        def head_steps():
            steps = []
            for p, rows_part in enumerate(row_steps(row_steps([])[1])[0]):
                _, turned, start, put_off = PHASES[p]
                lead_steps = products_of([(b + (p == 0), g) for b, g in PHASES[p - 1][1]])[-PHASES[p - 1][3]:]
                made, body_steps = products_of(turned), []
                turns = [("turn", b, g, t) for b, g in turned for t in range(tiles_of(g))]
                done = 0
                for at, turn in enumerate(turns):
                    body_steps.append(turn)
                    while done < min(at - 1, (at + 1) * (len(made) - put_off) // len(turns)):
                        body_steps.append(made[done])
                        done += 1
                total, passed = sum(cost(step) for step in rows_part), 0
                n_lead, n_body = len(lead_steps), len(body_steps)
                for at, step in enumerate(rows_part):
                    steps.append(step)
                    passed += cost(step)
                    part = passed / total
                    last = at == len(rows_part) - 1
                    while lead_steps and (last or part > start * (1 - (len(lead_steps) - 1) / n_lead)):
                        steps.append(lead_steps.pop(0))
                    while body_steps and (last or part > start + (1 - start) * (1 - len(body_steps) / n_body)):
                        if lead_steps:
                            break
                        kind, back, g, *t = body_steps[0]
                        if kind == "turn" and t == [0] and any(
                                e[0] == "end" and e[2] - NT * e[1] == 4 * g + 3 - NT * back for e in rows_part[at + 1:]):
                            break
                        steps.append(body_steps.pop(0))
                steps += lead_steps + body_steps
            return steps

        def products_of(groups):
            return [("product" if t < tiles_of(g) else "out", b, g) + ((t,) if t < tiles_of(g) else ())
                    for b, g in groups for t in range(tiles_of(g) + 1)]

        PHASES = (((0, 1), ((1, 3),), 0.2, 7), ((2,), ((0, 0), (0, 1)), 0.15, 7), ((3,), ((0, 2),), 0.2, 7))
        SCALE_AFTER, END_AFTER = (2, 5) if da else (2, 2)
        STEPS = head_steps()

        def walk(h, pair, u, handlers, back=(0, 1)):
            for kind, b, *args in STEPS:
                if b in back and kind in handlers:
                    handlers[kind](h - b if b else h, *args, u=u ^ b, pair=None if b else pair)

        def heads(engine, handlers):
            walk(0, 0, 0, handlers, (0,))
            with engine.Fori(0, H // 2 - 1) as j:
                walk(2 * j + 1, j, 1, handlers)
                walk(2 * j + 2, j + 1, 0, handlers)
            walk(H - 1, H // 2 - 1, 1, handlers)
            walk(H, H // 2, 0, handlers, (1,))

        def key_cols(t):
            return (0, META) if t == 0 else (META + P * (t - 1), P)

        def first_tile(g, t):
            return max(0, t - 1 - 4 * g)

        BY_DVE = [not da and at % 2 == 1 for at in range(NKT)]

        def last_user(n, slots):
            return max(a for a in range(NKT) if a % slots == n)

        def slot_free(engine, h, n):
            if n >= NPT:
                engine.wait_ge(pv_done, NKT * h + n - NPT + 1)
            elif not (isinstance(h, int) and h == 0):
                engine.wait_ge(pv_done, NKT * (h - 1) + last_user(n, NPT) + 1)

        with nc.Block() as block:
            @block.sync
            def _(sp):
                def load_keys(h, u, cols=slice(0, L), loaded=keys_loaded):
                    if da:
                        for c in range(2):
                            rows = slice(c * DA_HD, (c + 1) * DA_HD)
                            for j, src in enumerate((scr.qk_hi, scr.qk_lo)):
                                for half in range(2):
                                    sp.dma_start(f32(keys[half * 64:half * 64 + 64, u, 2 * c + j, cols]),
                                                 flat(src[ds(h + DA_H, 1), rows, cols])).then_inc(loaded[u], 16)
                    else:
                        for j, src in enumerate((scr.mk_hi, scr.mk_lo)):
                            sp.dma_start(f32(keys[:, u, j, cols]), flat(src[ds(h, 1), :, cols])).then_inc(loaded[u], 16)

                def load_bias(h, u, cols=slice(0, L), loaded=bias_loaded):
                    if da:
                        sp.dma_start(bias[:, u, cols], flat(io.bias[ds(h, 1), :, cols])).then_inc(loaded[u], 16)
                    elif h is None:
                        sp.dma_start(bias[:, 0, cols], io.bias[DA_H, :, cols]).then_inc(loaded[0], 16)

                def load_q(h, pair, u, g):
                    cols = slice(512 * g, 512 * g + 512)
                    if da:
                        for c in range(2):
                            for j, src in enumerate((scr.qk_hi, scr.qk_lo)):
                                sp.dma_start(f32(qs[64 * j:64 * j + 64, g % 2, c]),
                                             flat(src[ds(h, 1), c * 64:c * 64 + 64, META + 512 * g:META + 512 * g + 512])).then_inc(q_loaded[g % 2], 16)
                    else:
                        for j, src in enumerate((scr.mq_hi, scr.mq_lo)):
                            sp.dma_start(f32(qs[:, g % 2, j]), flat(src[ds(h, 1), :, cols])).then_inc(q_loaded[g % 2], 16)
                        for j, src in enumerate((scr.mqr_hi, scr.mqr_lo)):
                            sp.dma_start(f32(qs[64 * j:64 * j + 64, g % 2, 2]),
                                         flat(src[ds(pair, 1), u * 64:u * 64 + 64, cols])).then_inc(q_loaded[g % 2], 16)

                def load_v(h, g):
                    src = scr.v if da else scr.mv
                    cols = ds(h * P, P)
                    sp.dma_start(v[:, 4 * g:4 * g + 4, :],
                                 src[META + 512 * g:META + 512 * g + 512, cols].rearrange("(t p) n -> p t n", p=P)).then_inc(v_loaded[g], 16)
                    if g == 0:
                        sp.dma_start(v_meta[:, :], src[0:META, cols]).then_inc(v_loaded[g], 16)

                def store(h, g):
                    sp.wait_ge(o_copied, NG * h + g + 1)
                    sp.dma_start(flat(scr.yT[ds(h + (0 if da else DA_H), 1), :, 512 * g:512 * g + 512]), o_out[:, g % 2]).then_inc(o_stored[g % 2], 16)

                def scores_done(h, g):
                    sp.wait_ge(scores_ready, NCH * h + sum(1 for i, *_ in chunks if i < 4 * (g + 1)))

                def head(h, pair, u):
                    first, last = isinstance(h, int) and h == 0, isinstance(h, int) and h == H - 1
                    scores_done(h, 0)
                    load_q(h, pair, u, 2)

                    def next_v(g):
                        sp.wait_ge(pv_done, NKT * (h - 1) + kt_base[NG - 1] + 5 + 4 * g)
                        load_v(h, g)

                    if not first:
                        store(h - 1, 2)
                        for g in range(2):
                            next_v(g)
                    if not last:
                        if not first:
                            sp.wait_ge(scores_read, NCH * h)
                        load_keys(h + 1, 1 - u)
                        load_bias(h + 1, 1 - u)
                    if not first:
                        for g in range(2, NG):
                            next_v(g)
                        store(h - 1, 3)
                    scores_done(h, 1)
                    load_q(h, pair, u, 3)
                    scores_done(h, 2)
                    if not last:
                        load_q(h + 1, pair + u, 1 - u, 0)
                    store(h, 0)
                    scores_done(h, 3)
                    if not last:
                        load_q(h + 1, pair + u, 1 - u, 1)
                    store(h, 1)

                whole, early, late = (0 if da else None), slice(0, GROUP0_W), slice(GROUP0_W, L)
                load_keys(0, 0, early, [start_loaded])
                load_q(0, 0, 0, 0)
                load_bias(whole, 0, slice(L - GROUP0_W, L), [start_loaded])
                if not da:
                    for cols, loaded in ((early, start_loaded), (late, const_loaded)):
                        for j, src in enumerate((scr.c_hi, scr.c_lo)):
                            sp.dma_start(f32(rope_keys[:, j, cols]), src[:, 3, cols]).then_inc(loaded, 16)
                if da:
                    for j, src in enumerate((io.lam_q1, io.lam_k1, io.lam_q2, io.lam_k2)):
                        sp.dma_start(lam_in[:, j], src.broadcast_to([P, DA_HD])).then_inc(start_loaded, 16)
                sp.dma_start(ident[:, :], ident_d).then_inc(const_loaded, 16)
                load_keys(0, 0, late)
                load_bias(whole, 0, slice(0, L - GROUP0_W))
                load_q(0, 0, 0, 1)
                for g in range(NG):
                    load_v(0, g)
                head(0, 0, 0)
                with sp.Fori(0, H // 2 - 1) as j:
                    head(2 * j + 1, j, 1)
                    head(2 * j + 2, j + 1, 0)
                head(H - 1, H // 2 - 1, 1)
                store(H - 1, 2)
                store(H - 1, 3)
                for u in range(2):
                    sp.wait_ge(o_stored[u], 16 * 2 * H)

            @block.gpsimd
            def _(pool):
                def scaled(h, i, u, **at):
                    hold(pool, inv_ready, NT * h + i + 1)
                    pool.tensor_scalar(row(i, u), row(i, u), inv[:, i % 2, 0:1], 1.0, ALU.mult,
                                       ALU.mult).then_inc(first_scaled if da else probs_ready, 1)

                heads(pool, {"scale": scaled})

            @block.scalar
            def _(act):
                def exp(h, i, c, u, **at):
                    act.wait_ge(max_ready, NT * COMPS * h + COMPS * i + c + 1)
                    act.activation(comp_row(i, c, u), comp_row(i, c, u), ACT.Exp, bias=nmax[:, i % 2, c:c + 1], scale=scale,
                                   accum_out=total[:, i % 2, c:c + 1]).then_inc(exp_ready, 1)

                def copy(h, g, t, **at):
                    n = kt_base[g] + t
                    if not BY_DVE[n]:
                        c0 = P * first_tile(g, t)
                        rows = key_cols(t)[1]
                        slot_free(act, h, n)
                        act.wait_ge(pT_ready, NKT * h + n + 1)
                        act.activation(pT[0:rows, n % NPT, c0:512], ps_t[n % NTB][0:rows, c0:512], ACT.Copy).then_inc(act_copied, 1)

                def out(h, g, **at):
                    act.wait_ge(pv_done, NKT * h + kt_base[g] + tiles_of(g))
                    if not (isinstance(h, int) and h == 0 and g < 2):
                        act.wait_ge(o_stored[g % 2], 16 * (2 * h + g // 2))
                    act.activation(o_out[:, g % 2], ps_o[:, :], ACT.Copy).then_inc(o_copied, 1)

                if da:
                    for j in range(2):
                        act.wait_ge(lam_step, j + 1)
                        act.activation(lam[:, j:j + 1], lam[:, j:j + 1], ACT.Exp).then_inc(lam_exp, 1)
                heads(act, {"exp": exp, "turn": copy, "out": out})

            @block.vector
            def _(dve):
                def chunk(h, n, pair, u):
                    i, c, k0, w = chunks[n]
                    g = i // 4
                    first_head = isinstance(h, int) and h == 0
                    if n == (chunks.index((4, 0, 0, row_chunks(4)[0][1])) if first_head else 0) and (da or first_head):
                        dve.wait_ge(bias_loaded[u], 16 * (pair + 1))
                    if i % 4 == 0 and c == 0 and k0 == 0:
                        if g == 3:
                            dve.wait_ge(pT_ready, NKT * h + kt_base[2])
                        elif g != 1 and not (isinstance(h, int) and h == 0):
                            dve.wait_ge(pT_ready, NKT * (h - 1) + (kt_base[3] if g == 0 else NKT))
                    nth = sum(1 for m in range(n) if chunks[m][:2] == (i, c))
                    b0 = (NT - 1 - i) * P + k0
                    hold(dve, scores_ready, NCH * h + n + 1)
                    dve.tensor_tensor_reduce(out=comp_row(i, c, u)[:, k0:k0 + w], in0=ps_s[n % NSB][:, 0:w],
                                             in1=bias[:, u if da else 0, b0:b0 + w], scale=1.0, scalar=LOWEST,
                                             op0=ALU.add, op1=ALU.max,
                                             accum_out=mx[:, i % 2, c, nth:nth + 1]).then_inc(scores_read, 1)
                    if k0 + w == META + P * (i + 1):
                        dve.wait_ge(scores_read, NCH * h + n + 1)
                        dve.tensor_scalar(nmax_all[:, 0:nth + 1], mx[:, i % 2, c, 0:nth + 1], -scale, None, ALU.mult, ALU.min,
                                          accum_out=nmax[:, i % 2, c:c + 1]).then_inc(max_ready, 1)

                def invert(h, i, u, **at):
                    dve.wait_ge(exp_ready, NT * COMPS * h + COMPS * i + 1)
                    if not (isinstance(h, int) and h == 0 and i < 2):
                        dve.wait_ge(first_scaled if da else probs_ready, NT * h + i - 1)
                    dve.reciprocal(inv[:, i % 2, 0:1], total[:, i % 2, 0:1]).then_inc(inv_ready, 1)

                def end(h, i, u, **at):
                    if not da:
                        return
                    n = 2 * (NT * h + i)
                    dve.wait_ge(exp_ready, NT * COMPS * h + COMPS * (i + 1))
                    dve.reciprocal(inv[:, i % 2, 1:2], total[:, i % 2, 1:2]).then_inc(inv2_step, 1)
                    dve.wait_ge(inv2_step, n + 1)
                    dve.tensor_scalar(inv2[:, i % 2:i % 2 + 1], inv[:, i % 2, 1:2], lam[:, 3:4], None, ALU.mult).then_inc(inv2_step, 1)
                    dve.wait_ge(inv2_step, n + 2)
                    dve.wait_ge(first_scaled, NT * h + i + 1)
                    dve.scalar_tensor_tensor(out=row(i, u), in0=comp_row(i, 1, u), scalar=inv2[:, i % 2:i % 2 + 1], in1=row(i, u),
                                             op0=ALU.mult, op1=ALU.add).then_inc(probs_ready, 1)

                def copy(h, g, t, **at):
                    n = kt_base[g] + t
                    if BY_DVE[n]:
                        c0 = P * first_tile(g, t)
                        rows = key_cols(t)[1]
                        slot_free(dve, h, n)
                        dve.wait_ge(pT_ready, NKT * h + n + 1)
                        dve.tensor_copy(pT[0:rows, n % NPT, c0:512], ps_t[n % NTB][0:rows, c0:512]).then_inc(dve_copied, 1)

                dve.wait_ge(start_loaded, 16 * START_LOADS)
                if da:
                    for j in range(2):
                        dve.tensor_tensor_reduce(out=lam_in[:, 2 * j], in0=lam_in[:, 2 * j], in1=lam_in[:, 2 * j + 1], scale=1.0,
                                                 scalar=0.0, op0=ALU.mult, op1=ALU.add, accum_out=lam[:, j:j + 1]).then_inc(lam_step, 1)
                    dve.wait_ge(lam_exp, 2)
                    dve.tensor_tensor(lam[:, 2:3], lam[:, 1:2], lam[:, 0:1], ALU.subtract).then_inc(lam_step, 1)
                    dve.wait_ge(lam_step, 3)
                    dve.tensor_scalar(lam[:, 3:4], lam[:, 2:3], -LAMBDA_INIT, None, ALU.add).then_inc(lam_step, 1)
                    dve.wait_ge(lam_step, 4)
                heads(dve, {"chunk": chunk, "scale": invert, "end": end, "turn": copy})

            @block.tensor
            def _(pe):
                def scores(h, n, pair, u):
                    i, c, k0, w = chunks[n]
                    g, b = i // 4, i % 4
                    first_head = isinstance(h, int) and h == 0
                    if n == (chunks.index((4, 0, 0, row_chunks(4)[0][1])) if first_head else 0):
                        pe.wait_ge(keys_loaded[u], 16 * KEY_LOADS * (pair + 1))
                        if first_head:
                            pe.wait_ge(const_loaded, 16 * (1 if da else 3))
                    if b == 0 and c == 0 and k0 == 0:
                        pe.wait_ge(q_loaded[g % 2], 16 * Q_LOADS * (2 * h + g // 2 + 1))
                    if not (isinstance(h, int) and h == 0 and n < NSB):
                        pe.wait_ge(scores_read, NCH * h + n - NSB + 1)
                    cols = slice(P * b, P * b + P)
                    if da:
                        pairs = [(qs[:, g % 2, c, cols], keys[:, u, 2 * c + j, k0:k0 + w]) for j in range(2)]
                    else:
                        q_hi, q_lo, q_rope = (qs[:, g % 2, j, cols] for j in range(3))
                        k_hi, k_lo = (keys[:, u, j, k0:k0 + w] for j in range(2))
                        pairs = [(q_hi, k_hi), (q_hi, k_lo), (q_lo, k_hi)]
                        pairs += [(q_rope, rope_keys[:, j, k0:k0 + w]) for j in range(2)]
                    for j, (q, k) in enumerate(pairs):
                        m = pe.matmul(ps_s[n % NSB][:, 0:w], q, k, start=j == 0, stop=j == len(pairs) - 1)
                    m.then_inc(scores_ready, 1)

                def copied(h, n):
                    by_dve = sum(BY_DVE[:n + 1])
                    if BY_DVE[n]:
                        pe.wait_ge(dve_copied, sum(BY_DVE) * h + by_dve)
                    else:
                        pe.wait_ge(act_copied, (NKT - sum(BY_DVE)) * h + n + 1 - by_dve)

                def turn(h, g, t, u, **at):
                    if t == 0:
                        pe.wait_ge(probs_ready, NT * h + 4 * g + 4)
                    n, (k0, rows) = kt_base[g] + t, key_cols(t)
                    if n >= NTB:
                        copied(h, n - NTB)
                    elif not (isinstance(h, int) and h == 0):
                        copied(h - 1, last_user(n, NTB))
                    for b in range(first_tile(g, t), 4):
                        m = pe.transpose(ps_t[n % NTB][0:rows, P * b:P * b + P], row(4 * g + b, u)[:, k0:k0 + rows], ident[:, :])
                    m.then_inc(pT_ready, 1)

                def product(h, g, t, **at):
                    n, rows = kt_base[g] + t, key_cols(t)[1]
                    copied(h, n)
                    if t == 0:
                        pe.wait_ge(v_loaded[0], 32 * (h + 1))
                        if not (isinstance(h, int) and h == 0 and g == 0):
                            pe.wait_ge(o_copied, NG * h + g)
                    elif t % 4 == 1 and t > 1:
                        pe.wait_ge(v_loaded[t // 4], 16 * (h + 1))
                    c0 = P * first_tile(g, t)
                    pe.matmul(ps_o[:, c0:512], v_meta[:, :] if t == 0 else v[:, t - 1], pT[0:rows, n % NPT, c0:512],
                              start=t == 0, stop=t == tiles_of(g) - 1).then_inc(pv_done, 1)

                pe.wait_ge(start_loaded, 16 * START_LOADS)
                heads(pe, {"chunk": scores, "turn": turn, "product": product})


def mix_out(nc, io, scr):
    with ExitStack() as ctx:
        mem = Memory(nc, ctx)
        w_raw = mem.sb("mo_w_raw", [P, 2, D])
        w_hi = mem.sb("mo_w_hi", [P, KD, D], F32R)
        w_lo = mem.sb("mo_w_lo", [P, KD, D], F32R)
        g_sub = mem.sb("mo_g_sub", [P, 2])
        ones = mem.sb("mo_ones", [P, P])
        eps = mem.sb("mo_eps", [P, 1])
        ident = mem.sb("mo_ident", [P, P])
        g_post = mem.sb("mo_g_post", [P, D])
        y = mem.sb("mo_y", [P, 2, KD, P])
        y_hi = mem.sb("mo_y_hi", [P, 2, KD, P], F32R)
        y_lo = mem.sb("mo_y_lo", [P, 2, KD, P], F32R)
        sq = mem.sb("mo_sq", [P, DA_H * P])
        y_rstd = mem.sb("mo_y_rstd", [P, DA_H * P])
        xres = mem.sb("mo_xres", [P, 2, D])
        h = mem.sb("mo_h", [P, 2, D])
        hn = mem.sb("mo_hn", [P, 2, D])
        junk = mem.sb("mo_junk", [P, D])
        u_hi = mem.sb("mo_u_hi", [P, 2, KD, P], F32R)
        u_lo = mem.sb("mo_u_lo", [P, 2, KD, P], F32R)
        stat = mem.sb("mo_stat", [P, 2, 6])
        ps_r = mem.ps("mo_ps_r")
        ps_m = [mem.ps(f"mo_ps_m{i}", D) for i in range(2)]
        ps_t = mem.ps("mo_ps_t", D)
        const_loaded, const_set = mem.sem("mo_const_loaded"), mem.sem("mo_const_set")
        w_loaded = [mem.sem(f"mo_w_loaded{u}") for u in range(2)]
        w_gained, w_hi_ready, w_lo_ready = (mem.sem(f"mo_w_{s}") for s in ("gained", "hi_ready", "lo_ready"))
        y_loaded = [mem.sem(f"mo_y_loaded{u}") for u in range(2)]
        x_loaded = [mem.sem(f"mo_x_loaded{u}") for u in range(2)]
        sq_ready, mean_ready, y_log_ready, y_rstd_ready, y_normed = (mem.sem(f"mo_y_{s}") for s in ("sq", "mean", "log", "rstd", "normed"))
        y_hi_ready, y_lo_ready, mix_ready = (mem.sem(f"mo_{s}") for s in ("y_hi_ready", "y_lo_ready", "mix_ready"))
        stat_step = mem.sem("mo_stat_step")
        post_ready, h_ready, hn_ready, hT_ready = (mem.sem(f"mo_{s}_ready") for s in ("post", "h", "hn", "hT"))
        u_hi_ready, u_lo_ready = mem.sem("mo_u_hi_ready"), mem.sem("mo_u_lo_ready")
        h_stored = [mem.sem(f"mo_h_stored{u}") for u in range(2)]
        u_stored = [mem.sem(f"mo_u_stored{u}") for u in range(2)]

        def steps(engine, body):
            for s in range(4):
                body(s, s % 2, s // 2, True, s >= 2, True)
            with engine.Fori(0, NT // 2 - 2) as j:
                for u in range(2):
                    body(2 * j + 4 + u, u, j + 2, True, True, False)
            for s in range(NT, NT + 2):
                body(s, s % 2, s // 2, False, True, False)

        with nc.Block() as block:
            @block.sync
            def _(sp):
                def load_w(k):
                    if k >= 2:
                        sp.wait_ge(w_lo_ready, k - 1)
                    sp.dma_start(w_raw[:, k % 2], io.w_o[0, k * P:(k + 1) * P, :]).then_inc(w_loaded[k % 2], 16)

                def load_y(t, u):
                    sp.dma_start(y[:, u], scr.yT[:, :, ds(t * P, P)].rearrange("f p t -> p f t")).then_inc(y_loaded[u], 16)

                def load_x(t, u):
                    sp.dma_start(xres[:, u], flat(io.x[:, ds(t * P, P), :])).then_inc(x_loaded[u], 16)

                load_w(0)
                load_w(1)
                sp.dma_start(g_sub[:, 0:1], io.g_da_sub).then_inc(const_loaded, 16)
                sp.dma_start(ident[:, :], io.ident).then_inc(const_loaded, 16)
                sp.dma_start(g_post[:, :], io.g_attn_post.broadcast_to([P, D])).then_inc(const_loaded, 16)
                for t in range(2):
                    load_y(t, t)
                for k in range(2, KD):
                    load_w(k)
                for t in range(2):
                    load_x(t, t)

                def body(s, u, nth, prep, post, first):
                    if not post:
                        return
                    if prep:
                        hold(sp, y_lo_ready, s - 1)
                        load_y(s, u)
                    cols = ds((s - 2) * P, P)
                    hold(sp, h_ready, s - 1)
                    sp.dma_start(scr.h[cols, :], h[:, u]).then_inc(h_stored[u], 16)
                    if prep:
                        load_x(s, u)
                    hold(sp, u_lo_ready, s - 1)
                    for src, dst in ((u_hi, scr.u_hi), (u_lo, scr.u_lo)):
                        sp.dma_start(dst[:, :, cols], f32(src[:, u])).then_inc(u_stored[u], 16)

                steps(sp, body)
                for u in range(2):
                    sp.wait_ge(h_stored[u], 16 * NT // 2)
                    sp.wait_ge(u_stored[u], 32 * NT // 2)

            @block.gpsimd
            def _(pool):
                pool.memset(ones[:, :], 1.0 / DA_V).then_inc(const_set, 1)
                pool.memset(eps[:, :], EPS).then_inc(const_set, 1)
                pool.wait_ge(const_loaded, 48)
                pool.tensor_scalar(g_sub[:, 1:2], g_sub[:, 0:1], 1.0 - LAMBDA_INIT, 1.0, ALU.mult, ALU.mult).then_inc(const_set, 1)
                pool.wait_ge(const_set, 3)
                for k in range(DA_H):
                    pool.wait_ge(w_loaded[k % 2], 16 * (k // 2) + 16)
                    pool.tensor_scalar(w_raw[:, k % 2], w_raw[:, k % 2], g_sub[:, 1:2], 1.0, ALU.mult, ALU.mult).then_inc(w_gained, 1)

                def body(s, u, nth, prep, post, first):
                    if not post:
                        return
                    if not first:
                        pool.wait_ge(hT_ready, s - 3)
                    pool.wait_ge(stat_step, 6 * (s - 1))
                    pool.nop(nofuse=True)
                    pool.tensor_scalar(hn[:, u], h[:, u], stat[:, u, 5:6], 1.0, ALU.mult, ALU.mult).then_inc(hn_ready, 1)

                steps(pool, body)

            @block.scalar
            def _(act):
                act.preload_act_table_set("natural_log_exp_and_others")
                act.wait_ge(const_set, 3)
                for k in range(KD):
                    if k < DA_H:
                        act.wait_ge(w_gained, k + 1)
                    else:
                        act.wait_ge(w_loaded[k % 2], 16 * (k // 2) + 16)
                    act.activation(w_hi[:, k], w_raw[:, k % 2], ACT.Copy).then_inc(w_hi_ready, 1)

                def rstd(src, s, u, at):
                    n = 6 * (s - 2) + at
                    act.activation(junk[:, :], src, ACT.Square, accum_out=stat[:, u, at:at + 1]).then_inc(stat_step, 1)
                    act.wait_ge(stat_step, n + 1)
                    act.activation(stat[:, u, at + 1:at + 2], stat[:, u, at:at + 1], ACT.Ln, bias=eps[:, :], scale=1.0 / D).then_inc(stat_step, 1)
                    act.wait_ge(stat_step, n + 2)
                    act.activation(stat[:, u, at + 2:at + 3], stat[:, u, at + 1:at + 2], ACT.Exp, scale=-0.5).then_inc(stat_step, 1)

                def body(s, u, nth, prep, post, first):
                    if post:
                        act.wait_ge(mix_ready, s - 1)
                        rstd(ps_m[u][:, :], s, u, 0)
                    if prep:
                        act.wait_ge(y_loaded[u], 16 * nth + 16)
                        act.activation(sq[:, :].rearrange("p (f t) -> p f t", f=DA_H), y[:, u, 0:DA_H], ACT.Square).then_inc(sq_ready, 1)
                    if post:
                        act.wait_ge(h_ready, s - 1)
                        rstd(h[:, u], s, u, 3)
                    if prep:
                        act.wait_ge(mean_ready, s + 1)
                        act.activation(y_rstd[:, :], ps_r[:, :], ACT.Ln, bias=eps[:, :]).then_inc(y_log_ready, 1)
                        act.wait_ge(y_log_ready, s + 1)
                        act.activation(y_rstd[:, :], y_rstd[:, :], ACT.Exp, scale=-0.5).then_inc(y_rstd_ready, 1)
                        act.wait_ge(y_normed, s + 1)
                        act.activation(y_hi[:, u], y[:, u], ACT.Copy).then_inc(y_hi_ready, 1)
                    if post:
                        act.wait_ge(hT_ready, s - 1)
                        if not first:
                            act.wait_ge(u_stored[u], 32 * (nth - 1))
                        act.activation(u_hi[:, u], ps_t[:, :].rearrange("p (k t) -> p k t", k=KD), ACT.Copy).then_inc(u_hi_ready, 1)

                steps(act, body)

            @block.vector
            def _(dve):
                for k in range(KD):
                    dve.wait_ge(w_hi_ready, k + 1)
                    dve.tensor_tensor(w_lo[:, k], w_raw[:, k % 2], f32(w_hi[:, k]), ALU.subtract).then_inc(w_lo_ready, 1)

                def body(s, u, nth, prep, post, first):
                    if post:
                        if not first:
                            dve.wait_ge(h_stored[u], 16 * (nth - 1))
                            dve.wait_ge(hn_ready, s - 3)
                        dve.wait_ge(stat_step, 6 * (s - 2) + 3)
                        dve.scalar_tensor_tensor(out=h[:, u], in0=ps_m[u][:, :], scalar=stat[:, u, 2:3], in1=g_post[:, :],
                                                 op0=ALU.mult, op1=ALU.mult).then_inc(post_ready, 1)
                        dve.wait_ge(x_loaded[u], 16 * nth)
                        dve.wait_ge(post_ready, s - 1)
                        dve.tensor_tensor(h[:, u], h[:, u], xres[:, u], ALU.add).then_inc(h_ready, 1)
                    if prep:
                        dve.wait_ge(y_rstd_ready, s + 1)
                        dve.tensor_tensor(y[:, u, 0:DA_H], y[:, u, 0:DA_H], y_rstd[:, :].rearrange("p (f t) -> p f t", f=DA_H),
                                          ALU.mult).then_inc(y_normed, 1)
                        dve.wait_ge(y_hi_ready, s + 1)
                        dve.tensor_tensor(y_lo[:, u], y[:, u], f32(y_hi[:, u]), ALU.subtract).then_inc(y_lo_ready, 1)
                    if post:
                        dve.wait_ge(u_hi_ready, s - 1)
                        dve.tensor_tensor(u_lo[:, u], ps_t[:, :].rearrange("p (k t) -> p k t", k=KD), f32(u_hi[:, u]),
                                          ALU.subtract).then_inc(u_lo_ready, 1)

                dve.wait_ge(const_loaded, 48)
                steps(dve, body)

            @block.tensor
            def _(pe):
                pe.wait_ge(const_set, 3)
                pe.wait_ge(const_loaded, 48)

                def product(s, u, half):
                    cols = slice(512 * half, 512 * half + 512)
                    for k in range(KD):
                        for i, (a, w) in enumerate(((y_hi, w_hi), (y_hi, w_lo), (y_lo, w_hi))):
                            m = pe.matmul(ps_m[1 - u][:, cols], a[:, 1 - u, k], w[:, k, cols],
                                          start=k == 0 and i == 0, stop=k == KD - 1 and i == 2)
                    return m

                def body(s, u, nth, prep, post, first):
                    has_product = not isinstance(s, int) or 1 <= s <= NT
                    if has_product:
                        if isinstance(s, int) and s == 1:
                            pe.wait_ge(w_lo_ready, KD)
                        pe.wait_ge(y_lo_ready, s)
                        if not isinstance(s, int) or s >= 3:
                            pe.wait_ge(post_ready, s - 2)
                        product(s, u, 0)
                    if prep:
                        pe.wait_ge(sq_ready, s + 1)
                        pe.matmul(ps_r[:, :], ones[:, :], sq[:, :], start=True, stop=True).then_inc(mean_ready, 1)
                    if has_product:
                        product(s, u, 1).then_inc(mix_ready, 1)
                    if post:
                        pe.wait_ge(hn_ready, s - 1)
                        if not (isinstance(s, int) and s == 2):
                            pe.wait_ge(u_lo_ready, s - 2)
                        for k in range(KD):
                            m = pe.transpose(ps_t[:, k * P:(k + 1) * P], hn[:, u, k * P:(k + 1) * P], ident[:, :])
                        m.then_inc(hT_ready, 1)

                steps(pe, body)


def mlp(nc, io, scr):
    GT = 1024
    NGR = SEQ // GT
    TG = GT // P
    NM = DFF // P
    NC = NM // 2
    with ExitStack() as ctx:
        mem = Memory(nc, ctx)
        u_hi = mem.sb("ff_u_hi", [P, KD, GT], F32R)
        u_lo = mem.sb("ff_u_lo", [P, KD, GT], F32R)
        hid_hi = mem.sb("ff_hid_hi", [P, 4, GT], F32R)
        hid_lo = mem.sb("ff_hid_lo", [P, 4, GT], F32R)
        acc = mem.sb("ff_acc", [P, TG, D])
        w1_raw = mem.sb("ff_w1_raw", [P, KD, P])
        w1_hi = mem.sb("ff_w1_hi", [P, 2, KD, P], F32R)
        w1_lo = mem.sb("ff_w1_lo", [P, 2, KD, P], F32R)
        w2_raw = mem.sb("ff_w2_raw", [P, D])
        w2_hi = mem.sb("ff_w2_hi", [P, 4, D], F32R)
        w2_lo = mem.sb("ff_w2_lo", [P, 4, D], F32R)
        relu = mem.sb("ff_relu", [P, GT])
        square = mem.sb("ff_square", [P, GT])
        g_post = mem.sb("ff_g_post", [P, D])
        h_in = mem.sb("ff_h_in", [P, 2, D])
        g_pre = mem.sb("ff_g_pre", [P, KD])
        eps = mem.sb("ff_eps", [P, 1])
        stat = mem.sb("ff_stat", [P, 3])
        ps1 = [mem.ps(f"ff_ps1_{i}", GT) for i in range(2)]
        ps2 = [mem.ps(f"ff_ps2_{i}", D) for i in range(2)]
        const_loaded, eps_set = mem.sem("ff_const_loaded"), mem.sem("ff_eps_set")
        u_loaded = [mem.sem(f"ff_u_loaded{k}") for k in range(KD)]
        w1_loaded, w1_gained, w1_hi_ready, w1_lo_ready = (mem.sem(f"ff_w1_{s}") for s in ("loaded", "gained", "hi_ready", "lo_ready"))
        w2_loaded, w2_hi_ready, w2_lo_ready = (mem.sem(f"ff_w2_{s}") for s in ("loaded", "hi_ready", "lo_ready"))
        pre_ready, relu_ready, square_ready = (mem.sem(f"ff_{s}_ready") for s in ("pre", "relu", "square"))
        hid_hi_ready, hid_lo_ready = mem.sem("ff_hid_hi_ready"), mem.sem("ff_hid_lo_ready")
        part_ready, part_added = mem.sem("ff_part_ready"), mem.sem("ff_part_added")
        stat_step = mem.sem("ff_stat_step")
        post_ready, out_ready = mem.sem("ff_post_ready"), mem.sem("ff_out_ready")
        h_loaded = [mem.sem(f"ff_h_loaded{u}") for u in range(2)]
        out_stored = [mem.sem(f"ff_out_stored{t}") for t in range(TG)]
        w1_v = io.w_ff1.rearrange("a (k p) n -> p (a k) n", p=P)

        def chunk_steps(engine, body, peeled=2):
            body(0, 0)
            body(1, 1)
            end = NC if peeled == 2 else NC - 2
            with engine.Fori(0, (end - 2) // 2) as j:
                body(2 * j + 2, 0)
                body(2 * j + 3, 1)
            for c in range(end, NC):
                body(c, c % 2)

        with nc.Block() as block:
            @block.sync
            def _(sp):
                def load_w1(G, m):
                    static = isinstance(m, int)
                    if not (static and NM * G + m == 0):
                        hold(sp, w1_lo_ready, NM * G + m)
                    col = (m % NM) * P if static else m * P
                    sp.dma_start(w1_raw[:, :, :], w1_v[:, :, ds(col, P)]).then_inc(w1_loaded, 16)

                def load_w2(G, m):
                    if not (isinstance(m, int) and NM * G + m == 0):
                        hold(sp, w2_lo_ready, NM * G + m)
                    sp.dma_start(w2_raw[:, :], flat(io.w_ff2[:, ds(m * P, P), :])).then_inc(w2_loaded, 16)

                def load_u(G):
                    for k in range(KD):
                        for src, dst in ((scr.u_hi, u_hi), (scr.u_lo, u_lo)):
                            sp.dma_start(f32(dst[:, k]), src[:, k, G * GT:(G + 1) * GT]).then_inc(u_loaded[k], 16)

                def load_h(n):
                    sp.dma_start(h_in[:, n % 2], scr.h[n * P:(n + 1) * P, :]).then_inc(h_loaded[n % 2], 16)

                sp.dma_start(g_pre[:, :], io.g_mlp_pre).then_inc(const_loaded, 16)
                load_w1(0, 0)
                load_u(0)
                sp.dma_start(g_post[:, :], io.g_mlp_post.broadcast_to([P, D])).then_inc(const_loaded, 16)
                load_w1(0, 1)
                load_h(0)
                for G in range(NGR):
                    load_w2(G, 0)
                    load_w1(G, 2)
                    with sp.Fori(1, NM - 2) as m:
                        load_w2(G, m)
                        load_w1(G, m + 2)
                    for m in range(NM - 2, NM):
                        load_w2(G, m)
                        if G < NGR - 1:
                            load_w1(G, m + 2)
                    if G < NGR - 1:
                        sp.wait_ge(pre_ready, NM * (G + 1))
                        load_u(G + 1)
                    for t in range(TG):
                        n = TG * G + t
                        if n + 1 < TG * NGR:
                            if n:
                                sp.wait_ge(out_ready, n)
                            load_h(n + 1)
                        sp.wait_ge(out_ready, n + 1)
                        sp.dma_start(io.out[0, n * P:(n + 1) * P, :], acc[:, t]).then_inc(out_stored[t], 16)
                for t in range(TG):
                    sp.wait_ge(out_stored[t], 16 * NGR)

            @block.gpsimd
            def _(pool):
                def gain(n):
                    pool.wait_ge(w1_loaded, 16 * n + 16)
                    pool.tensor_tensor(w1_raw[:, :, :], w1_raw[:, :, :], g_pre[:, :].unsqueeze(2).broadcast_to([P, KD, P]),
                                       ALU.mult).then_inc(w1_gained, 1)

                pool.memset(eps[:, :], EPS).then_inc(eps_set, 1)
                pool.wait_ge(const_loaded, 32)
                gain(0)
                gain(1)
                for G in range(NGR):
                    def body(c, u):
                        for e in range(2):
                            n = NM * G + 2 * c + e
                            if not (isinstance(n, int) and n == 0):
                                pool.wait_ge(hid_lo_ready, n)
                            pool.wait_ge(relu_ready, n + 1)
                            pool.tensor_tensor(square[:, :], relu[:, :], relu[:, :], ALU.mult).then_inc(square_ready, 1)
                            if not (isinstance(n, int) and n + 2 >= NM * NGR):
                                gain(n + 2)

                    chunk_steps(pool, body, 4)

            @block.scalar
            def _(act):
                def split_w1(n, slot):
                    act.wait_ge(w1_gained, n + 1)
                    if not (isinstance(n, int) and n < 2):
                        act.wait_ge(pre_ready, n - 1)
                    act.activation(w1_hi[:, slot], w1_raw[:, :, :], ACT.Copy).then_inc(w1_hi_ready, 1)

                act.preload_act_table_set("natural_log_exp_and_others")
                split_w1(0, 0)
                split_w1(1, 1)
                act.wait_ge(eps_set, 1)
                for G in range(NGR):
                    def body(c, u):
                        for e in range(2):
                            n = NM * G + 2 * c + e
                            act.wait_ge(w2_loaded, 16 * n + 16)
                            if not (isinstance(n, int) and n < 4):
                                act.wait_ge(part_ready, TG * (NC * G + c - 1))
                            act.activation(w2_hi[:, 2 * u + e], w2_raw[:, :], ACT.Copy).then_inc(w2_hi_ready, 1)
                            act.wait_ge(pre_ready, n + 1)
                            if not (isinstance(n, int) and n == 0):
                                act.wait_ge(square_ready, n)
                                act.wait_ge(hid_hi_ready, n)
                            act.activation(relu[:, :], ps1[e][:, :], ACT.Relu).then_inc(relu_ready, 1)
                            act.wait_ge(relu_ready, n + 1)
                            act.activation(hid_hi[:, 2 * u + e], relu[:, :], ACT.Square).then_inc(hid_hi_ready, 1)
                            if not (isinstance(n, int) and n + 2 >= NM * NGR):
                                split_w1(n + 2, e)

                    chunk_steps(act, body, 4)
                    for t in range(TG):
                        n = TG * G + t
                        act.wait_ge(part_added, TG * NC * (G + 1) - TG + t + 1)
                        if n:
                            act.wait_ge(post_ready, n)
                        act.activation(relu[:, :], acc[:, t], ACT.Square, accum_out=stat[:, 0:1]).then_inc(stat_step, 1)
                        act.wait_ge(stat_step, 3 * n + 1)
                        act.activation(stat[:, 1:2], stat[:, 0:1], ACT.Ln, bias=eps[:, :], scale=1.0 / D).then_inc(stat_step, 1)
                        act.wait_ge(stat_step, 3 * n + 2)
                        act.activation(stat[:, 2:3], stat[:, 1:2], ACT.Exp, scale=-0.5).then_inc(stat_step, 1)

            @block.vector
            def _(dve):
                def split_w1(n, slot):
                    dve.wait_ge(w1_hi_ready, n + 1)
                    dve.tensor_tensor(w1_lo[:, slot], w1_raw[:, :, :], f32(w1_hi[:, slot]), ALU.subtract).then_inc(w1_lo_ready, 1)

                def add(G, c, t):
                    dve.wait_ge(part_ready, TG * (NC * G + c) + t + 1)
                    if isinstance(c, int) and c == 0:
                        if G:
                            dve.wait_ge(out_stored[t], 16 * G)
                        dve.tensor_copy(acc[:, t], ps2[t % 2][:, :]).then_inc(part_added, 1)
                    else:
                        dve.wait_ge(part_added, TG * (NC * G + c - 1) + t + 1)
                        dve.tensor_tensor(acc[:, t], acc[:, t], ps2[t % 2][:, :], ALU.add).then_inc(part_added, 1)

                split_w1(0, 0)
                split_w1(1, 1)
                dve.wait_ge(const_loaded, 32)
                for G in range(NGR):
                    def body(c, u):
                        for e in range(2):
                            n = NM * G + 2 * c + e
                            dve.wait_ge(w2_hi_ready, n + 1)
                            dve.tensor_tensor(w2_lo[:, 2 * u + e], w2_raw[:, :], f32(w2_hi[:, 2 * u + e]), ALU.subtract).then_inc(w2_lo_ready, 1)
                            adds = [] if isinstance(c, int) and c == 0 else list(range(TG // 2 * e, TG // 2 * (e + 1)))
                            for t in adds[:1]:
                                add(G, c - 1, t)
                            dve.wait_ge(hid_hi_ready, n + 1)
                            dve.wait_ge(square_ready, n + 1)
                            dve.tensor_tensor(hid_lo[:, 2 * u + e], square[:, :], f32(hid_hi[:, 2 * u + e]),
                                              ALU.subtract).then_inc(hid_lo_ready, 1)
                            for t in adds[1:3]:
                                add(G, c - 1, t)
                            if not (isinstance(n, int) and n + 2 >= NM * NGR):
                                split_w1(n + 2, e)
                            for t in adds[3:]:
                                add(G, c - 1, t)

                    chunk_steps(dve, body, 4)
                    add(G, NC - 1, 0)
                    for t in range(TG):
                        if t + 1 < TG:
                            add(G, NC - 1, t + 1)
                        n = TG * G + t
                        dve.wait_ge(stat_step, 3 * n + 3)
                        dve.scalar_tensor_tensor(out=acc[:, t], in0=acc[:, t], scalar=stat[:, 2:3], in1=g_post[:, :],
                                                 op0=ALU.mult, op1=ALU.mult).then_inc(post_ready, 1)
                        dve.wait_ge(h_loaded[n % 2], 16 * (n // 2) + 16)
                        dve.wait_ge(post_ready, n + 1)
                        dve.tensor_tensor(acc[:, t], acc[:, t], h_in[:, n % 2], ALU.add).then_inc(out_ready, 1)

            @block.tensor
            def _(pe):
                def hidden(G, c, e):
                    n = NM * G + 2 * c + e
                    pe.wait_ge(w1_lo_ready, n + 1)
                    if not (isinstance(n, int) and n < 2):
                        pe.wait_ge(relu_ready, n - 1)
                    for half in range(2):
                        cols = slice(512 * half, 512 * half + 512)
                        for k in range(KD):
                            if isinstance(c, int) and c == e == half == 0:
                                pe.wait_ge(u_loaded[k], 32 * (G + 1))
                            for i, (w, a) in enumerate(((w1_hi, u_hi), (w1_hi, u_lo), (w1_lo, u_hi))):
                                m = pe.matmul(ps1[e][:, cols], w[:, e, k], a[:, k, cols],
                                              start=k == 0 and i == 0, stop=k == KD - 1 and i == 2)
                    m.then_inc(pre_ready, 1)

                def part(G, c, u, t):
                    n = TG * (NC * G + c) + t
                    if not (isinstance(n, int) and n < 2):
                        pe.wait_ge(part_added, n - 1)
                    if t == 0:
                        pe.wait_ge(w2_lo_ready, NM * G + 2 * c + 2)
                        pe.wait_ge(hid_lo_ready, NM * G + 2 * c + 2)
                    for half in range(2):
                        cols = slice(512 * half, 512 * half + 512)
                        for e in range(2):
                            for i, (a, w) in enumerate(((hid_hi, w2_hi), (hid_hi, w2_lo), (hid_lo, w2_hi))):
                                m = pe.matmul(ps2[t % 2][:, cols], a[:, 2 * u + e, t * P:(t + 1) * P], w[:, 2 * u + e, cols],
                                              start=e == 0 and i == 0, stop=e == 1 and i == 2)
                    m.then_inc(part_ready, 1)

                for G in range(NGR):
                    def body(c, u):
                        last = isinstance(c, int) and c == NC - 1
                        for e in range(2):
                            hidden(G, c, e)
                            if last and e == 0:
                                continue
                            if not (isinstance(c, int) and c == 0):
                                for t in range(0 if last else TG // 2 * e, TG // 2 * (e + 1)):
                                    part(G, c - 1, 1 - u, t)

                    chunk_steps(pe, body, 4)
                    for t in range(TG):
                        part(G, NC - 1, 1, t)


class Arrays:
    pass


SCRATCH = {
    "qk_hi": (8, P, L), "qk_lo": (8, P, L),
    "c_hi": (P, 4, L), "c_lo": (P, 4, L),
    "v": (L, DA_W), "mv": (L, MLA_H * MLA_V),
    "mq_hi": (MLA_H, P, SEQ), "mq_lo": (MLA_H, P, SEQ),
    "mqr_hi": (2, P, SEQ), "mqr_lo": (2, P, SEQ),
    "mk_hi": (MLA_H, P, L), "mk_lo": (MLA_H, P, L),
    "yT": (8, P, SEQ),
    "u_hi": (P, KD, SEQ), "u_lo": (P, KD, SEQ),
    "h": (SEQ, D),
}


def build(nc, ins, out, stages=7, scratch_aps=None):
    io, scr = Arrays(), Arrays()
    (io.x, io.meta, io.g_attn_pre, io.w_in, io.lam_q1, io.lam_k1, io.lam_q2, io.lam_k2, io.g_da_sub, io.g_mla_q,
     io.w_q_up, io.g_mla_kv, io.w_kv_up, io.w_o, io.g_attn_post, io.g_mlp_pre, io.w_ff1, io.w_ff2, io.g_mlp_post,
     io.ident, io.trig_tm, io.trig_fm, io.bias) = ins
    io.out = out
    a = scratch_aps or {n: nc.dram_tensor(f"scr_{n}", s, F32).ap() for n, s in SCRATCH.items()}
    (scr.qk_hi, scr.qk_lo, scr.c_hi, scr.c_lo, scr.v, scr.mv, scr.mq_hi, scr.mq_lo, scr.mqr_hi, scr.mqr_lo, scr.mk_hi, scr.mk_lo,
     scr.yT, scr.u_hi, scr.u_lo, scr.h) = (a[n] for n in SCRATCH)
    if stages & 1:
        with ExitStack() as ctx:
            mem = Memory(nc, ctx)
            u_hi = mem.sb("u_hi", [P, KD, L], F32R)
            u_lo = mem.sb("u_lo", [P, KD, L], F32R)
            ident = mem.sb("ident", [P, P])
            g_col = mem.sb("g_col", [P, KD])
            eps = mem.sb("eps", [P, 1])
            cv_w = mem.sb("cv_w", [P, KD, CV_W])
            with nc.sbuf_tensor("qk_w_raw", [P, 2, KD, P], F32) as qk_w:
                norm_in(nc, io, u_hi, u_lo, ident, g_col, eps, qk_w)
                qk_proj(nc, io, scr, u_hi, u_lo, g_col, qk_w, cv_w)
            cv_proj(nc, io, scr, u_hi, u_lo, ident, g_col, eps, cv_w)
    if stages & 2:
        mla_up(nc, io, scr)
    if stages & 4:
        attention(nc, io, scr, io.ident, True)
    if stages & 8:
        attention(nc, io, scr, io.ident, False)
    if stages & 16:
        mix_out(nc, io, scr)
    if stages & 32:
        mlp(nc, io, scr)


def constants():
    inv_freq = (1.0 / (np.float32(10000.0) ** (np.arange(0, ROPE, 2, dtype=np.float32) / np.float32(ROPE)))).astype(np.float32)
    ang = np.arange(L, dtype=np.float32)[:, None] * inv_freq[None, :]
    cos, sin = np.cos(ang).astype(np.float32), np.sin(ang).astype(np.float32)
    trig_tm = np.stack([np.concatenate([cos, cos], 1), np.concatenate([-sin, sin], 1)], 1)
    trig_fm = np.ascontiguousarray(np.tile(trig_tm[META:].transpose(2, 1, 0), (2, 1, 1)))
    p, c = np.arange(P)[:, None], np.arange(L)[None, :]
    dist = np.abs(META + p + (NT - 1) * P - c).astype(np.float32)
    seen = (p >= CHUNK) | (c < (NT - 1) * P + META + CHUNK)
    bias = np.zeros((DA_H + 1, P, L), np.float32)
    for h in range(DA_H):
        slope = np.float32(2.0 ** (-8.0 * (h + 1) / DA_H))
        bias[h] = np.where(seen, -slope * dist / np.float32(DA_SCALE), np.float32(NEG))
    bias[DA_H] = np.where(seen, 0.0, NEG)
    return {"ident": np.eye(P, dtype=np.float32), "trig_tm": np.ascontiguousarray(trig_tm), "trig_fm": trig_fm, "bias": bias}


INPUTS = ["x", "meta_tokens", "g_attn_pre", "w_in", "da_lambda_q1", "da_lambda_k1", "da_lambda_q2", "da_lambda_k2", "g_da_sub",
          "g_mla_q", "w_mla_q_up", "g_mla_kv", "w_mla_kv_up", "w_o", "g_attn_post", "g_mlp_pre", "w_ff1", "w_ff2", "g_mlp_post"]


COLUMNS = ("g_attn_pre", "g_da_sub", "g_mla_q", "g_mla_kv", "g_mlp_pre")


def laid_out(inputs):
    arrays = {n: np.ascontiguousarray(inputs[n]) for n in INPUTS}
    for n in COLUMNS:
        arrays[n] = np.ascontiguousarray(arrays[n].reshape(-1, P).T)
    arrays.update(constants())
    return arrays


def kernel(**inputs):
    import concourse.bacc as bacc
    from concourse.bass_utils import run_bass_kernel_spmd

    nc = bacc.Bacc("TRN2", target_bir_lowering=False, num_devices=1)
    arrays = laid_out(inputs)
    ins = [nc.dram_tensor(f"in_{n}", a.shape, mybir.dt.from_np(a.dtype), kind="ExternalInput").ap() for n, a in arrays.items()]
    out = nc.dram_tensor("out", (1, SEQ, D), F32, kind="ExternalOutput").ap()
    build(nc, ins, out, 63)
    r = run_bass_kernel_spmd(nc, [{f"in_{n}": a for n, a in arrays.items()}], core_ids=[0])
    return r.results[0]["out"]
```

```python
import math
from contextlib import ExitStack

import numpy as np
import concourse.bass as bass
from concourse import mybir

F32 = mybir.dt.float32
F32R = mybir.dt.float32r
ALU = mybir.AluOpType
ACT = mybir.ActivationFunctionType
AX = mybir.AxisListType

P = 128
D = 1024
SEQ = 2048
META = 16
L = SEQ + META
CHUNK = 64
NT = SEQ // P
KD = D // P
EPS = 1e-6
NEG = -1e30
LOWEST = -3.0e38
DA_H, DA_HD, DA_V = 4, 64, 128
MLA_H, NOPE, ROPE, MLA_V = 4, 128, 64, 128
QR, KVR = 256, 128
DFF = 4096
DA_W = DA_H * DA_V
C_Q, C_KV, C_R = 3 * DA_W, 3 * DA_W + QR, 3 * DA_W + QR + KVR
IN_W = C_R + ROPE
LAMBDA_INIT = 0.8 - 0.6 * math.exp(-0.0)
DA_SCALE = DA_HD ** -0.5
MLA_SCALE = (NOPE + ROPE) ** -0.5
TOK_CHUNKS = [(0, META)] + [(META + 512 * i, 512) for i in range(SEQ // 512)]
EVEN_CHUNKS = [(c, min(416, L - c)) for c in range(0, L, 416)]
TILES = [(0, META)] + [(META + P * i, P) for i in range(NT)]
ds = bass.ds


def f32(ap):
    return ap.bitcast(F32)


def hold(engine, sem, value):
    engine.wait_ge(sem, value)
    engine.nop(nofuse=True)


def flat(ap):
    return ap.rearrange("a p n -> p (a n)")


class Memory:

    def __init__(self, nc, ctx):
        self.nc, self.ctx, self.sems = nc, ctx, []
        ctx.callback(self.clear)

    def clear(self):
        if self.sems:
            self.nc.clear_and_free_semaphores(self.sems)
            self.nc.all_engine_barrier()

    def sb(self, name, shape, dt=F32):
        return self.ctx.enter_context(self.nc.sbuf_tensor(name, shape, dt))

    def ps(self, name, cols=512):
        return self.ctx.enter_context(self.nc.psum_tensor(name, [P, cols], F32))

    def sem(self, name):
        self.sems.append(self.nc.alloc_semaphore(name))
        return self.sems[-1]


def w_in_rows(io):
    return io.w_in.rearrange("a (k p) n -> p (a k) n", p=P)


def norm_in(nc, io, u_hi, u_lo, ident, g_col, eps, w_first):
    with ExitStack() as ctx:
        mem = Memory(nc, ctx)
        NX = 4
        xt = mem.sb("ni_xt", [P, NX, D])
        xn = mem.sb("ni_xn", [P, 2, D])
        junk = mem.sb("ni_junk", [P, D])
        ssq = mem.sb("ni_ssq", [P, NX])
        std = mem.sb("ni_std", [P, NX])
        rstd = mem.sb("ni_rstd", [P, NX])
        pt = [mem.ps(f"ni_pt{i}", D) for i in range(2)]
        const_loaded, eps_ready, w_loaded = (mem.sem(f"ni_{s}") for s in ("const_loaded", "eps_ready", "w_loaded"))
        x_loaded = [mem.sem(f"ni_x_loaded{v}") for v in range(NX)]
        ssq_ready, std_ready, rstd_ready = (mem.sem(f"ni_{s}_ready") for s in ("ssq", "std", "rstd"))
        xn_ready, xT_ready = mem.sem("ni_xn_ready"), mem.sem("ni_xT_ready")
        hi_ready, lo_ready = mem.sem("ni_hi_ready"), mem.sem("ni_lo_ready")

        def turned(u, rows):
            return pt[u][:, :].rearrange("p (k t) -> p k t", k=KD)[:, :, 0:rows]

        with nc.Block() as block:
            @block.sync
            def _(sp):
                sp.dma_start(xt[0:META, 0, :], io.meta).then_inc(x_loaded[0], 16)
                sp.dma_start(xt[:, 1, :], io.x[0, 0:P, :]).then_inc(x_loaded[1], 16)
                sp.dma_start(ident[:, :], io.ident).then_inc(const_loaded, 16)
                sp.dma_start(g_col[:, :], io.g_attn_pre).then_inc(const_loaded, 16)

                def load(n, v):
                    sp.wait_ge(xn_ready, n - NX + 1)
                    sp.dma_start(xt[:, v, :], flat(io.x[:, ds((n - 1) * P, P), :])).then_inc(x_loaded[v], 16)

                for v in range(2, NX):
                    sp.dma_start(xt[:, v, :], io.x[0, (v - 1) * P:v * P, :]).then_inc(x_loaded[v], 16)
                for u in range(2):
                    sp.dma_start(w_first[:, u], w_in_rows(io)[:, :, u * P:(u + 1) * P]).then_inc(w_loaded, 16)
                with sp.Fori(0, NT // NX - 1) as j:
                    for v in range(NX):
                        load(NX * j + NX + v, v)
                load(NT, 0)
                sp.wait_ge(const_loaded, 32)

            @block.gpsimd
            def _(pool):
                pool.memset(eps[:, :], EPS).then_inc(eps_ready, 1)
                pool.wait_ge(const_loaded, 32)
                pool.wait_ge(w_loaded, 32)
                for u in range(2):
                    pool.tensor_tensor(w_first[:, u], w_first[:, u], g_col[:, :].unsqueeze(2).broadcast_to([P, KD, P]), ALU.mult)

            @block.scalar
            def _(act):
                def stats(n, v, nth, rows):
                    act.wait_ge(x_loaded[v], 16 * nth + 16)
                    act.activation(junk[0:rows, :], xt[0:rows, v, :], ACT.Square,
                                   accum_out=ssq[0:rows, v:v + 1]).then_inc(ssq_ready, 1)

                def root(n, v, rows):
                    act.wait_ge(ssq_ready, n + 1)
                    act.activation(std[0:rows, v:v + 1], ssq[0:rows, v:v + 1], ACT.Sqrt,
                                   bias=eps[0:rows, :], scale=1.0 / D).then_inc(std_ready, 1)

                def high(n, u, rows, col):
                    act.wait_ge(xT_ready, n + 1)
                    act.activation(u_hi[:, :, ds(col, rows)], turned(u, rows), ACT.Copy).then_inc(hi_ready, 1)

                act.wait_ge(eps_ready, 1)
                def high_of(n):
                    high(n, n % 2, TILES[n][1], TILES[n][0])

                for n in range(NX):
                    stats(n, n, 0, TILES[n][1])
                    root(n, n, TILES[n][1])
                    if n >= 2:
                        high_of(n - 2)
                with act.Fori(0, NT // NX - 1) as j:
                    for v in range(NX):
                        n = NX * j + NX + v
                        stats(n, v, j + 1, P)
                        root(n, v, P)
                        high(n - 2, v % 2, P, META + (n - 3) * P)
                stats(NT, 0, NT // NX, P)
                root(NT, 0, P)
                for n in range(NT - 2, NT + 1):
                    high_of(n)

            @block.vector
            def _(dve):
                def scale(n, v, rows, first):
                    u = v % 2
                    dve.wait_ge(std_ready, n + 1)
                    dve.reciprocal(rstd[0:rows, v:v + 1], std[0:rows, v:v + 1]).then_inc(rstd_ready, 1)
                    if not first:
                        dve.wait_ge(xT_ready, n - 1)
                    dve.wait_ge(rstd_ready, n + 1)
                    dve.tensor_scalar(xn[0:rows, u, :], xt[0:rows, v, :], rstd[0:rows, v:v + 1], None,
                                      ALU.mult).then_inc(xn_ready, 1)

                def low(n, u, rows, col):
                    dve.wait_ge(hi_ready, n + 1)
                    dve.tensor_tensor(u_lo[:, :, ds(col, rows)], turned(u, rows), f32(u_hi[:, :, ds(col, rows)]),
                                      ALU.subtract).then_inc(lo_ready, 1)

                def low_of(n):
                    low(n, n % 2, TILES[n][1], TILES[n][0])

                for n in range(NX):
                    scale(n, n, TILES[n][1], n < 2)
                    if n >= 2:
                        low_of(n - 2)
                with dve.Fori(0, NT // NX - 1) as j:
                    for v in range(NX):
                        n = NX * j + NX + v
                        scale(n, v, P, False)
                        low(n - 2, v % 2, P, META + (n - 3) * P)
                scale(NT, 0, P, False)
                for n in range(NT - 2, NT + 1):
                    low_of(n)

            @block.tensor
            def _(pe):
                def turn(n, u, rows, first):
                    pe.wait_ge(xn_ready, n + 1)
                    if not first:
                        pe.wait_ge(lo_ready, n - 1)
                    for k in range(KD):
                        t = pe.transpose(pt[u][:, k * P:k * P + rows], xn[0:rows, u, k * P:(k + 1) * P],
                                         ident[0:rows, 0:rows])
                    t.then_inc(xT_ready, 1)

                pe.wait_ge(const_loaded, 32)
                turn(0, 0, META, True)
                turn(1, 1, P, True)
                with pe.Fori(0, NT // 2 - 1) as j:
                    turn(2 * j + 2, 0, P, False)
                    turn(2 * j + 3, 1, P, False)
                turn(NT, 0, P, False)


def qk_proj(nc, io, scr, u_hi, u_lo, g_col, w_raw, cv_w):
    NM, NQ = 2 * DA_W // P, len(EVEN_CHUNKS)
    with ExitStack() as ctx:
        mem = Memory(nc, ctx)
        w_hi = mem.sb("qk_w_hi", [P, 2, KD, P], F32R)
        w_lo = mem.sb("qk_w_lo", [P, 2, KD, P], F32R)
        o_hi = mem.sb("qk_o_hi", [P, L], F32R)
        o_lo = mem.sb("qk_o_lo", [P, L], F32R)
        ps = [mem.ps(f"qk_ps{q}") for q in range(NQ)]
        w_loaded = [mem.sem(f"qk_w_loaded{u}") for u in range(2)]
        w_gained, w_hi_ready, w_lo_ready = (mem.sem(f"qk_w_{s}") for s in ("gained", "hi_ready", "lo_ready"))
        sums_ready, hi_ready, lo_ready = (mem.sem(f"qk_{s}_ready") for s in ("sums", "hi", "lo"))
        stored = [mem.sem(f"qk_stored{q}") for q in range(NQ)]
        cv_loaded = mem.sem("qk_cv_loaded")
        w_v = w_in_rows(io)

        with nc.Block() as block:
            @block.sync
            def _(sp):
                def store(m):
                    for q, (c0, n) in enumerate(EVEN_CHUNKS):
                        sp.wait_ge(lo_ready, NQ * m + q + 1)
                        for src, dst in ((o_hi, scr.qk_hi), (o_lo, scr.qk_lo)):
                            sp.dma_start(flat(dst[ds(m, 1), :, c0:c0 + n]), f32(src[:, c0:c0 + n])).then_inc(stored[q], 16)

                for at, c0, n in CV_COLS[0]:
                    sp.dma_start(cv_w[:, :, at:at + n], w_v[:, :, c0:c0 + n]).then_inc(cv_loaded, 16)
                with sp.Fori(0, NM // 2 - 1) as j:
                    for u in range(2):
                        sp.wait_ge(w_lo_ready, 2 * j + u + 1)
                        sp.dma_start(w_raw[:, u], w_v[:, :, ds((2 * j + u + 2) * P, P)]).then_inc(w_loaded[u], 16)
                        store(2 * j + u)
                store(NM - 2)
                store(NM - 1)
                for q in range(NQ):
                    sp.wait_ge(stored[q], 32 * NM)

            @block.gpsimd
            def _(pool):
                with pool.Fori(0, NM // 2 - 1) as j:
                    for u in range(2):
                        pool.wait_ge(w_loaded[u], 16 * j + 16)
                        pool.tensor_tensor(w_raw[:, u], w_raw[:, u], g_col[:, :].unsqueeze(2).broadcast_to([P, KD, P]),
                                           ALU.mult).then_inc(w_gained, 1)
                pool.wait_ge(cv_loaded, 16 * len(CV_COLS[0]))
                pool.tensor_tensor(cv_w[:, :, :], cv_w[:, :, :], g_col[:, :].unsqueeze(2).broadcast_to([P, KD, CV_W]), ALU.mult)

            @block.scalar
            def _(act):
                def split(m, u, first):
                    if not first:
                        act.wait_ge(w_gained, m - 1)
                        act.wait_ge(sums_ready, NQ * (m - 1))
                    act.activation(w_hi[:, u], w_raw[:, u], ACT.Copy).then_inc(w_hi_ready, 1)

                def high(m, first):
                    for q, (c0, n) in enumerate(EVEN_CHUNKS):
                        act.wait_ge(sums_ready, NQ * m + q + 1)
                        if not first:
                            act.wait_ge(stored[q], 32 * m)
                        act.activation(o_hi[:, c0:c0 + n], ps[q][:, 0:n], ACT.Copy).then_inc(hi_ready, 1)

                split(0, 0, True)
                split(1, 1, True)
                high(0, True)
                split(2, 0, False)
                high(1, False)
                with act.Fori(0, NM // 2 - 2) as j:
                    split(2 * j + 3, 1, False)
                    high(2 * j + 2, False)
                    split(2 * j + 4, 0, False)
                    high(2 * j + 3, False)
                split(NM - 1, 1, False)
                high(NM - 2, False)
                high(NM - 1, False)

            @block.vector
            def _(dve):
                def split(m, u):
                    dve.wait_ge(w_hi_ready, m + 1)
                    dve.tensor_tensor(w_lo[:, u], w_raw[:, u], f32(w_hi[:, u]), ALU.subtract).then_inc(w_lo_ready, 1)

                def low(m):
                    for q, (c0, n) in enumerate(EVEN_CHUNKS):
                        dve.wait_ge(hi_ready, NQ * m + q + 1)
                        dve.tensor_tensor(o_lo[:, c0:c0 + n], ps[q][:, 0:n], f32(o_hi[:, c0:c0 + n]),
                                          ALU.subtract).then_inc(lo_ready, 1)

                split(0, 0)
                split(1, 1)
                low(0)
                split(2, 0)
                low(1)
                with dve.Fori(0, NM // 2 - 2) as j:
                    split(2 * j + 3, 1)
                    low(2 * j + 2)
                    split(2 * j + 4, 0)
                    low(2 * j + 3)
                split(NM - 1, 1)
                low(NM - 2)
                low(NM - 1)

            @block.tensor
            def _(pe):
                def product(m, u, first):
                    pe.wait_ge(w_lo_ready, m + 1)
                    for q, (c0, n) in enumerate(EVEN_CHUNKS):
                        if not first:
                            pe.wait_ge(lo_ready, NQ * (m - 1) + q + 1)
                        for k in range(KD):
                            for i, (w, a) in enumerate(((w_hi, u_hi), (w_hi, u_lo), (w_lo, u_hi))):
                                t = pe.matmul(ps[q][:, 0:n], w[:, u, k], a[:, k, c0:c0 + n],
                                              start=(k == 0 and i == 0), stop=(k == KD - 1 and i == 2))
                        t.then_inc(sums_ready, 1)

                product(0, 0, True)
                product(1, 1, False)
                with pe.Fori(0, NM // 2 - 1) as j:
                    product(2 * j + 2, 0, False)
                    product(2 * j + 3, 1, False)


CV_W = 512
CV_COLS = [[(0, C_Q, QR + KVR + ROPE), (QR + KVR + ROPE, C_R + ROPE // 2, ROPE // 2), (QR + KVR + ROPE + ROPE // 2, C_R, ROPE // 2)],
           [(0, 2 * DA_W, DA_W)]]


def cv_proj(nc, io, scr, u_hi, u_lo, ident, g_col, eps, cv_w):
    W = CV_W
    NP = 4
    with ExitStack() as ctx:
        mem = Memory(nc, ctx)
        w_hi = mem.sb("cv_w_hi", [P, KD, W], F32R)
        w_lo = mem.sb("cv_w_lo", [P, KD, W], F32R)
        trig = mem.sb("cv_trig", [P, 2, 2, ROPE])
        cn = mem.sb("cv_cn", [P, 2, W])
        tmp = mem.sb("cv_tmp", [P, 2, 2, ROPE])
        junk = mem.sb("cv_junk", [P, QR])
        ssq = mem.sb("cv_ssq", [P, 2, 2])
        std = mem.sb("cv_std", [P, 2, 2])
        rstd = mem.sb("cv_rstd", [P, 2, 2])
        o_hi = mem.sb("cv_o_hi", [P, 2, W], F32R)
        o_lo = mem.sb("cv_o_lo", [P, 2, W], F32R)
        v_out = mem.sb("cv_v_out", [P, 2, W])
        v_copied = mem.sem("cv_v_copied")
        v_stored = [mem.sem(f"cv_v_stored{u}") for u in range(2)]
        ps = [mem.ps(f"cv_ps{i}") for i in range(2)]
        pt = [mem.ps(f"cv_pt{i}") for i in range(2)]
        w_loaded, w_gained, w_hi_ready, w_lo_ready = (mem.sem(f"cv_w_{s}") for s in ("loaded", "gained", "hi_ready", "lo_ready"))
        trig_loaded = [mem.sem(f"cv_trig_loaded{u}") for u in range(2)]
        sums_ready, ssq_ready, root_ready, rstd_ready = (mem.sem(f"cv_{s}_ready") for s in ("sums", "ssq", "root", "rstd"))
        rot_ready, cn_ready, cT_ready = (mem.sem(f"cv_{s}_ready") for s in ("rot", "cn", "cT"))
        hi_ready, lo_ready = mem.sem("cv_hi_ready"), mem.sem("cv_lo_ready")
        stored = [mem.sem(f"cv_stored{u}") for u in range(2)]
        N = len(TILES)
        KP = KD // NP

        with nc.Block() as block:
            @block.sync
            def _(sp):
                def load_trig(n):
                    r0, rows = TILES[n]
                    if n >= 2:
                        sp.wait_ge(rot_ready, 2 * (n - 1))
                    sp.dma_start(trig[0:rows, n % 2], io.trig_tm[r0:r0 + rows]).then_inc(trig_loaded[n % 2], 16)

                load_trig(0)
                load_trig(1)
                sp.wait_ge(w_lo_ready, NP)
                for at, c0, n in CV_COLS[1]:
                    sp.dma_start(cv_w[:, :, at:at + n], w_in_rows(io)[:, :, c0:c0 + n]).then_inc(w_loaded, 16)
                for n, (r0, rows) in enumerate(TILES):
                    sp.wait_ge(lo_ready, n + 1)
                    for src, dst in ((o_hi, scr.c_hi), (o_lo, scr.c_lo)):
                        sp.dma_start(dst[:, :, r0:r0 + rows], f32(src[:, n % 2]).rearrange("p (f t) -> p f t", f=4)[:, :, 0:rows]).then_inc(stored[n % 2], 16)
                    if n + 2 < N:
                        load_trig(n + 2)
                for n, (r0, rows) in enumerate(TILES):
                    sp.wait_ge(v_copied, n + 1)
                    sp.dma_start(scr.v[r0:r0 + rows, :], v_out[0:rows, n % 2]).then_inc(v_stored[n % 2], 16)
                for u in range(2):
                    sp.wait_ge(stored[u], 32 * len(range(u, N, 2)))
                    sp.wait_ge(v_stored[u], 16 * len(range(u, N, 2)))

            @block.gpsimd
            def _(pool):
                pool.wait_ge(w_loaded, 16 * len(CV_COLS[1]))
                pool.tensor_tensor(cv_w[:, :, :], cv_w[:, :, :], g_col[:, :].unsqueeze(2).broadcast_to([P, KD, W]), ALU.mult).then_inc(w_gained, 1)

            @block.scalar
            def _(act):
                def split(g):
                    if g >= NP:
                        act.wait_ge(w_gained, 1)
                        act.wait_ge(sums_ready, N)
                    q = g % NP
                    act.activation(w_hi[:, q * KP:(q + 1) * KP], cv_w[:, q * KP:(q + 1) * KP], ACT.Copy).then_inc(w_hi_ready, 1)

                def stats(n):
                    rows = TILES[n][1]
                    act.wait_ge(sums_ready, n + 1)
                    act.activation(junk[0:rows, 0:QR], ps[n % 2][0:rows, 0:QR], ACT.Square,
                                   accum_out=ssq[0:rows, n % 2, 0:1]).then_inc(ssq_ready, 1)
                    act.wait_ge(ssq_ready, 2 * n + 1)
                    act.activation(junk[0:rows, 0:KVR], ps[n % 2][0:rows, QR:QR + KVR], ACT.Square,
                                   accum_out=ssq[0:rows, n % 2, 1:2]).then_inc(ssq_ready, 1)
                    act.wait_ge(ssq_ready, 2 * n + 2)
                    act.activation(std[0:rows, n % 2, 0:1], ssq[0:rows, n % 2, 0:1], ACT.Sqrt,
                                   bias=eps[0:rows, :], scale=1.0 / QR)
                    act.activation(std[0:rows, n % 2, 1:2], ssq[0:rows, n % 2, 1:2], ACT.Sqrt,
                                   bias=eps[0:rows, :], scale=1.0 / KVR).then_inc(root_ready, 1)

                def high(n):
                    rows = TILES[n][1]
                    act.wait_ge(cT_ready, n + 1)
                    if n >= 2:
                        act.wait_ge(stored[n % 2], 32 * (n // 2))
                    act.activation(o_hi[:, n % 2].rearrange("p (f t) -> p f t", f=4)[:, :, 0:rows],
                                   pt[n % 2][:, :].rearrange("p (f t) -> p f t", f=4)[:, :, 0:rows],
                                   ACT.Copy).then_inc(hi_ready, 1)

                for g in range(NP):
                    split(g)
                for n in range(N):
                    stats(n)
                    if n:
                        high(n - 1)
                high(N - 1)
                for g in range(NP, 2 * NP):
                    split(g)
                for n in range(N):
                    m, rows = N + n, TILES[n][1]
                    act.wait_ge(sums_ready, m + 1)
                    if n >= 2:
                        act.wait_ge(v_stored[n % 2], 16 * (n // 2))
                    act.activation(v_out[0:rows, n % 2], ps[m % 2][0:rows, :], ACT.Copy).then_inc(v_copied, 1)

            @block.vector
            def _(dve):
                def split(g):
                    q = g % NP
                    dve.wait_ge(w_hi_ready, g + 1)
                    dve.tensor_tensor(w_lo[:, q * KP:(q + 1) * KP], cv_w[:, q * KP:(q + 1) * KP], f32(w_hi[:, q * KP:(q + 1) * KP]),
                                      ALU.subtract).then_inc(w_lo_ready, 1)

                def normalise(n):
                    u, rows = n % 2, TILES[n][1]
                    kr, swapped = QR + KVR, QR + KVR + ROPE
                    dve.wait_ge(trig_loaded[u], 16 * (n // 2) + 16)
                    dve.wait_ge(ssq_ready, 2 * n + 2)
                    dve.tensor_tensor(tmp[0:rows, u, 0], ps[u][0:rows, kr:kr + ROPE], trig[0:rows, u, 0], ALU.mult).then_inc(rot_ready, 1)
                    dve.tensor_tensor(tmp[0:rows, u, 1], ps[u][0:rows, swapped:swapped + ROPE], trig[0:rows, u, 1],
                                      ALU.mult).then_inc(rot_ready, 1)
                    dve.wait_ge(root_ready, n + 1)
                    dve.reciprocal(rstd[0:rows, u], std[0:rows, u]).then_inc(rstd_ready, 1)
                    dve.wait_ge(rot_ready, 2 * n + 2)
                    if n >= 2:
                        dve.wait_ge(cT_ready, n - 1)
                    dve.tensor_tensor(cn[0:rows, u, kr:kr + ROPE], tmp[0:rows, u, 0], tmp[0:rows, u, 1], ALU.add)
                    dve.tensor_tensor(cn[0:rows, u, swapped:swapped + ROPE], tmp[0:rows, u, 0], tmp[0:rows, u, 1], ALU.add)
                    dve.wait_ge(rstd_ready, n + 1)
                    dve.tensor_scalar(cn[0:rows, u, 0:QR], ps[u][0:rows, 0:QR], rstd[0:rows, u, 0:1], None, ALU.mult)
                    dve.tensor_scalar(cn[0:rows, u, QR:kr], ps[u][0:rows, QR:kr], rstd[0:rows, u, 1:2], None,
                                      ALU.mult).then_inc(cn_ready, 1)

                def low(m, bank):
                    rows = TILES[m][1]
                    o, h, s = (a.rearrange("p (f t) -> p f t", f=4)[:, :, 0:rows]
                               for a in (o_lo[:, m % 2], f32(o_hi[:, m % 2]), bank[:, :]))
                    dve.wait_ge(hi_ready, m + 1)
                    dve.tensor_tensor(o, s, h, ALU.subtract).then_inc(lo_ready, 1)

                for g in range(NP):
                    split(g)
                for n in range(N):
                    normalise(n)
                    if n:
                        low(n - 1, pt[(n - 1) % 2])
                low(N - 1, pt[(N - 1) % 2])
                for g in range(NP, 2 * NP):
                    split(g)

            @block.tensor
            def _(pe):
                def product(m):
                    c0, rows = TILES[m % N]
                    if m >= N + 2:
                        pe.wait_ge(v_copied, m - 1 - N)
                    elif m >= 2:
                        pe.wait_ge(cn_ready, m - 1)
                    for k in range(KD):
                        if m % N == 0 and k % KP == 0:
                            pe.wait_ge(w_lo_ready, NP * (m // N) + k // KP + 1)
                        for i, (a, w) in enumerate(((u_hi, w_hi), (u_hi, w_lo), (u_lo, w_hi))):
                            t = pe.matmul(ps[m % 2][0:rows, :], a[:, k, c0:c0 + rows], w[:, k],
                                          start=(k == 0 and i == 0), stop=(k == KD - 1 and i == 2))
                    t.then_inc(sums_ready, 1)

                def turn(n):
                    rows = TILES[n][1]
                    pe.wait_ge(cn_ready, n + 1)
                    if n >= 2:
                        pe.wait_ge(lo_ready, n - 1)
                    for f in range(4):
                        t = pe.transpose(pt[n % 2][:, f * P:f * P + rows], cn[0:rows, n % 2, f * P:(f + 1) * P],
                                         ident[0:rows, 0:rows])
                    t.then_inc(cT_ready, 1)

                for n in range(N):
                    product(n)
                    if n:
                        turn(n - 1)
                turn(N - 1)
                for n in range(N):
                    product(N + n)


def mla_up(nc, io, scr):
    NQF, NR = MLA_H * NOPE, MLA_H * ROPE
    WQ = NQF + 2 * NR
    WKV = MLA_H * (NOPE + MLA_V)
    KQ = QR // P
    HALF = ROPE // 2
    PIECES = [(0, META + 512)] + [(META + 512 * q, 512) for q in range(1, SEQ // 512)]
    with ExitStack() as ctx:
        mem = Memory(nc, ctx)
        c_hi = mem.sb("mu_c_hi", [P, KQ + 1, L], F32R)
        c_lo = mem.sb("mu_c_lo", [P, KQ + 1, L], F32R)
        w_raw = mem.sb("mu_w_raw", [P, KQ * WQ + WKV])
        w_hi = mem.sb("mu_w_hi", [P, KQ * WQ + WKV], F32R)
        w_lo = mem.sb("mu_w_lo", [P, KQ * WQ + WKV], F32R)
        g_q = mem.sb("mu_g_q", [P, KQ])
        g_kv = mem.sb("mu_g_kv", [P, 1])
        trig = mem.sb("mu_trig", [P, 2, SEQ])
        rot = mem.sb("mu_rot", [P, 2, 2, 512])
        NS = 8
        out = mem.sb("mu_out", [P, NS, 512])
        NB = 8
        ps = [mem.ps(f"mu_ps{i}") for i in range(NB)]
        q_w_loaded, kv_w_loaded = mem.sem("mu_q_w_loaded"), mem.sem("mu_kv_w_loaded")
        c_loaded = [mem.sem(f"mu_c_loaded{q}") for q in range(len(PIECES))]
        trig_loaded = [mem.sem(f"mu_trig_loaded{q}") for q in range(len(PIECES))]
        w_gained, w_hi_ready, w_lo_ready = (mem.sem(f"mu_w_{s}") for s in ("gained", "hi_ready", "lo_ready"))
        sums_ready, rot_ready = mem.sem("mu_sums_ready"), mem.sem("mu_rot_ready")
        taken = {who: mem.sem(f"mu_taken_by_{who}") for who in ("act", "dve", "pool")}
        stored = [mem.sem(f"mu_stored{u}") for u in range(NS)]
        q_w = [w[:, 0:KQ * WQ].rearrange("p (k n) -> p k n", k=KQ) for w in (w_raw, w_hi, w_lo)]
        kv_w = [w[:, KQ * WQ:KQ * WQ + WKV] for w in (w_raw, w_hi, w_lo)]

        jobs = []
        for piece, (p0, pn) in enumerate(PIECES):
            queries = (max(p0, META), pn - (META if p0 == 0 else 0))
            for t in TOK_CHUNKS:
                if p0 <= t[0] < p0 + pn:
                    jobs += [(piece, "k", h * NOPE, t, scr.mk[h]) for h in range(MLA_H)]
            jobs += [(piece, "v", MLA_H * NOPE, t, scr.mv) for t in TILES if p0 <= t[0] < p0 + pn]
            jobs += [(piece, "rope", NQF + p * P, queries, scr.mqr[p]) for p in range(NR // P)]
            jobs += [(piece, "q", h * NOPE, queries, scr.mq[h]) for h in range(MLA_H)]
        Q_AT = 8
        takers, taken_by = [], []
        for _, kind, *_ in jobs:
            others = sum(who != "pool" for who in takers)
            takers.append("pool" if kind == "rope" else ("act", "dve")[others % 2])
            taken_by.append(sum(who == takers[-1] for who in takers))
        bank, first_banks, ropes = 0, [], []
        for _, kind, *_ in jobs:
            first_banks.append(bank)
            ropes.append(sum(b == "rope" for _, b, *_ in jobs[:len(ropes)]))
            bank += 2 if kind == "rope" else 1

        def size(job):
            _, kind, _, (c0, n), _ = job
            return (n, 512) if kind == "v" else (P, n)

        def before(last):
            return max((i for i, b in enumerate(first_banks) for w in range(2 if jobs[i][1] == "rope" else 1)
                        if b + w <= last - NB), default=None)

        def take(engine, who, i):
            if i >= NS:
                engine.wait_ge(stored[i % NS], 16 * (i // NS))
            if who != "pool":
                engine.wait_ge(sums_ready, i + 1)
            rows, cols = size(jobs[i])
            return out[0:rows, i % NS, 0:cols], ps[first_banks[i] % NB][0:rows, 0:cols]

        with nc.Block() as block:
            @block.sync
            def _(sp):
                def load_piece(q):
                    c0, n = PIECES[q]
                    for src, dst in ((scr.c_hi, c_hi), (scr.c_lo, c_lo)):
                        sp.dma_start(f32(dst[:, :, c0:c0 + n]), src[:, 0:KQ + 1, c0:c0 + n]).then_inc(c_loaded[q], 16)

                def load_trig(q):
                    c0, n = PIECES[q]
                    t0, t1 = max(c0, META) - META, c0 + n - META
                    sp.dma_start(trig[:, :, t0:t1], io.trig_fm[:, :, t0:t1]).then_inc(trig_loaded[q], 16)

                src = io.w_kv_up[0].rearrange("p (h n) -> p h n", h=MLA_H)
                for part in range(2):
                    sp.dma_start(kv_w[0][:, part * 512:(part + 1) * 512].rearrange("p (h n) -> p h n", h=MLA_H),
                                 src[:, :, part * NOPE:part * NOPE + 128]).then_inc(kv_w_loaded, 16)
                sp.dma_start(g_kv[:, :], io.g_mla_kv).then_inc(kv_w_loaded, 16)
                load_piece(0)
                for k in range(KQ):
                    src = io.w_q_up[0, k * P:(k + 1) * P, :].rearrange("p (h n) -> p h n", h=MLA_H)
                    to = q_w[0][:, k]
                    swapped = to[:, NQF + NR:WQ].rearrange("p (h n) -> p h n", h=MLA_H)
                    for dst, part in ((to[:, 0:NQF].rearrange("p (h n) -> p h n", h=MLA_H), src[:, :, 0:NOPE]),
                                      (to[:, NQF:NQF + NR].rearrange("p (h n) -> p h n", h=MLA_H), src[:, :, NOPE:NOPE + ROPE]),
                                      (swapped[:, :, 0:HALF], src[:, :, NOPE + HALF:NOPE + ROPE]),
                                      (swapped[:, :, HALF:ROPE], src[:, :, NOPE:NOPE + HALF])):
                        sp.dma_start(dst, part).then_inc(q_w_loaded, 16)
                sp.dma_start(g_q[:, :], io.g_mla_q).then_inc(q_w_loaded, 16)
                load_trig(0)
                for i, (piece, kind, _, (c0, n), dst) in enumerate(jobs):
                    if (i == 0 or jobs[i - 1][0] != piece) and piece + 1 < len(PIECES):
                        load_piece(piece + 1)
                        load_trig(piece + 1)
                    rows, cols = size(jobs[i])
                    if kind == "v":
                        dst = dst[c0:c0 + n, :]
                    elif kind == "k":
                        dst = dst[:, c0:c0 + n]
                    else:
                        dst = dst[:, c0 - META:c0 - META + n]
                    sp.wait_ge(taken[takers[i]], taken_by[i])
                    sp.dma_start(dst, out[0:rows, i % NS, 0:cols]).then_inc(stored[i % NS], 16)
                for u in range(NS):
                    sp.wait_ge(stored[u], 16 * len(jobs[u::NS]))

            @block.gpsimd
            def _(pool):
                pool.wait_ge(kv_w_loaded, 16 * 3)
                pool.tensor_scalar(kv_w[0], kv_w[0], g_kv[:, :], 1.0, ALU.mult, ALU.mult).then_inc(w_gained, 1)
                pool.wait_ge(q_w_loaded, 16 * (4 * KQ + 1))
                for k in range(KQ):
                    pool.tensor_scalar(q_w[0][:, k], q_w[0][:, k], g_q[:, k:k + 1], 1.0, ALU.mult, ALU.mult).then_inc(w_gained, 1)
                for i in range(len(jobs)):
                    if takers[i] == "pool":
                        r = ropes[i]
                        dst, _ = take(pool, "pool", i)
                        pool.wait_ge(rot_ready, 2 * r + 2)
                        pool.tensor_tensor(dst, rot[:, r % 2, 0], rot[:, r % 2, 1], ALU.add).then_inc(taken["pool"], 1)

            @block.scalar
            def _(act):
                def split(g):
                    act.wait_ge(w_gained, g + 1)
                    dst, src = (q_w[1][:, g - 1], q_w[0][:, g - 1]) if g else (kv_w[1], kv_w[0])
                    act.activation(dst, src, ACT.Copy).then_inc(w_hi_ready, 1)
                split(0)
                for i in range(len(jobs)):
                    if i == Q_AT:
                        for g in range(1, KQ + 1):
                            split(g)
                    if takers[i] == "act":
                        dst, src = take(act, "act", i)
                        act.activation(dst, src, ACT.Copy).then_inc(taken["act"], 1)

            @block.vector
            def _(dve):
                def split(g):
                    dve.wait_ge(w_hi_ready, g + 1)
                    dst, hi, src = (q_w[2][:, g - 1], q_w[1][:, g - 1], q_w[0][:, g - 1]) if g else (kv_w[2], kv_w[1], kv_w[0])
                    dve.tensor_tensor(dst, src, f32(hi), ALU.subtract).then_inc(w_lo_ready, 1)
                split(0)
                for i, (piece, _, _, (c0, n), _) in enumerate(jobs):
                    if i == Q_AT:
                        for g in range(1, KQ + 1):
                            split(g)
                    if takers[i] == "dve":
                        dst, src = take(dve, "dve", i)
                        dve.tensor_copy(dst, src).then_inc(taken["dve"], 1)
                    elif takers[i] == "pool":
                        r = ropes[i]
                        dve.wait_ge(trig_loaded[piece], 16)
                        dve.wait_ge(sums_ready, i + 1)
                        if r >= 2:
                            dve.wait_ge(taken["pool"], r - 1)
                        for part in range(2):
                            dve.tensor_tensor(rot[:, r % 2, part], ps[(first_banks[i] + part) % NB][:, :],
                                              trig[:, part, c0 - META:c0 - META + n], ALU.mult).then_inc(rot_ready, 1)

            @block.tensor
            def _(pe):
                pe.wait_ge(w_lo_ready, 1)
                for i, (piece, kind, w0, (c0, n), _) in enumerate(jobs):
                    if i == 0 or jobs[i - 1][0] != piece:
                        pe.wait_ge(c_loaded[piece], 32)
                    if kind == "rope":
                        pe.wait_ge(w_lo_ready, KQ + 1)
                    banks = [first_banks[i], first_banks[i] + 1] if kind == "rope" else [first_banks[i]]
                    last = before(banks[-1])
                    for who in taken:
                        count = 0 if last is None else sum(t == who for t in takers[:last + 1])
                        if count:
                            pe.wait_ge(taken[who], count)
                    for part, bank in enumerate(banks):
                        steps = [(k, i3) for k in (range(KQ) if kind in ("q", "rope") else range(1)) for i3 in range(3)]
                        for k, i3 in steps:
                            wi, ci = ((1, c_hi), (1, c_lo), (2, c_hi))[i3]
                            if kind in ("q", "rope"):
                                w = q_w[wi][:, k, w0 + part * NR:w0 + part * NR + P]
                                c = ci[:, k, c0:c0 + n]
                            else:
                                w = kv_w[wi][:, w0:w0 + (512 if kind == "v" else P)]
                                c = ci[:, KQ, c0:c0 + n]
                            first, stop = (k, i3) == steps[0], (k, i3) == steps[-1]
                            if kind == "v":
                                t = pe.matmul(ps[bank % NB][0:n, :], c, w, start=first, stop=stop)
                            else:
                                t = pe.matmul(ps[bank % NB][:, 0:n], w, c, start=first, stop=stop)
                    t.then_inc(sums_ready, 1)


def row_chunks(i):
    width = META + P * (i + 1)
    n = -(-width // 512)
    step = -(-width // n // 4) * 4
    return [(c, min(step, width - c)) for c in range(0, width, step)]


def attention(nc, io, scr, ident, da, work=None):
    name = "da" if da else "ml"
    H = DA_H if da else MLA_H
    COMPS = 2 if da else 1
    NG = NT // 4
    scale = DA_SCALE if da else MLA_SCALE
    NKB = 4 if da else 2
    with ExitStack() as ctx:
        mem = Memory(nc, ctx)
        keys = mem.sb(f"{name}_keys", [P, 2, NKB, L], F32R)
        rope_keys = None if da else mem.sb("ml_rope_keys", [P, 2, L], F32R)
        NQB = 2 if da else 3
        qs = mem.sb(f"{name}_qs", [P, 2, NQB, 512], F32R)
        v = mem.sb(f"{name}_v", [P, NT, P])
        v_meta = mem.sb(f"{name}_v_meta", [META, P])
        bias = mem.sb(f"{name}_bias", [P, 2 if da else 1, L])
        GROUP0_W = META + 512
        rows = [mem.sb(f"{name}_rows{u}", [P, 4, L]) for u in range(2)]
        second = mem.sb(f"{name}_second", [P, 2, L]) if da else None
        NPT = 8
        NTB = 3
        pT = mem.sb(f"{name}_pT", [P, NPT, 512])
        o_out = mem.sb(f"{name}_o_out", [P, 2, 512])
        if not da:
            k_raw = mem.sb("ml_k_raw", [P, L])
            q_raw = mem.sb("ml_q_raw", [P, 2, 2, 512])
        mx = mem.sb(f"{name}_mx", [P, 2, COMPS, 5])
        nmax = mem.sb(f"{name}_nmax", [P, 2, COMPS])
        nmax_all = mem.sb(f"{name}_nmax_all", [P, 5])
        total = mem.sb(f"{name}_total", [P, 2, COMPS])
        inv = mem.sb(f"{name}_inv", [P, 2, COMPS])
        inv2 = mem.sb(f"{name}_inv2", [P, 2])
        lam_in = mem.sb(f"{name}_lam_in", [P, 4, DA_HD])
        lam = mem.sb(f"{name}_lam", [P, 4])
        NSB = 4
        ps_s = [mem.ps(f"{name}_ps_s{i}") for i in range(NSB)]
        ps_t = [mem.ps(f"{name}_ps_t{i}") for i in range(NTB)]
        ps_o = mem.ps(f"{name}_ps_o")
        g_sub = mem.sb(f"{name}_g_sub", [P, 2])
        w_o_loaded, gain_made = mem.sem(f"{name}_w_o_loaded"), mem.sem(f"{name}_gain_made")
        start_loaded = [mem.sem(f"{name}_start_loaded{g}") for g in range(NG)]
        ident_loaded = mem.sem(f"{name}_ident_loaded")
        lam_loaded, lam_step = mem.sem(f"{name}_lam_loaded"), mem.sem(f"{name}_lam_step")
        lam_exp = mem.sem(f"{name}_lam_exp")
        k_raw_loaded, k_hi_ready, k_split = (mem.sem(f"{name}_{s}") for s in ("k_raw_loaded", "k_hi_ready", "k_split"))
        q_hi_ready, q_split = mem.sem(f"{name}_q_hi_ready"), mem.sem(f"{name}_q_split")
        keys_loaded = [mem.sem(f"{name}_keys_loaded{u}") for u in range(2)]
        bias_loaded = [mem.sem(f"{name}_bias_loaded{u}") for u in range(2)]
        q_loaded = [mem.sem(f"{name}_q_loaded{u}") for u in range(2)]
        v_loaded = [mem.sem(f"{name}_v_loaded{g}") for g in range(NG)]
        scores_ready, scores_read = mem.sem(f"{name}_scores_ready"), mem.sem(f"{name}_scores_read")
        max_ready, exp_ready = mem.sem(f"{name}_max_ready"), mem.sem(f"{name}_exp_ready")
        inv_ready, first_scaled, probs_ready = (mem.sem(f"{name}_{s}") for s in ("inv_ready", "first_scaled", "probs_ready"))
        inv2_step = mem.sem(f"{name}_inv2_step")
        pT_ready, pv_done = mem.sem(f"{name}_pT_ready"), mem.sem(f"{name}_pv_done")
        act_copied, dve_copied = mem.sem(f"{name}_act_copied"), mem.sem(f"{name}_dve_copied")
        o_copied = mem.sem(f"{name}_o_copied")
        o_stored = [mem.sem(f"{name}_o_stored{u}") for u in range(2)]

        chunks = [(i, c, k0, n) for i in range(NT) for c in range(COMPS) for k0, n in row_chunks(i)]
        NCH = len(chunks)
        tiles_of = lambda g: 1 + 4 * (g + 1)
        NKT = sum(tiles_of(g) for g in range(NG))
        kt_base = [sum(tiles_of(a) for a in range(g)) for g in range(NG)]
        KEY_LOADS = 4
        START_LOADS = 1 + (KEY_LOADS if da else 3)
        Q_LOADS = 2 if da else 3
        KEY_PIECES = [(0, GROUP0_W)] + [(GROUP0_W + 512 * q, 512) for q in range(NG - 1)]

        def row(i, u):
            g = i // 4
            start = GROUP0_W if g == 1 else 0
            return rows[u ^ (g == 2)][:, i % 4, start:start + META + P * (i + 1)]

        def comp_row(i, c, u):
            return row(i, u) if c == 0 else second[:, i % 2, 0:META + P * (i + 1)]

        def row_steps(carried):
            phases, later = [], list(carried)
            for groups, *_ in PHASES:
                steps = []
                for n, (i, c, k0, w) in enumerate(chunks):
                    if i // 4 not in groups:
                        continue
                    steps += [("chunk", 0, n)] + SPLITS.get(n, [])
                    later = [(left - 1, step) for left, step in later]
                    steps += [step for left, step in later if left <= 0]
                    later = [(left, step) for left, step in later if left > 0]
                    if k0 + w == META + P * (i + 1):
                        steps += [step for _, step in later if step[2] - NT * step[1] < i]
                        later = [(left, step) for left, step in later if step[2] - NT * step[1] >= i]
                        later.append((1, ("exp", 0, i, c)))
                        if c == 0:
                            later.append((SCALE_AFTER, ("scale", 0, i)))
                        if c == COMPS - 1:
                            later.append((END_AFTER, ("end", 0, i)))
                phases.append(steps)
            return phases, [(left, (step[0], 1) + step[2:]) for left, step in later]

        def first_chunk(i):
            return min(n for n, chunk in enumerate(chunks) if chunk[0] == i)

        SPLITS = {}
        if not da:
            SPLITS = {first_chunk(0): [("split_q", 0, 1)], first_chunk(6): [("split_q", 0, 2)],
                      first_chunk(10): [("split_q", 0, 3)], first_chunk(15) + 1: [("split_next_q", 0)]}
            for piece, i in ((1, 2), (2, 5), (3, 9)):
                SPLITS.setdefault(first_chunk(i), []).append(("split_first_keys", 0, piece))
            for piece in range(len(KEY_PIECES)):
                SPLITS.setdefault(first_chunk(12) + 2 + 3 * piece, []).append(("split_next_keys", 0, piece))

        def cost(step):
            if step[0] == "chunk":
                return chunks[step[2]][3] + 60
            return META + P * (step[2] + 1) + 250 if step[0] == "end" and da else 0

        def head_steps():
            steps = []
            for p, rows_part in enumerate(row_steps(row_steps([])[1])[0]):
                _, turned, start, put_off = PHASES[p]
                lead_steps = products_of([(b + (p == 0), g) for b, g in PHASES[p - 1][1]])[-PHASES[p - 1][3]:]
                made, body_steps = products_of(turned), []
                turns = [("turn", b, g, t) for b, g in turned for t in range(tiles_of(g))]
                done = 0
                for at, turn in enumerate(turns):
                    body_steps.append(turn)
                    while done < min(at - 1, (at + 1) * (len(made) - put_off) // len(turns)):
                        body_steps.append(made[done])
                        done += 1
                total, passed = sum(cost(step) for step in rows_part), 0
                n_lead, n_body = len(lead_steps), len(body_steps)
                for at, step in enumerate(rows_part):
                    steps.append(step)
                    passed += cost(step)
                    part = passed / total
                    last = at == len(rows_part) - 1
                    while lead_steps and (last or part > start * (1 - (len(lead_steps) - 1) / n_lead)):
                        steps.append(lead_steps.pop(0))
                    while body_steps and (last or part > start + (1 - start) * (1 - len(body_steps) / n_body)):
                        if lead_steps:
                            break
                        kind, back, g, *t = body_steps[0]
                        if kind == "turn" and t == [0] and any(
                                e[0] == "end" and e[2] - NT * e[1] == 4 * g + 3 - NT * back for e in rows_part[at + 1:]):
                            break
                        steps.append(body_steps.pop(0))
                steps += lead_steps + body_steps
            return steps

        def products_of(groups):
            return [("product" if t < tiles_of(g) else "out", b, g) + ((t,) if t < tiles_of(g) else ())
                    for b, g in groups for t in range(tiles_of(g) + 1)]

        PHASES = (((0, 1), ((1, 3),), 0.2, 7), ((2,), ((0, 0), (0, 1)), 0.15, 7), ((3,), ((0, 2),), 0.2, 7))
        SCALE_AFTER, END_AFTER = (2, 5) if da else (2, 2)
        STEPS = head_steps()

        def walk(h, pair, u, handlers, back=(0, 1)):
            for kind, b, *args in STEPS:
                if b in back and kind in handlers:
                    handlers[kind](h - b if b else h, *args, u=u ^ b, pair=None if b else pair)

        def heads(engine, handlers):
            walk(0, 0, 0, handlers, (0,))
            with engine.Fori(0, H // 2 - 1) as j:
                walk(2 * j + 1, j, 1, handlers)
                walk(2 * j + 2, j + 1, 0, handlers)
            walk(H - 1, H // 2 - 1, 1, handlers)
            walk(H, H // 2, 0, handlers, (1,))

        def key_cols(t):
            return (0, META) if t == 0 else (META + P * (t - 1), P)

        def first_tile(g, t):
            return max(0, t - 1 - 4 * g)

        BY_DVE = [not da and at % 2 == 1 for at in range(NKT)]

        def splits(split_q, split_keys):
            def next_keys(h, piece, u, pair):
                if not (isinstance(h, int) and h == H - 1):
                    split_keys(h + 1, 1 - u, piece)

            def next_q(h, **at):
                if not (isinstance(h, int) and h == H - 1):
                    split_q(h + 1, 0)

            def first_keys(h, piece, **at):
                if isinstance(h, int) and h == 0:
                    split_keys(0, 0, piece)

            return {"split_q": split_q, "split_next_q": next_q, "split_next_keys": next_keys, "split_first_keys": first_keys}

        def last_user(n, slots):
            return max(a for a in range(NKT) if a % slots == n)

        def slot_free(engine, h, n):
            if n >= NPT:
                engine.wait_ge(pv_done, NKT * h + n - NPT + 1)
            elif not (isinstance(h, int) and h == 0):
                engine.wait_ge(pv_done, NKT * (h - 1) + last_user(n, NPT) + 1)

        with nc.Block() as block:
            @block.sync
            def _(sp):
                def by_component(src, h, cols):
                    return src[ds(h, 1), :, cols].rearrange("a (c p) n -> p (a c) n", c=2)

                def load_keys(h, u, cols=slice(0, L), signal=None):
                    if da:
                        for j, src in enumerate((scr.qk_hi, scr.qk_lo)):
                            for half in range(2):
                                sp.dma_start(f32(keys[half * 64:half * 64 + 64, u, j::2, cols]),
                                             by_component(src, h + DA_H, cols)).then_inc(signal or keys_loaded[u], 16)
                    else:
                        sp.dma_start(k_raw[:, cols], flat(scr.mk[ds(h, 1), :, cols])).then_inc(signal or k_raw_loaded, 16)

                def load_bias(h, u):
                    if da:
                        sp.dma_start(bias[:, u], flat(io.bias[ds(h, 1), :, :])).then_inc(bias_loaded[u], 16)

                def load_q(h, pair, u, g):
                    cols = slice(512 * g, 512 * g + 512)
                    if da:
                        for j, src in enumerate((scr.qk_hi, scr.qk_lo)):
                            sp.dma_start(f32(qs[64 * j:64 * j + 64, g % 2]),
                                         by_component(src, h, slice(META + 512 * g, META + 512 * g + 512))).then_inc(q_loaded[g % 2], 16)
                    else:
                        sp.dma_start(q_raw[:, g % 2, 0], flat(scr.mq[ds(h, 1), :, cols])).then_inc(q_loaded[g % 2], 16)
                        for half in range(2):
                            sp.dma_start(q_raw[64 * half:64 * half + 64, g % 2, 1],
                                         flat(scr.mqr[ds(pair, 1), u * 64:u * 64 + 64, cols])).then_inc(q_loaded[g % 2], 16)

                def load_v(h, g):
                    src = scr.v if da else scr.mv
                    cols = ds(h * P, P)
                    sp.dma_start(v[:, 4 * g:4 * g + 4, :],
                                 src[META + 512 * g:META + 512 * g + 512, cols].rearrange("(t p) n -> p t n", p=P)).then_inc(v_loaded[g], 16)
                    if g == 0:
                        sp.dma_start(v_meta[:, :], src[0:META, cols]).then_inc(v_loaded[g], 16)

                def store(h, g):
                    sp.wait_ge(o_copied, NG * h + g + 1)
                    sp.dma_start(flat(scr.yT[ds(h + (0 if da else DA_H), 1), :, 512 * g:512 * g + 512]), o_out[:, g % 2]).then_inc(o_stored[g % 2], 16)

                def scores_done(h, g):
                    sp.wait_ge(scores_ready, NCH * h + sum(1 for i, *_ in chunks if i < 4 * (g + 1)))

                def head(h, pair, u):
                    first, last = isinstance(h, int) and h == 0, isinstance(h, int) and h == H - 1
                    scores_done(h, 0)
                    load_q(h, pair, u, 2)

                    def next_v(g):
                        sp.wait_ge(pv_done, NKT * (h - 1) + kt_base[NG - 1] + 5 + 4 * g)
                        load_v(h, g)

                    if not first:
                        store(h - 1, 2)
                        for g in range(2):
                            next_v(g)
                    if not last:
                        if not first:
                            sp.wait_ge(scores_read, NCH * h)
                        if not da:
                            sp.wait_ge(k_split, len(KEY_PIECES) * (h + 1))
                        load_keys(h + 1, 1 - u)
                        load_bias(h + 1, 1 - u)
                    if not first:
                        for g in range(2, NG):
                            next_v(g)
                        store(h - 1, 3)
                    scores_done(h, 1)
                    load_q(h, pair, u, 3)
                    scores_done(h, 2)
                    if not last:
                        load_q(h + 1, pair + u, 1 - u, 0)
                    store(h, 0)
                    scores_done(h, 3)
                    if not last:
                        load_q(h + 1, pair + u, 1 - u, 1)
                    store(h, 1)

                for g, (c0, n) in enumerate(KEY_PIECES):
                    cols, back_cols = slice(c0, c0 + n), slice(L - c0 - n, L - c0)
                    if g < 2:
                        load_q(0, 0, 0, g)
                    load_keys(0, 0, cols, start_loaded[g])
                    if da:
                        sp.dma_start(bias[:, 0, back_cols], io.bias[0, :, back_cols]).then_inc(start_loaded[g], 16)
                    else:
                        sp.dma_start(bias[:, 0, back_cols], io.bias[DA_H, :, back_cols]).then_inc(start_loaded[g], 16)
                        for j, src in enumerate((scr.c_hi, scr.c_lo)):
                            sp.dma_start(f32(rope_keys[:, j, cols]), src[:, 3, cols]).then_inc(start_loaded[g], 16)
                    if g == 0 and da:
                        for j, src in enumerate((io.lam_q1, io.lam_k1, io.lam_q2, io.lam_k2)):
                            sp.dma_start(lam_in[:, j], src.broadcast_to([P, DA_HD])).then_inc(lam_loaded, 16)
                        sp.dma_start(ident[:, :], io.ident).then_inc(ident_loaded, 16)
                for g in range(NG):
                    load_v(0, g)
                if work is not None:
                    sp.dma_start(work[:, :, :], io.w_o[0, 0:DA_W, :].rearrange("(k p) n -> p k n", p=P)).then_inc(w_o_loaded, 16)
                    sp.dma_start(g_sub[:, 0:1], io.g_da_sub).then_inc(w_o_loaded, 16)
                head(0, 0, 0)
                with sp.Fori(0, H // 2 - 1) as j:
                    head(2 * j + 1, j, 1)
                    head(2 * j + 2, j + 1, 0)
                head(H - 1, H // 2 - 1, 1)
                store(H - 1, 2)
                store(H - 1, 3)
                for u in range(2):
                    sp.wait_ge(o_stored[u], 16 * 2 * H)

            @block.gpsimd
            def _(pool):
                def scaled(h, i, u, **at):
                    hold(pool, inv_ready, NT * h + i + 1)
                    pool.tensor_scalar(row(i, u), row(i, u), inv[:, i % 2, 0:1], 1.0, ALU.mult,
                                       ALU.mult).then_inc(first_scaled if da else probs_ready, 1)

                heads(pool, {"scale": scaled})
                if work is not None:
                    pool.wait_ge(w_o_loaded, 32)
                    pool.tensor_scalar(g_sub[:, 1:2], g_sub[:, 0:1], 1.0 - LAMBDA_INIT, 1.0, ALU.mult, ALU.mult).then_inc(gain_made, 1)
                    pool.wait_ge(gain_made, 1)
                    for k in range(DA_H):
                        pool.tensor_scalar(work[:, k], work[:, k], g_sub[:, 1:2], 1.0, ALU.mult, ALU.mult)

            @block.scalar
            def _(act):
                def exp(h, i, c, u, **at):
                    act.wait_ge(max_ready, NT * COMPS * h + COMPS * i + c + 1)
                    act.activation(comp_row(i, c, u), comp_row(i, c, u), ACT.Exp, bias=nmax[:, i % 2, c:c + 1], scale=scale,
                                   accum_out=total[:, i % 2, c:c + 1]).then_inc(exp_ready, 1)
                    if da and isinstance(h, int) and (h, i, c) == (0, 0, 1):
                        for j in range(2):
                            act.wait_ge(lam_step, j + 1)
                            act.activation(lam[:, j:j + 1], lam[:, j:j + 1], ACT.Exp).then_inc(lam_exp, 1)

                def copy(h, g, t, **at):
                    n = kt_base[g] + t
                    if not BY_DVE[n]:
                        c0 = P * first_tile(g, t)
                        rows = key_cols(t)[1]
                        slot_free(act, h, n)
                        act.wait_ge(pT_ready, NKT * h + n + 1)
                        act.activation(pT[0:rows, n % NPT, c0:512], ps_t[n % NTB][0:rows, c0:512], ACT.Copy).then_inc(act_copied, 1)

                def out(h, g, **at):
                    act.wait_ge(pv_done, NKT * h + kt_base[g] + tiles_of(g))
                    if not (isinstance(h, int) and h == 0 and g < 2):
                        act.wait_ge(o_stored[g % 2], 16 * (2 * h + g // 2))
                    act.activation(o_out[:, g % 2], ps_o[:, :], ACT.Copy).then_inc(o_copied, 1)

                def split_keys(h, u, piece):
                    c0, n = KEY_PIECES[piece]
                    if isinstance(h, int) and h == 0:
                        act.wait_ge(start_loaded[piece], 16 * START_LOADS)
                    else:
                        act.wait_ge(k_raw_loaded, 16 * h)
                    act.activation(keys[:, u, 0, c0:c0 + n], k_raw[:, c0:c0 + n], ACT.Copy).then_inc(k_hi_ready, 1)

                def split_q(h, g, **at):
                    act.wait_ge(q_loaded[g % 2], 16 * Q_LOADS * (2 * h + g // 2 + 1))
                    if not (isinstance(h, int) and h == 0 and g < 2):
                        act.wait_ge(scores_ready, NCH * h + first_chunk(4 * g - 4) if g >= 2 else
                                    NCH * (h - 1) + (first_chunk(4 * g + 12) if g == 0 else NCH))
                    for part in range(2):
                        act.activation(qs[:, g % 2, 2 * part], q_raw[:, g % 2, part], ACT.Copy).then_inc(q_hi_ready, 1)

                if not da:
                    split_keys(0, 0, 0)
                    split_q(0, 0)
                heads(act, {"exp": exp, "turn": copy, "out": out, **splits(split_q, split_keys)})

            @block.vector
            def _(dve):
                def chunk(h, n, pair, u):
                    i, c, k0, w = chunks[n]
                    g = i // 4
                    first_head = isinstance(h, int) and h == 0
                    if first_head and n == first_chunk(4 * g):
                        dve.wait_ge(start_loaded[g], 16 * START_LOADS)
                    elif da and n == 0:
                        dve.wait_ge(bias_loaded[u], 16 * (pair + u))
                    if i % 4 == 0 and c == 0 and k0 == 0:
                        if g == 3:
                            dve.wait_ge(pT_ready, NKT * h + kt_base[2])
                        elif g != 1 and not (isinstance(h, int) and h == 0):
                            dve.wait_ge(pT_ready, NKT * (h - 1) + (kt_base[3] if g == 0 else NKT))
                    nth = sum(1 for m in range(n) if chunks[m][:2] == (i, c))
                    b0 = (NT - 1 - i) * P + k0
                    hold(dve, scores_ready, NCH * h + n + 1)
                    dve.tensor_tensor_reduce(out=comp_row(i, c, u)[:, k0:k0 + w], in0=ps_s[n % NSB][:, 0:w],
                                             in1=bias[:, u if da else 0, b0:b0 + w], scale=1.0, scalar=LOWEST,
                                             op0=ALU.add, op1=ALU.max,
                                             accum_out=mx[:, i % 2, c, nth:nth + 1]).then_inc(scores_read, 1)
                    if k0 + w == META + P * (i + 1):
                        dve.wait_ge(scores_read, NCH * h + n + 1)
                        dve.tensor_scalar(nmax_all[:, 0:nth + 1], mx[:, i % 2, c, 0:nth + 1], -scale, None, ALU.mult, ALU.min,
                                          accum_out=nmax[:, i % 2, c:c + 1]).then_inc(max_ready, 1)
                    if da and first_head and n == 1:
                        lambda_sums()

                def lambda_sums():
                    dve.wait_ge(lam_loaded, 64)
                    for j in range(2):
                        dve.tensor_tensor_reduce(out=lam_in[:, 2 * j], in0=lam_in[:, 2 * j], in1=lam_in[:, 2 * j + 1], scale=1.0,
                                                 scalar=0.0, op0=ALU.mult, op1=ALU.add, accum_out=lam[:, j:j + 1]).then_inc(lam_step, 1)

                def minus_lambda():
                    dve.wait_ge(lam_exp, 2)
                    dve.tensor_tensor(lam[:, 2:3], lam[:, 1:2], lam[:, 0:1], ALU.subtract).then_inc(lam_step, 1)
                    dve.wait_ge(lam_step, 3)
                    dve.tensor_scalar(lam[:, 3:4], lam[:, 2:3], -LAMBDA_INIT, None, ALU.add).then_inc(lam_step, 1)
                    dve.wait_ge(lam_step, 4)

                def invert(h, i, u, **at):
                    dve.wait_ge(exp_ready, NT * COMPS * h + COMPS * i + 1)
                    if not (isinstance(h, int) and h == 0 and i < 2):
                        dve.wait_ge(first_scaled if da else probs_ready, NT * h + i - 1)
                    dve.reciprocal(inv[:, i % 2, 0:1], total[:, i % 2, 0:1]).then_inc(inv_ready, 1)

                def end(h, i, u, **at):
                    if not da:
                        return
                    if isinstance(h, int) and (h, i) == (0, 0):
                        minus_lambda()
                    n = 2 * (NT * h + i)
                    dve.wait_ge(exp_ready, NT * COMPS * h + COMPS * (i + 1))
                    dve.reciprocal(inv[:, i % 2, 1:2], total[:, i % 2, 1:2]).then_inc(inv2_step, 1)
                    dve.wait_ge(inv2_step, n + 1)
                    dve.tensor_scalar(inv2[:, i % 2:i % 2 + 1], inv[:, i % 2, 1:2], lam[:, 3:4], None, ALU.mult).then_inc(inv2_step, 1)
                    dve.wait_ge(inv2_step, n + 2)
                    dve.wait_ge(first_scaled, NT * h + i + 1)
                    dve.scalar_tensor_tensor(out=row(i, u), in0=comp_row(i, 1, u), scalar=inv2[:, i % 2:i % 2 + 1], in1=row(i, u),
                                             op0=ALU.mult, op1=ALU.add).then_inc(probs_ready, 1)

                def copy(h, g, t, **at):
                    n = kt_base[g] + t
                    if BY_DVE[n]:
                        c0 = P * first_tile(g, t)
                        rows = key_cols(t)[1]
                        slot_free(dve, h, n)
                        dve.wait_ge(pT_ready, NKT * h + n + 1)
                        dve.tensor_copy(pT[0:rows, n % NPT, c0:512], ps_t[n % NTB][0:rows, c0:512]).then_inc(dve_copied, 1)

                def split_keys(h, u, piece):
                    c0, n = KEY_PIECES[piece]
                    dve.wait_ge(k_hi_ready, len(KEY_PIECES) * h + piece + 1)
                    dve.tensor_tensor(keys[:, u, 1, c0:c0 + n], k_raw[:, c0:c0 + n], f32(keys[:, u, 0, c0:c0 + n]),
                                      ALU.subtract).then_inc(k_split, 1)

                def split_q(h, g, **at):
                    dve.wait_ge(q_hi_ready, 2 * (NG * h + g) + 2)
                    dve.tensor_tensor(qs[:, g % 2, 1], q_raw[:, g % 2, 0], f32(qs[:, g % 2, 0]), ALU.subtract).then_inc(q_split, 1)
                    low = slice(ROPE, 2 * ROPE)
                    dve.tensor_tensor(qs[low, g % 2, 2], q_raw[low, g % 2, 1], f32(qs[low, g % 2, 2]), ALU.subtract).then_inc(q_split, 1)

                if not da:
                    split_keys(0, 0, 0)
                    split_q(0, 0)
                heads(dve, {"chunk": chunk, "scale": invert, "end": end, "turn": copy, **splits(split_q, split_keys)})

            @block.tensor
            def _(pe):
                def scores(h, n, pair, u):
                    i, c, k0, w = chunks[n]
                    g, b = i // 4, i % 4
                    first_head = isinstance(h, int) and h == 0
                    if first_head and n == first_chunk(4 * g):
                        pe.wait_ge(start_loaded[g], 16 * START_LOADS)
                        if not da:
                            pe.wait_ge(k_split, g + 1)
                    elif n == 0:
                        if da:
                            pe.wait_ge(keys_loaded[u], 16 * KEY_LOADS * (pair + u))
                        else:
                            pe.wait_ge(k_split, len(KEY_PIECES) * (h + 1))
                    if b == 0 and c == 0 and k0 == 0:
                        if da:
                            pe.wait_ge(q_loaded[g % 2], 16 * Q_LOADS * (2 * h + g // 2 + 1))
                        else:
                            pe.wait_ge(q_split, 2 * (NG * h + g + 1))
                    if not (isinstance(h, int) and h == 0 and n < NSB):
                        pe.wait_ge(scores_read, NCH * h + n - NSB + 1)
                    cols = slice(P * b, P * b + P)
                    if da:
                        pairs = [(qs[:, g % 2, c, cols], keys[:, u, 2 * c + j, k0:k0 + w]) for j in range(2)]
                    else:
                        q_hi, q_lo, q_rope = (qs[:, g % 2, j, cols] for j in range(3))
                        k_hi, k_lo = (keys[:, u, j, k0:k0 + w] for j in range(2))
                        pairs = [(q_hi, k_hi), (q_hi, k_lo), (q_lo, k_hi)]
                        pairs += [(q_rope, rope_keys[:, j, k0:k0 + w]) for j in range(2)]
                    for j, (q, k) in enumerate(pairs):
                        m = pe.matmul(ps_s[n % NSB][:, 0:w], q, k, start=j == 0, stop=j == len(pairs) - 1)
                    m.then_inc(scores_ready, 1)

                def copied(h, n):
                    by_dve = sum(BY_DVE[:n + 1])
                    if BY_DVE[n]:
                        pe.wait_ge(dve_copied, sum(BY_DVE) * h + by_dve)
                    else:
                        pe.wait_ge(act_copied, (NKT - sum(BY_DVE)) * h + n + 1 - by_dve)

                def turn(h, g, t, u, **at):
                    if t == 0:
                        pe.wait_ge(probs_ready, NT * h + 4 * g + 4)
                    n, (k0, rows) = kt_base[g] + t, key_cols(t)
                    if n >= NTB:
                        copied(h, n - NTB)
                    elif not (isinstance(h, int) and h == 0):
                        copied(h - 1, last_user(n, NTB))
                    for b in range(first_tile(g, t), 4):
                        m = pe.transpose(ps_t[n % NTB][0:rows, P * b:P * b + P], row(4 * g + b, u)[:, k0:k0 + rows], ident[:, :])
                    m.then_inc(pT_ready, 1)

                def product(h, g, t, **at):
                    n, rows = kt_base[g] + t, key_cols(t)[1]
                    copied(h, n)
                    if t == 0:
                        pe.wait_ge(v_loaded[0], 32 * (h + 1))
                        if not (isinstance(h, int) and h == 0 and g == 0):
                            pe.wait_ge(o_copied, NG * h + g)
                    elif t % 4 == 1 and t > 1:
                        pe.wait_ge(v_loaded[t // 4], 16 * (h + 1))
                    c0 = P * first_tile(g, t)
                    pe.matmul(ps_o[:, c0:512], v_meta[:, :] if t == 0 else v[:, t - 1], pT[0:rows, n % NPT, c0:512],
                              start=t == 0, stop=t == tiles_of(g) - 1).then_inc(pv_done, 1)

                if da:
                    pe.wait_ge(ident_loaded, 16)
                heads(pe, {"chunk": scores, "turn": turn, "product": product})


def mix_out(nc, io, scr, res_hi, res_lo, work, ident, w1_raw, g_pre):
    NRES = res_hi.shape[2] // P
    with ExitStack() as ctx:
        mem = Memory(nc, ctx)
        xres, hn = work[:, 0:2], work[:, 2:4]
        w_hi = mem.sb("mo_w_hi", [P, KD, D], F32R)
        w_lo = mem.sb("mo_w_lo", [P, KD, D], F32R)
        ones = mem.sb("mo_ones", [P, P])
        eps = mem.sb("mo_eps", [P, 1])
        g_post = mem.sb("mo_g_post", [P, D])
        y = mem.sb("mo_y", [P, 2, KD, P])
        y_hi = mem.sb("mo_y_hi", [P, 2, KD, P], F32R)
        y_lo = mem.sb("mo_y_lo", [P, 2, KD, P], F32R)
        sq = mem.sb("mo_sq", [P, DA_H * P])
        y_rstd = mem.sb("mo_y_rstd", [P, DA_H * P])
        h = mem.sb("mo_h", [P, 2, D])
        u_hi = mem.sb("mo_u_hi", [P, 2, KD, P], F32R)
        u_lo = mem.sb("mo_u_lo", [P, 2, KD, P], F32R)
        stat = mem.sb("mo_stat", [P, 2, 6])
        ps_r = mem.ps("mo_ps_r")
        ps_m = [mem.ps(f"mo_ps_m{i}", D) for i in range(2)]
        ps_t = mem.ps("mo_ps_t", D)
        const_loaded, const_set = mem.sem("mo_const_loaded"), mem.sem("mo_const_set")
        w_loaded = [mem.sem(f"mo_w_loaded{v}") for v in range(4)]
        w_hi_ready, w_lo_ready, w1_loaded = (mem.sem(f"mo_{s}") for s in ("w_hi_ready", "w_lo_ready", "w1_loaded"))
        y_loaded = [mem.sem(f"mo_y_loaded{u}") for u in range(2)]
        x_loaded = [mem.sem(f"mo_x_loaded{u}") for u in range(2)]
        sq_ready, mean_ready, y_log_ready, y_rstd_ready, y_normed = (mem.sem(f"mo_y_{s}") for s in ("sq", "mean", "log", "rstd", "normed"))
        y_hi_ready, y_lo_ready, mix_ready = (mem.sem(f"mo_{s}") for s in ("y_hi_ready", "y_lo_ready", "mix_ready"))
        stat_step = mem.sem("mo_stat_step")
        post_ready, h_ready, hn_ready, hT_ready = (mem.sem(f"mo_{s}_ready") for s in ("post", "h", "hn", "hT"))
        u_hi_ready, u_lo_ready = mem.sem("mo_u_hi_ready"), mem.sem("mo_u_lo_ready")
        h_stored = [mem.sem(f"mo_h_stored{u}") for u in range(2)]
        u_stored = [mem.sem(f"mo_u_stored{u}") for u in range(2)]

        def steps(engine, body):
            for s in range(4):
                body(s, s % 2, s // 2, True, s >= 2, True, True)
            with engine.Fori(2, NRES // 2 + 1) as j:
                for u in range(2):
                    body(2 * j + u, u, j, True, True, False, True)
            for s in range(NRES + 2, NRES + 4):
                body(s, s % 2, s // 2, True, True, False, False)
            with engine.Fori(NRES // 2 + 2, NT // 2) as j:
                for u in range(2):
                    body(2 * j + u, u, j, True, True, False, False)
            for s in range(NT, NT + 2):
                body(s, s % 2, s // 2, False, True, False, False)

        W_FIRST = 2

        def u_place(s, u, stays):
            if stays:
                return res_hi[:, :, ds((s - 2) * P, P)], res_lo[:, :, ds((s - 2) * P, P)]
            return u_hi[:, u], u_lo[:, u]

        with nc.Block() as block:
            @block.sync
            def _(sp):
                def load_w(k):
                    sp.wait_ge(w_lo_ready, k - 3)
                    sp.dma_start(work[:, k % 4], io.w_o[0, k * P:(k + 1) * P, :]).then_inc(w_loaded[k % 4], 16)

                def load_y(t, u):
                    sp.dma_start(y[:, u], scr.yT[:, :, ds(t * P, P)].rearrange("f p t -> p f t")).then_inc(y_loaded[u], 16)

                def load_x(t, u):
                    sp.dma_start(xres[:, u], flat(io.x[:, ds(t * P, P), :])).then_inc(x_loaded[u], 16)

                def store_u(t, u):
                    hold(sp, u_lo_ready, t + 1)
                    for src, dst in ((u_hi, scr.u_hi), (u_lo, scr.u_lo)):
                        sp.dma_start(dst[:, :, ds((t - NRES) * P, P)], f32(src[:, u])).then_inc(u_stored[u], 16)

                load_y(0, 0)
                load_y(1, 1)
                sp.dma_start(g_post[:, :], io.g_attn_post.broadcast_to([P, D])).then_inc(const_loaded, 16)
                for k in range(4, KD):
                    load_w(k)
                for t in range(2):
                    sp.wait_ge(w_lo_ready, t + 5)
                    load_x(t, t)
                sp.dma_start(w1_raw[:, :, :], w1_rows(io)[:, :, 0:P]).then_inc(w1_loaded, 16)
                sp.dma_start(g_pre[:, :], io.g_mlp_pre).then_inc(w1_loaded, 16)

                def body(s, u, nth, prep, post, first, stays):
                    if not post:
                        return
                    if prep:
                        hold(sp, y_lo_ready, s - 1)
                        load_y(s, u)
                    if not stays and not (isinstance(s, int) and s == NRES + 2):
                        store_u(s - 3, 1 - u)
                    cols = ds((s - 2) * P, P)
                    hold(sp, h_ready, s - 1)
                    sp.dma_start(scr.h[cols, :], h[:, u]).then_inc(h_stored[u], 16)
                    if prep:
                        load_x(s, u)

                steps(sp, body)
                store_u(NT - 1, (NT - 1) % 2)
                for u in range(2):
                    sp.wait_ge(h_stored[u], 16 * NT // 2)
                    sp.wait_ge(u_stored[u], 32 * (NT - NRES) // 2)

            @block.gpsimd
            def _(pool):
                pool.memset(ones[:, :], 1.0 / DA_V).then_inc(const_set, 1)
                pool.memset(eps[:, :], EPS).then_inc(const_set, 1)

                def body(s, u, nth, prep, post, first, stays):
                    if not post:
                        return
                    if not first:
                        pool.wait_ge(hT_ready, s - 3)
                    pool.wait_ge(stat_step, 6 * (s - 1))
                    pool.nop(nofuse=True)
                    pool.tensor_scalar(hn[:, u], h[:, u], stat[:, u, 5:6], 1.0, ALU.mult, ALU.mult).then_inc(hn_ready, 1)

                steps(pool, body)
                pool.wait_ge(w1_loaded, 32)
                pool.tensor_tensor(w1_raw[:, :, :], w1_raw[:, :, :], g_pre[:, :].unsqueeze(2).broadcast_to([P, KD, P]), ALU.mult)

            @block.scalar
            def _(act):
                act.preload_act_table_set("natural_log_exp_and_others")
                act.wait_ge(const_set, 2)

                def split_w(k):
                    if k >= 4:
                        act.wait_ge(w_loaded[k % 4], 16)
                    act.activation(w_hi[:, k], work[:, k % 4], ACT.Copy).then_inc(w_hi_ready, 1)

                def slot_stored(s, u, nth):
                    if not (isinstance(s, int) and s < NRES + 4):
                        act.wait_ge(u_stored[u], 32 * (nth - 1 - NRES // 2))

                def rstd(src, s, u, at):
                    n = 6 * (s - 2) + at
                    act.activation(hn[:, u], src, ACT.Square, accum_out=stat[:, u, at:at + 1]).then_inc(stat_step, 1)
                    act.wait_ge(stat_step, n + 1)
                    act.activation(stat[:, u, at + 1:at + 2], stat[:, u, at:at + 1], ACT.Ln, bias=eps[:, :], scale=1.0 / D).then_inc(stat_step, 1)
                    act.wait_ge(stat_step, n + 2)
                    act.activation(stat[:, u, at + 2:at + 3], stat[:, u, at + 1:at + 2], ACT.Exp, scale=-0.5).then_inc(stat_step, 1)

                def body(s, u, nth, prep, post, first, stays):
                    if post:
                        act.wait_ge(mix_ready, s - 1)
                        rstd(ps_m[u][:, :], s, u, 0)
                    if prep:
                        act.wait_ge(y_loaded[u], 16 * nth + 16)
                        act.activation(sq[:, :].rearrange("p (f t) -> p f t", f=DA_H), y[:, u, 0:DA_H], ACT.Square).then_inc(sq_ready, 1)
                    if post:
                        act.wait_ge(h_ready, s - 1)
                        rstd(h[:, u], s, u, 3)
                    if prep:
                        act.wait_ge(mean_ready, s + 1)
                        act.activation(y_rstd[:, :], ps_r[:, :], ACT.Ln, bias=eps[:, :]).then_inc(y_log_ready, 1)
                        act.wait_ge(y_log_ready, s + 1)
                        act.activation(y_rstd[:, :], y_rstd[:, :], ACT.Exp, scale=-0.5).then_inc(y_rstd_ready, 1)
                        act.wait_ge(y_normed, s + 1)
                        act.activation(y_hi[:, u], y[:, u], ACT.Copy).then_inc(y_hi_ready, 1)
                    if post:
                        act.wait_ge(hT_ready, s - 1)
                        if not stays:
                            slot_stored(s, u, nth)
                        act.activation(u_place(s, u, stays)[0], ps_t[:, :].rearrange("p (k t) -> p k t", k=KD), ACT.Copy).then_inc(u_hi_ready, 1)
                    if isinstance(s, int) and s == 0:
                        for k in range(W_FIRST, KD):
                            split_w(k)

                for k in range(W_FIRST):
                    split_w(k)

                steps(act, body)

            @block.vector
            def _(dve):
                def split_w(k):
                    dve.wait_ge(w_hi_ready, k + 1)
                    dve.tensor_tensor(w_lo[:, k], work[:, k % 4], f32(w_hi[:, k]), ALU.subtract).then_inc(w_lo_ready, 1)

                def body(s, u, nth, prep, post, first, stays):
                    if post:
                        if not first:
                            dve.wait_ge(h_stored[u], 16 * (nth - 1))
                            dve.wait_ge(hn_ready, s - 3)
                        dve.wait_ge(stat_step, 6 * (s - 2) + 3)
                        dve.scalar_tensor_tensor(out=h[:, u], in0=ps_m[u][:, :], scalar=stat[:, u, 2:3], in1=g_post[:, :],
                                                 op0=ALU.mult, op1=ALU.mult).then_inc(post_ready, 1)
                        dve.wait_ge(x_loaded[u], 16 * nth)
                        dve.wait_ge(post_ready, s - 1)
                        dve.tensor_tensor(h[:, u], h[:, u], xres[:, u], ALU.add).then_inc(h_ready, 1)
                    if prep:
                        dve.wait_ge(y_rstd_ready, s + 1)
                        dve.tensor_tensor(y[:, u, 0:DA_H], y[:, u, 0:DA_H], y_rstd[:, :].rearrange("p (f t) -> p f t", f=DA_H),
                                          ALU.mult).then_inc(y_normed, 1)
                        dve.wait_ge(y_hi_ready, s + 1)
                        dve.tensor_tensor(y_lo[:, u], y[:, u], f32(y_hi[:, u]), ALU.subtract).then_inc(y_lo_ready, 1)
                    if post:
                        dve.wait_ge(u_hi_ready, s - 1)
                        to_hi, to_lo = u_place(s, u, stays)
                        dve.tensor_tensor(to_lo, ps_t[:, :].rearrange("p (k t) -> p k t", k=KD), f32(to_hi),
                                          ALU.subtract).then_inc(u_lo_ready, 1)

                    if isinstance(s, int) and s == 0:
                        for k in range(W_FIRST, KD):
                            split_w(k)

                for k in range(W_FIRST):
                    split_w(k)
                dve.wait_ge(const_loaded, 16)
                steps(dve, body)

            @block.tensor
            def _(pe):
                pe.wait_ge(const_set, 2)

                def product(s, u, half):
                    cols = slice(512 * half, 512 * half + 512)
                    for k in range(KD):
                        if isinstance(s, int) and s == 1 and half == 0:
                            pe.wait_ge(w_lo_ready, k + 1)
                        for i, (a, w) in enumerate(((y_hi, w_hi), (y_hi, w_lo), (y_lo, w_hi))):
                            m = pe.matmul(ps_m[1 - u][:, cols], a[:, 1 - u, k], w[:, k, cols],
                                          start=k == 0 and i == 0, stop=k == KD - 1 and i == 2)
                    return m

                def body(s, u, nth, prep, post, first, stays):
                    has_product = not isinstance(s, int) or 1 <= s <= NT
                    if has_product:
                        pe.wait_ge(y_lo_ready, s)
                        if not isinstance(s, int) or s >= 3:
                            pe.wait_ge(post_ready, s - 2)
                        product(s, u, 0)
                    if prep:
                        pe.wait_ge(sq_ready, s + 1)
                        pe.matmul(ps_r[:, :], ones[:, :], sq[:, :], start=True, stop=True).then_inc(mean_ready, 1)
                    if has_product:
                        product(s, u, 1).then_inc(mix_ready, 1)
                    if post:
                        pe.wait_ge(hn_ready, s - 1)
                        if not (isinstance(s, int) and s == 2):
                            pe.wait_ge(u_lo_ready, s - 2)
                        for k in range(KD):
                            m = pe.transpose(ps_t[:, k * P:(k + 1) * P], hn[:, u, k * P:(k + 1) * P], ident[:, :])
                        m.then_inc(hT_ready, 1)

                steps(pe, body)


def w1_rows(io):
    return io.w_ff1.rearrange("a (k p) n -> p (a k) n", p=P)


def mlp(nc, io, scr, u_hi, u_lo, w1_raw, g_pre, work):
    GT = u_hi.shape[2]
    NGR = SEQ // GT
    assert GT == D
    TG = GT // P
    NM = DFF // P
    NC = NM // 2
    with ExitStack() as ctx:
        mem = Memory(nc, ctx)
        hid_hi = mem.sb("ff_hid_hi", [P, 4, GT], F32R)
        hid_lo = mem.sb("ff_hid_lo", [P, 4, GT], F32R)
        acc = mem.sb("ff_acc", [P, TG, D])
        w1_hi = mem.sb("ff_w1_hi", [P, 2, KD, P], F32R)
        w1_lo = mem.sb("ff_w1_lo", [P, 2, KD, P], F32R)
        relu, square, w2_raw, g_post = (work[:, j] for j in range(4))
        w2_hi = mem.sb("ff_w2_hi", [P, 4, D], F32R)
        w2_lo = mem.sb("ff_w2_lo", [P, 4, D], F32R)
        h_in = mem.sb("ff_h_in", [P, 2, D])
        eps = mem.sb("ff_eps", [P, 1])
        stat = mem.sb("ff_stat", [P, 3])
        ps1 = [mem.ps(f"ff_ps1_{i}", GT) for i in range(2)]
        ps2 = [mem.ps(f"ff_ps2_{i}", D) for i in range(2)]
        post_gain_loaded, eps_set = mem.sem("ff_post_gain_loaded"), mem.sem("ff_eps_set")
        u_loaded = [mem.sem(f"ff_u_loaded{k}") for k in range(KD)]
        w1_loaded, w1_gained, w1_hi_ready, w1_lo_ready = (mem.sem(f"ff_w1_{s}") for s in ("loaded", "gained", "hi_ready", "lo_ready"))
        w2_loaded, w2_hi_ready, w2_lo_ready = (mem.sem(f"ff_w2_{s}") for s in ("loaded", "hi_ready", "lo_ready"))
        pre_ready, relu_ready, square_ready = (mem.sem(f"ff_{s}_ready") for s in ("pre", "relu", "square"))
        hid_hi_ready, hid_lo_ready = mem.sem("ff_hid_hi_ready"), mem.sem("ff_hid_lo_ready")
        part_ready, part_added = mem.sem("ff_part_ready"), mem.sem("ff_part_added")
        stat_step = mem.sem("ff_stat_step")
        post_ready, out_ready = mem.sem("ff_post_ready"), mem.sem("ff_out_ready")
        h_loaded = [mem.sem(f"ff_h_loaded{u}") for u in range(2)]
        out_stored = [mem.sem(f"ff_out_stored{t}") for t in range(TG)]
        w1_v = w1_rows(io)

        def add_h(engine, n):
            engine.wait_ge(h_loaded[n % 2], 16 * (n // 2) + 16)
            engine.wait_ge(post_ready, n + 1)
            engine.tensor_tensor(acc[:, n % TG], acc[:, n % TG], h_in[:, n % 2], ALU.add).then_inc(out_ready, 1)

        def chunk_steps(engine, body, peeled=2):
            body(0, 0)
            body(1, 1)
            end = NC if peeled == 2 else NC - 2
            with engine.Fori(0, (end - 2) // 2) as j:
                body(2 * j + 2, 0)
                body(2 * j + 3, 1)
            for c in range(end, NC):
                body(c, c % 2)

        with nc.Block() as block:
            @block.sync
            def _(sp):
                def load_w1(G, m):
                    static = isinstance(m, int)
                    hold(sp, w1_lo_ready, NM * G + m)
                    col = (m % NM) * P if static else m * P
                    sp.dma_start(w1_raw[:, :, :], w1_v[:, :, ds(col, P)]).then_inc(w1_loaded, 16)

                def load_w2(G, m):
                    if not (isinstance(m, int) and NM * G + m == 0):
                        hold(sp, w2_lo_ready, NM * G + m)
                    sp.dma_start(w2_raw, flat(io.w_ff2[:, ds(m * P, P), :])).then_inc(w2_loaded, 16)

                def load_u(G):
                    for k in range(KD):
                        for src, dst in ((scr.u_hi, u_hi), (scr.u_lo, u_lo)):
                            sp.dma_start(f32(dst[:, k]), src[:, k, (G - 1) * GT:G * GT]).then_inc(u_loaded[k], 16)

                def load_h(n):
                    sp.dma_start(h_in[:, n % 2], scr.h[n * P:(n + 1) * P, :]).then_inc(h_loaded[n % 2], 16)

                load_w1(0, 1)
                sp.dma_start(g_post, io.g_mlp_post.broadcast_to([P, D])).then_inc(post_gain_loaded, 16)
                load_h(0)
                load_h(1)
                load_w2(0, 0)
                load_w1(0, 2)
                for G in range(NGR):
                    with sp.Fori(1, NM - 2) as m:
                        load_w2(G, m)
                        load_w1(G, m + 2)
                    for m in range(NM - 2, NM):
                        load_w2(G, m)
                        if G < NGR - 1:
                            load_w1(G, m + 2)
                    if G < NGR - 1:
                        sp.wait_ge(pre_ready, NM * (G + 1))
                        load_u(G + 1)
                        load_w2(G + 1, 0)
                        load_w1(G + 1, 2)
                    for t in range(TG):
                        n = TG * G + t
                        sp.wait_ge(out_ready, n + 1)
                        if n + 2 < TG * NGR:
                            load_h(n + 2)
                        sp.dma_start(io.out[0, n * P:(n + 1) * P, :], acc[:, t]).then_inc(out_stored[t], 16)
                for t in range(TG):
                    sp.wait_ge(out_stored[t], 16 * NGR)

            @block.gpsimd
            def _(pool):
                def gain(n):
                    pool.wait_ge(w1_loaded, 16 * n)
                    pool.tensor_tensor(w1_raw[:, :, :], w1_raw[:, :, :], g_pre[:, :].unsqueeze(2).broadcast_to([P, KD, P]),
                                       ALU.mult).then_inc(w1_gained, 1)

                pool.memset(eps[:, :], EPS).then_inc(eps_set, 1)
                gain(1)
                for G in range(NGR):
                    def body(c, u):
                        for e in range(2):
                            n = NM * G + 2 * c + e
                            if not (isinstance(n, int) and n == 0):
                                pool.wait_ge(hid_lo_ready, n)
                            pool.wait_ge(relu_ready, n + 1)
                            pool.tensor_tensor(square, relu, relu, ALU.mult).then_inc(square_ready, 1)
                            if not (isinstance(n, int) and n + 2 >= NM * NGR):
                                gain(n + 2)

                    chunk_steps(pool, body, 4)
                    for n in range(TG * G, min(TG * (G + 1), TG * NGR - 1)):
                        add_h(pool, n)

            @block.scalar
            def _(act):
                def split_w1(n, slot):
                    if not (isinstance(n, int) and n == 0):
                        act.wait_ge(w1_gained, n)
                    if not (isinstance(n, int) and n < 2):
                        act.wait_ge(pre_ready, n - 1)
                    act.activation(w1_hi[:, slot], w1_raw[:, :, :], ACT.Copy).then_inc(w1_hi_ready, 1)

                act.preload_act_table_set("natural_log_exp_and_others")
                split_w1(0, 0)
                split_w1(1, 1)
                act.wait_ge(eps_set, 1)
                for G in range(NGR):
                    def body(c, u):
                        for e in range(2):
                            n = NM * G + 2 * c + e
                            act.wait_ge(w2_loaded, 16 * n + 16)
                            if not (isinstance(n, int) and n < 4):
                                act.wait_ge(part_ready, TG * (NC * G + c - 1))
                            act.activation(w2_hi[:, 2 * u + e], w2_raw, ACT.Copy).then_inc(w2_hi_ready, 1)
                            act.wait_ge(pre_ready, n + 1)
                            if not (isinstance(n, int) and n == 0):
                                act.wait_ge(square_ready, n)
                                act.wait_ge(hid_hi_ready, n)
                            act.activation(relu, ps1[e][:, :], ACT.Relu).then_inc(relu_ready, 1)
                            act.wait_ge(relu_ready, n + 1)
                            act.activation(hid_hi[:, 2 * u + e], relu, ACT.Square).then_inc(hid_hi_ready, 1)
                            if not (isinstance(n, int) and n + 2 >= NM * NGR):
                                split_w1(n + 2, e)

                    chunk_steps(act, body, 4)
                    for t in range(TG):
                        n = TG * G + t
                        act.wait_ge(part_added, TG * NC * (G + 1) - TG + t + 1)
                        if n:
                            act.wait_ge(post_ready, n)
                        act.activation(relu, acc[:, t], ACT.Square, accum_out=stat[:, 0:1]).then_inc(stat_step, 1)
                        act.wait_ge(stat_step, 3 * n + 1)
                        act.activation(stat[:, 1:2], stat[:, 0:1], ACT.Ln, bias=eps[:, :], scale=1.0 / D).then_inc(stat_step, 1)
                        act.wait_ge(stat_step, 3 * n + 2)
                        act.activation(stat[:, 2:3], stat[:, 1:2], ACT.Exp, scale=-0.5).then_inc(stat_step, 1)

            @block.vector
            def _(dve):
                def split_w1(n, slot):
                    dve.wait_ge(w1_hi_ready, n + 1)
                    dve.tensor_tensor(w1_lo[:, slot], w1_raw[:, :, :], f32(w1_hi[:, slot]), ALU.subtract).then_inc(w1_lo_ready, 1)

                def add(G, c, t):
                    dve.wait_ge(part_ready, TG * (NC * G + c) + t + 1)
                    if isinstance(c, int) and c == 0:
                        if G:
                            dve.wait_ge(out_stored[t], 16 * G)
                        dve.tensor_copy(acc[:, t], ps2[t % 2][:, :]).then_inc(part_added, 1)
                    else:
                        dve.wait_ge(part_added, TG * (NC * G + c - 1) + t + 1)
                        dve.tensor_tensor(acc[:, t], acc[:, t], ps2[t % 2][:, :], ALU.add).then_inc(part_added, 1)

                split_w1(0, 0)
                split_w1(1, 1)
                dve.wait_ge(post_gain_loaded, 16)
                for G in range(NGR):
                    def body(c, u):
                        for e in range(2):
                            n = NM * G + 2 * c + e
                            dve.wait_ge(w2_hi_ready, n + 1)
                            dve.tensor_tensor(w2_lo[:, 2 * u + e], w2_raw, f32(w2_hi[:, 2 * u + e]), ALU.subtract).then_inc(w2_lo_ready, 1)
                            adds = [] if isinstance(c, int) and c == 0 else list(range(TG // 2 * e, TG // 2 * (e + 1)))
                            late = isinstance(c, int) and c == NC - 1 and e == 0
                            for t in [] if late else adds[:1]:
                                add(G, c - 1, t)
                            dve.wait_ge(hid_hi_ready, n + 1)
                            dve.wait_ge(square_ready, n + 1)
                            dve.tensor_tensor(hid_lo[:, 2 * u + e], square, f32(hid_hi[:, 2 * u + e]),
                                              ALU.subtract).then_inc(hid_lo_ready, 1)
                            for t in [] if late else adds[1:3]:
                                add(G, c - 1, t)
                            if not (isinstance(n, int) and n + 2 >= NM * NGR):
                                split_w1(n + 2, e)
                            for t in adds if late else adds[3:]:
                                add(G, c - 1, t)

                    chunk_steps(dve, body, 4)
                    add(G, NC - 1, 0)
                    for t in range(TG):
                        if t + 1 < TG:
                            add(G, NC - 1, t + 1)
                        n = TG * G + t
                        dve.wait_ge(stat_step, 3 * n + 3)
                        dve.scalar_tensor_tensor(out=acc[:, t], in0=acc[:, t], scalar=stat[:, 2:3], in1=g_post,
                                                 op0=ALU.mult, op1=ALU.mult).then_inc(post_ready, 1)
                        if n == TG * NGR - 1:
                            dve.wait_ge(out_ready, n)
                            add_h(dve, n)

            @block.tensor
            def _(pe):
                def hidden(G, c, e):
                    n = NM * G + 2 * c + e
                    pe.wait_ge(w1_lo_ready, n + 1)
                    if not (isinstance(n, int) and n < 2):
                        pe.wait_ge(relu_ready, n - 1)
                    for half in range(2):
                        cols = slice(512 * half, 512 * half + 512)
                        for k in range(KD):
                            if G and isinstance(c, int) and c == e == half == 0:
                                pe.wait_ge(u_loaded[k], 32 * G)
                            for i, (w, a) in enumerate(((w1_hi, u_hi), (w1_hi, u_lo), (w1_lo, u_hi))):
                                m = pe.matmul(ps1[e][:, cols], w[:, e, k], a[:, k, cols],
                                              start=k == 0 and i == 0, stop=k == KD - 1 and i == 2)
                    m.then_inc(pre_ready, 1)

                def part(G, c, u, t):
                    n = TG * (NC * G + c) + t
                    if not (isinstance(n, int) and n < 2):
                        pe.wait_ge(part_added, n - 1)
                    if t == 0:
                        pe.wait_ge(w2_lo_ready, NM * G + 2 * c + 2)
                        pe.wait_ge(hid_lo_ready, NM * G + 2 * c + 2)
                    for half in range(2):
                        cols = slice(512 * half, 512 * half + 512)
                        for e in range(2):
                            for i, (a, w) in enumerate(((hid_hi, w2_hi), (hid_hi, w2_lo), (hid_lo, w2_hi))):
                                m = pe.matmul(ps2[t % 2][:, cols], a[:, 2 * u + e, t * P:(t + 1) * P], w[:, 2 * u + e, cols],
                                              start=e == 0 and i == 0, stop=e == 1 and i == 2)
                    m.then_inc(part_ready, 1)

                for G in range(NGR):
                    def body(c, u):
                        last = isinstance(c, int) and c == NC - 1
                        for e in range(2):
                            hidden(G, c, e)
                            if last and e == 0:
                                continue
                            if not (isinstance(c, int) and c == 0):
                                for t in range(0 if last else TG // 2 * e, TG // 2 * (e + 1)):
                                    part(G, c - 1, 1 - u, t)

                    chunk_steps(pe, body, 4)
                    for t in range(TG):
                        part(G, NC - 1, 1, t)


class Arrays:
    pass


SCRATCH = {
    "qk_hi": (8, P, L), "qk_lo": (8, P, L),
    "c_hi": (P, 4, L), "c_lo": (P, 4, L),
    "v": (L, DA_W), "mv": (L, MLA_H * MLA_V),
    "mq": (MLA_H, P, SEQ), "mqr": (2, P, SEQ),
    "mk": (MLA_H, P, L),
    "yT": (8, P, SEQ),
    "u_hi": (P, KD, SEQ // 2), "u_lo": (P, KD, SEQ // 2),
    "h": (SEQ, D),
}


def build(nc, ins, out):
    io, scr = Arrays(), Arrays()
    (io.x, io.meta, io.g_attn_pre, io.w_in, io.lam_q1, io.lam_k1, io.lam_q2, io.lam_k2, io.g_da_sub, io.g_mla_q,
     io.w_q_up, io.g_mla_kv, io.w_kv_up, io.w_o, io.g_attn_post, io.g_mlp_pre, io.w_ff1, io.w_ff2, io.g_mlp_post,
     io.ident, io.trig_tm, io.trig_fm, io.bias) = ins
    io.out = out
    (scr.qk_hi, scr.qk_lo, scr.c_hi, scr.c_lo, scr.v, scr.mv, scr.mq, scr.mqr, scr.mk, scr.yT, scr.u_hi, scr.u_lo,
     scr.h) = (nc.dram_tensor(f"scr_{n}", s, F32).ap() for n, s in SCRATCH.items())
    with ExitStack() as ctx:
        mem = Memory(nc, ctx)
        u_hi = mem.sb("u_hi", [P, KD, L], F32R)
        u_lo = mem.sb("u_lo", [P, KD, L], F32R)
        ident = mem.sb("ident", [P, P])
        g_col = mem.sb("g_col", [P, KD])
        eps = mem.sb("eps", [P, 1])
        cv_w = mem.sb("cv_w", [P, KD, CV_W])
        with nc.sbuf_tensor("qk_w_raw", [P, 2, KD, P], F32) as qk_w:
            norm_in(nc, io, u_hi, u_lo, ident, g_col, eps, qk_w)
            qk_proj(nc, io, scr, u_hi, u_lo, g_col, qk_w, cv_w)
        cv_proj(nc, io, scr, u_hi, u_lo, ident, g_col, eps, cv_w)
    mla_up(nc, io, scr)
    with ExitStack() as ctx:
        mem = Memory(nc, ctx)
        ident = mem.sb("late_ident", [P, P])
        attention(nc, io, scr, ident, True)
        work = mem.sb("work", [P, DA_H, D])
        attention(nc, io, scr, ident, False, work)
        u_hi = mem.sb("ff_u_hi", [P, KD, SEQ // 2], F32R)
        u_lo = mem.sb("ff_u_lo", [P, KD, SEQ // 2], F32R)
        w1_raw = mem.sb("ff_w1_raw", [P, KD, P])
        g_pre = mem.sb("ff_g_pre", [P, KD])
        mix_out(nc, io, scr, u_hi, u_lo, work, ident, w1_raw, g_pre)
        mlp(nc, io, scr, u_hi, u_lo, w1_raw, g_pre, work)


def constants():
    inv_freq = (1.0 / (np.float32(10000.0) ** (np.arange(0, ROPE, 2, dtype=np.float32) / np.float32(ROPE)))).astype(np.float32)
    ang = np.arange(L, dtype=np.float32)[:, None] * inv_freq[None, :]
    cos, sin = np.cos(ang).astype(np.float32), np.sin(ang).astype(np.float32)
    trig_tm = np.stack([np.concatenate([cos, cos], 1), np.concatenate([-sin, sin], 1)], 1)
    trig_fm = np.ascontiguousarray(np.tile(trig_tm[META:].transpose(2, 1, 0), (2, 1, 1)))
    p, c = np.arange(P)[:, None], np.arange(L)[None, :]
    dist = np.abs(META + p + (NT - 1) * P - c).astype(np.float32)
    seen = (p >= CHUNK) | (c < (NT - 1) * P + META + CHUNK)
    bias = np.zeros((DA_H + 1, P, L), np.float32)
    for h in range(DA_H):
        slope = np.float32(2.0 ** (-8.0 * (h + 1) / DA_H))
        bias[h] = np.where(seen, -slope * dist / np.float32(DA_SCALE), np.float32(NEG))
    bias[DA_H] = np.where(seen, 0.0, NEG)
    return {"ident": np.eye(P, dtype=np.float32), "trig_tm": np.ascontiguousarray(trig_tm), "trig_fm": trig_fm, "bias": bias}


INPUTS = ["x", "meta_tokens", "g_attn_pre", "w_in", "da_lambda_q1", "da_lambda_k1", "da_lambda_q2", "da_lambda_k2", "g_da_sub",
          "g_mla_q", "w_mla_q_up", "g_mla_kv", "w_mla_kv_up", "w_o", "g_attn_post", "g_mlp_pre", "w_ff1", "w_ff2", "g_mlp_post"]


COLUMNS = ("g_attn_pre", "g_da_sub", "g_mla_q", "g_mla_kv", "g_mlp_pre")


def laid_out(inputs):
    arrays = {n: np.ascontiguousarray(inputs[n]) for n in INPUTS}
    for n in COLUMNS:
        arrays[n] = np.ascontiguousarray(arrays[n].reshape(-1, P).T)
    arrays.update(constants())
    return arrays


def kernel(**inputs):
    import concourse.bacc as bacc
    from concourse.bass_utils import run_bass_kernel_spmd

    nc = bacc.Bacc("TRN2", target_bir_lowering=False, num_devices=1)
    arrays = laid_out(inputs)
    ins = [nc.dram_tensor(f"in_{n}", a.shape, mybir.dt.from_np(a.dtype), kind="ExternalInput").ap() for n, a in arrays.items()]
    out = nc.dram_tensor("out", (1, SEQ, D), F32, kind="ExternalOutput").ap()
    build(nc, ins, out)
    r = run_bass_kernel_spmd(nc, [{f"in_{n}": a for n, a in arrays.items()}], core_ids=[0])
    return r.results[0]["out"]
```
